# Optimizing a Trainium2 kernel written in Bass

```python
import jax, jax.numpy as jnp
from jax import lax
import numpy as np
import math

D_MODEL = 1024
BATCH = 1
SEQ = 256
DEPTH = 2

CHUNK = 64
MIX_WIDTH = D_MODEL
RWKV_HEADS = 8
RWKV_HEAD_DIM = 64
RWKV_WIDTH = RWKV_HEADS * RWKV_HEAD_DIM
DECAY_LORA = 64
ICL_LORA = 64
GATE_LORA = 128
RWKV_IN = 3 * RWKV_WIDTH + DECAY_LORA + ICL_LORA + GATE_LORA
RET_HEADS = 4
RET_QK_DIM = 64
RET_V_DIM = 128
RET_QK_WIDTH = RET_HEADS * RET_QK_DIM
RET_V_WIDTH = RET_HEADS * RET_V_DIM
RET_IN = 2 * RET_QK_WIDTH + 2 * RET_V_WIDTH
PROJ_WIDTH = RWKV_IN + RET_IN
D_FF = 2816
ROPE_BASE = 10000.0
NORM_EPS = 1e-6
LN_X_EPS = 64e-5


def rms_norm(x, gain, eps=NORM_EPS):
    xf = x.astype(jnp.float32)
    y = xf * lax.rsqrt(jnp.mean(xf * xf, axis=-1, keepdims=True) + eps)
    return (y * gain.astype(jnp.float32)).astype(x.dtype)

def swiglu(h, w_gate, w_up, w_down):
    return (jax.nn.silu(h @ w_gate) * (h @ w_up)) @ w_down

def token_shift(p, mu):
    prev = jnp.pad(p, ((0, 0), (1, 0), (0, 0)))[:, :-1]
    return p + mu * (prev - p)

def rwkv7_scan(r, w, k, v, a, b):
    B, S, H, N = r.shape

    def step(state, inp):
        r_t, w_t, k_t, v_t, a_t, b_t = inp
        sa = jnp.einsum('bhvk,bhk->bhv', state, a_t)
        state = (state * w_t[:, :, None, :] + sa[..., None] * b_t[:, :, None, :]
                 + v_t[..., None] * k_t[:, :, None, :])
        return state, jnp.einsum('bhvk,bhk->bhv', state, r_t)

    xs = (jnp.moveaxis(r, 1, 0), jnp.moveaxis(w, 1, 0), jnp.moveaxis(k, 1, 0),
          jnp.moveaxis(v, 1, 0), jnp.moveaxis(a, 1, 0), jnp.moveaxis(b, 1, 0))
    state0 = jnp.zeros((B, H, N, N), jnp.float32)
    _, y = lax.scan(step, state0, xs)
    return jnp.moveaxis(y, 0, 1)

def rwkv7_group(p, mu, w0, w_lora_up, a0, a_lora_up, g_lora_up, k_k, k_a, r_k,
                ln_w, ln_b):
    B, S, _ = p.shape
    p = token_shift(p, mu)
    o1 = RWKV_WIDTH
    o2 = 2 * RWKV_WIDTH
    o3 = 3 * RWKV_WIDTH
    o4 = o3 + DECAY_LORA
    o5 = o4 + ICL_LORA
    r, k, v, w_d, a_d, g_d = jnp.split(p, [o1, o2, o3, o4, o5], axis=-1)
    f32 = jnp.float32
    log_w = -jax.nn.softplus(-(w0 + jnp.tanh(w_d) @ w_lora_up).astype(f32)) - 0.5
    decay = jnp.exp(-jnp.exp(log_w))
    a = jax.nn.sigmoid((a0 + a_d @ a_lora_up).astype(f32))
    g = (jax.nn.sigmoid(g_d) @ g_lora_up).astype(f32)

    def heads(t):
        return t.astype(f32).reshape(B, S, RWKV_HEADS, RWKV_HEAD_DIM)

    kk = heads(k * k_k)
    kk = kk * lax.rsqrt(jnp.maximum(jnp.sum(kk * kk, axis=-1, keepdims=True), 1e-24))
    k_h = heads(k.astype(f32) * (1.0 + (a - 1.0) * k_a.astype(f32)))
    r_h = heads(r)
    v_h = heads(v)
    a_h = heads(a)
    y = rwkv7_scan(r_h, heads(decay), k_h, v_h, -kk, kk * a_h)
    mean = jnp.mean(y, axis=-1, keepdims=True)
    var = jnp.mean(jnp.square(y - mean), axis=-1, keepdims=True)
    y = ((y - mean) * lax.rsqrt(var + LN_X_EPS)
         * ln_w.astype(f32).reshape(RWKV_HEADS, RWKV_HEAD_DIM)
         + ln_b.astype(f32).reshape(RWKV_HEADS, RWKV_HEAD_DIM))
    y = y + jnp.sum(r_h * k_h * r_k.astype(f32), axis=-1, keepdims=True) * v_h
    return (y.reshape(B, S, RWKV_WIDTH) * g).astype(p.dtype)

def rotary(x, pos):
    half = x.shape[-1] // 2
    inv_freq = 1.0 / (ROPE_BASE ** jnp.linspace(0.0, 1.0, half, dtype=jnp.float32))
    ang = pos[:, None] * inv_freq[None, :]
    cos = jnp.cos(ang)[None, :, None, :]
    sin = jnp.sin(ang)[None, :, None, :]
    x1, x2 = x[..., :half], x[..., half:]
    return jnp.concatenate([x1 * cos - x2 * sin, x1 * sin + x2 * cos], axis=-1)

def retention_chunkwise(q, k, v):
    B, S, H, dk = q.shape
    dv = v.shape[-1]
    nc = S // CHUNK
    log_gamma = jnp.log(1.0 - jnp.power(2.0, -5.0 - jnp.arange(H, dtype=jnp.float32)))
    qc = q.reshape(B, nc, CHUNK, H, dk)
    kc = k.reshape(B, nc, CHUNK, H, dk)
    vc = v.reshape(B, nc, CHUNK, H, dv)
    pos = jnp.arange(CHUNK, dtype=jnp.float32)
    dist = jnp.abs(pos[:, None] - pos[None, :])
    intra_decay = jnp.exp(log_gamma[:, None, None] * dist)
    scores = jnp.einsum('bnihd,bnjhd->bnhij', qc, kc) * intra_decay
    intra = jnp.einsum('bnhij,bnjhe->bnihe', scores, vc)
    key_w = jnp.exp(log_gamma[:, None] * (CHUNK - 1.0 - pos)[None, :])
    chunk_kv = jnp.einsum('bnjhd,hj,bnjhe->bnhde', kc, key_w, vc)
    chunk_decay = jnp.exp(log_gamma * CHUNK)[None, :, None, None]

    def step(state, kv_n):
        return state * chunk_decay + kv_n, state

    _, prev = lax.scan(step, jnp.zeros((B, H, dk, dv), jnp.float32),
                       jnp.moveaxis(chunk_kv, 1, 0))
    prev = jnp.moveaxis(prev, 0, 1)
    query_w = jnp.exp(log_gamma[:, None] * (pos + 1.0)[None, :])
    cross = jnp.einsum('bnihd,hi,bnhde->bnihe', qc, query_w, prev)
    return (intra + cross).reshape(B, S, H, dv)

def retnet_group(p):
    B, S, _ = p.shape
    f32 = jnp.float32
    q, k, v, g = jnp.split(p, [RET_QK_WIDTH, 2 * RET_QK_WIDTH,
                               2 * RET_QK_WIDTH + RET_V_WIDTH], axis=-1)
    pos = jnp.arange(S, dtype=f32)
    q = rotary(q.astype(f32).reshape(B, S, RET_HEADS, RET_QK_DIM), pos)
    k = rotary(k.astype(f32).reshape(B, S, RET_HEADS, RET_QK_DIM), pos) * (RET_QK_DIM ** -0.5)
    v = v.astype(f32).reshape(B, S, RET_HEADS, RET_V_DIM)
    o = retention_chunkwise(q, k, v)
    o = o * lax.rsqrt(jnp.mean(o * o, axis=-1, keepdims=True) + NORM_EPS)
    return (o.reshape(B, S, RET_V_WIDTH) * jax.nn.silu(g.astype(f32))).astype(p.dtype)

def first_inputs(seed: int = 0) -> dict:
    key = jax.random.key(seed)
    ks = jax.random.split(key, 32)
    f32 = jnp.float32

    def nrm(k, shape, scale):
        return jax.random.normal(k, shape, f32) * scale

    decay_speed = -7.0 + 5.0 * jnp.linspace(0.0, 1.0, RWKV_WIDTH, dtype=f32) ** 0.85 + 0.5
    return {
        "x": nrm(ks[0], (BATCH, SEQ, D_MODEL), 1.0),
        "ffn1_norm": 1.0 + nrm(ks[1], (DEPTH, D_MODEL), 0.1),
        "ffn1_w_gate": nrm(ks[2], (DEPTH, D_MODEL, D_FF), D_MODEL ** -0.5),
        "ffn1_w_up": nrm(ks[3], (DEPTH, D_MODEL, D_FF), D_MODEL ** -0.5),
        "ffn1_w_down": nrm(ks[4], (DEPTH, D_FF, D_MODEL), D_FF ** -0.5),
        "mix_norm": 1.0 + nrm(ks[5], (DEPTH, D_MODEL), 0.1),
        "w_in": nrm(ks[6], (DEPTH, D_MODEL, PROJ_WIDTH), D_MODEL ** -0.5),
        "shift_mu": jax.random.uniform(ks[7], (DEPTH, RWKV_IN), f32),
        "w0": decay_speed[None, :] + nrm(ks[8], (DEPTH, RWKV_WIDTH), 0.1),
        "w_lora_up": nrm(ks[9], (DEPTH, DECAY_LORA, RWKV_WIDTH), 0.1),
        "a0": nrm(ks[10], (DEPTH, RWKV_WIDTH), 0.1),
        "a_lora_up": nrm(ks[11], (DEPTH, ICL_LORA, RWKV_WIDTH), 0.5 * ICL_LORA ** -0.5),
        "g_lora_up": nrm(ks[12], (DEPTH, GATE_LORA, RWKV_WIDTH), GATE_LORA ** -0.5),
        "k_k": 0.85 + nrm(ks[13], (DEPTH, RWKV_WIDTH), 0.05),
        "k_a": 1.0 + nrm(ks[14], (DEPTH, RWKV_WIDTH), 0.05),
        "r_k": nrm(ks[15], (DEPTH, RWKV_HEADS, RWKV_HEAD_DIM), 0.1),
        "ln_x_w": 1.0 + nrm(ks[16], (DEPTH, RWKV_WIDTH), 0.1),
        "ln_x_b": nrm(ks[17], (DEPTH, RWKV_WIDTH), 0.01),
        "w_out": nrm(ks[18], (DEPTH, MIX_WIDTH, D_MODEL), MIX_WIDTH ** -0.5),
        "ffn2_norm": 1.0 + nrm(ks[19], (DEPTH, D_MODEL), 0.1),
        "ffn2_w_gate": nrm(ks[20], (DEPTH, D_MODEL, D_FF), D_MODEL ** -0.5),
        "ffn2_w_up": nrm(ks[21], (DEPTH, D_MODEL, D_FF), D_MODEL ** -0.5),
        "ffn2_w_down": nrm(ks[22], (DEPTH, D_FF, D_MODEL), D_FF ** -0.5),
        "final_norm": 1.0 + nrm(ks[23], (D_MODEL,), 0.1),
    }

def first_block(x, ffn1_norm, ffn1_w_gate, ffn1_w_up, ffn1_w_down, mix_norm, w_in,
              shift_mu, w0, w_lora_up, a0, a_lora_up, g_lora_up, k_k, k_a, r_k,
              ln_x_w, ln_x_b, w_out, ffn2_norm, ffn2_w_gate, ffn2_w_up, ffn2_w_down,
              final_norm):
    for l in range(DEPTH):
        x = x + 0.5 * swiglu(rms_norm(x, ffn1_norm[l]), ffn1_w_gate[l], ffn1_w_up[l],
                             ffn1_w_down[l])
        h = rms_norm(x, mix_norm[l])
        proj = h @ w_in[l]
        y_rwkv = rwkv7_group(proj[..., :RWKV_IN], shift_mu[l], w0[l], w_lora_up[l], a0[l],
                             a_lora_up[l], g_lora_up[l], k_k[l], k_a[l], r_k[l],
                             ln_x_w[l], ln_x_b[l])
        y_ret = retnet_group(proj[..., RWKV_IN:])
        mixed = jnp.concatenate([y_rwkv, y_ret], axis=-1).astype(x.dtype)
        x = x + mixed @ w_out[l]
        x = x + 0.5 * swiglu(rms_norm(x, ffn2_norm[l]), ffn2_w_gate[l], ffn2_w_up[l],
                             ffn2_w_down[l])
    return rms_norm(x, final_norm)


HEAD_DIM = 64
A_Q_HEADS = 8
A_KV_HEADS = 2
A_GROUP = A_Q_HEADS // A_KV_HEADS
WINDOW = 128
BLOCK = 128
ROPE_THETA = 500000.0
ROPE_DIM = HEAD_DIM // 4
A_WIDTH = A_Q_HEADS * HEAD_DIM
KV_WIDTH = A_KV_HEADS * HEAD_DIM
B_GROUPS = 8
B_GROUP_DIM = 64
B_WIDTH = B_GROUPS * B_GROUP_DIM
CHUNK_2 = 128
EVEN_IN_WIDTH = A_WIDTH + 2 * KV_WIDTH + 2 * B_WIDTH
EVEN_MIX_WIDTH = A_WIDTH + B_WIDTH
POOL_WINDOWS = (2, 4, 8, 16)
POOL_GROUPS = len(POOL_WINDOWS)
POOL_WIDTH = D_MODEL
POOL_GROUP_DIM = POOL_WIDTH // POOL_GROUPS
MEM_LEN = 256
X_HEADS = 4
X_HEAD_DIM = D_MODEL // X_HEADS
N_EXPERTS = 16
N_EXPERT_GROUPS = 4
EXPERTS_PER_GROUP = N_EXPERTS // N_EXPERT_GROUPS
TOP_K = 2
D_EXPERT = D_MODEL // 2
ALPHA = (2.0 * DEPTH) ** 0.25
BETA = (8.0 * DEPTH) ** -0.25
LN_EPS = 1e-5


def layer_norm(x, g, b):
    xf = x.astype(jnp.float32)
    mu = jnp.mean(xf, axis=-1, keepdims=True)
    var = jnp.mean(jnp.square(xf - mu), axis=-1, keepdims=True)
    y = (xf - mu) * lax.rsqrt(var + LN_EPS) * g.astype(jnp.float32) + b.astype(jnp.float32)
    return y.astype(x.dtype)

def partial_rope(t, positions):
    half = ROPE_DIM // 2
    inv_freq = ROPE_THETA ** (-(jnp.arange(half, dtype=jnp.float32) * 2.0 / ROPE_DIM))
    ang = positions.astype(jnp.float32)[..., None] * inv_freq
    cos = jnp.cos(ang)[:, :, None, :]
    sin = jnp.sin(ang)[:, :, None, :]
    tr = t[..., :ROPE_DIM].astype(jnp.float32)
    t1, t2 = tr[..., :half], tr[..., half:]
    rot = jnp.concatenate([t1 * cos - t2 * sin, t2 * cos + t1 * sin], axis=-1).astype(t.dtype)
    return jnp.concatenate([rot, t[..., ROPE_DIM:]], axis=-1)

def sliding_window_sink_attention(q, k, v, sinks):
    bsz, s_len = q.shape[0], q.shape[1]
    nb = s_len // BLOCK
    qb = q.reshape(bsz, nb, BLOCK, A_KV_HEADS, A_GROUP, HEAD_DIM)

    def with_prev(t):
        tb = t.reshape(bsz, nb, BLOCK, A_KV_HEADS, HEAD_DIM)
        prev = jnp.pad(tb[:, :-1], ((0, 0), (1, 0), (0, 0), (0, 0), (0, 0)))
        return jnp.concatenate([prev, tb], axis=2)

    kb, vb = with_prev(k), with_prev(v)
    s = jnp.einsum('bnqhgd,bnkhd->bnhgqk', qb, kb).astype(jnp.float32) * (HEAD_DIM ** -0.5)
    qi = jnp.arange(BLOCK)[:, None]
    kj = jnp.arange(2 * BLOCK)[None, :]
    rel = qi + BLOCK - kj
    band = (rel >= 0) & (rel < WINDOW)
    not_before_start = (jnp.arange(nb)[:, None, None] > 0) | (kj[None] >= BLOCK)
    valid = band[None] & not_before_start
    s = jnp.where(valid[None, :, None, None], s, -jnp.inf)
    sink = sinks.astype(jnp.float32).reshape(A_KV_HEADS, A_GROUP)[None, None, :, :, None, None]
    m = jnp.maximum(jnp.max(s, axis=-1, keepdims=True), sink)
    p = jnp.exp(s - m)
    denom = jnp.sum(p, axis=-1, keepdims=True) + jnp.exp(sink - m)
    p = (p / denom).astype(v.dtype)
    o = jnp.einsum('bnhgqk,bnkhd->bnqhgd', p, vb)
    return o.reshape(bsz, s_len, A_WIDTH)

def chunked_spatial_gating(u, v, ln_g, ln_b, w_s, b_s):
    bsz, s_len = u.shape[0], u.shape[1]
    nc = s_len // CHUNK_2
    vg = v.reshape(bsz, s_len, B_GROUPS, B_GROUP_DIM)
    vg = layer_norm(vg, ln_g.reshape(B_GROUPS, B_GROUP_DIM), ln_b.reshape(B_GROUPS, B_GROUP_DIM))
    vg = vg.reshape(bsz, nc, CHUNK_2, B_GROUPS, B_GROUP_DIM)
    causal = jnp.tril(jnp.ones((CHUNK_2, CHUNK_2), dtype=bool))
    w = jnp.where(causal[None], w_s, jnp.zeros_like(w_s))
    mixed = jnp.einsum('gts,bnsgc->bntgc', w, vg) + b_s.T[None, None, :, :, None]
    return u * mixed.reshape(bsz, s_len, B_WIDTH)

def even_mixer(x, positions, w_in, sinks, sgu_ln_g, sgu_ln_b, sgu_w, sgu_b, w_out):
    bsz, s_len, _ = x.shape
    h = x @ w_in
    c1 = A_WIDTH
    c2 = c1 + KV_WIDTH
    c3 = c2 + KV_WIDTH
    c4 = c3 + B_WIDTH
    q, k, v, bu, bv = h[..., :c1], h[..., c1:c2], h[..., c2:c3], h[..., c3:c4], h[..., c4:]
    q = partial_rope(q.reshape(bsz, s_len, A_Q_HEADS, HEAD_DIM), positions)
    k = partial_rope(k.reshape(bsz, s_len, A_KV_HEADS, HEAD_DIM), positions)
    v = v.reshape(bsz, s_len, A_KV_HEADS, HEAD_DIM)
    a_out = sliding_window_sink_attention(q, k, v, sinks)
    b_out = chunked_spatial_gating(jax.nn.gelu(bu), jax.nn.gelu(bv), sgu_ln_g, sgu_ln_b, sgu_w, sgu_b)
    return jnp.concatenate([a_out, b_out], axis=-1) @ w_out

def odd_mixer(x, w_in, pool_w, pool_scale, w_out):
    bsz, s_len, _ = x.shape
    h = x @ w_in
    hf = h.astype(jnp.float32)
    csum = jnp.cumsum(hf, axis=1)
    counts_base = jnp.arange(1, s_len + 1, dtype=jnp.float32)
    groups = []
    for g, win in enumerate(POOL_WINDOWS):
        sl = slice(g * POOL_GROUP_DIM, (g + 1) * POOL_GROUP_DIM)
        c = csum[..., sl]
        lagged = jnp.pad(c, ((0, 0), (win, 0), (0, 0)))[:, :s_len]
        count = jnp.minimum(counts_base, float(win))[None, :, None]
        groups.append((c - lagged) / count - hf[..., sl])
    pooled = jnp.stack(groups, axis=2).astype(x.dtype)
    mapped = jnp.einsum('bsgc,gcd->bsgd', pooled, pool_w).reshape(bsz, s_len, POOL_WIDTH)
    return (mapped * pool_scale) @ w_out

def memory_cross_attention(x, mem, wq, wkv, wo):
    bsz, s_len, _ = x.shape
    q = (x @ wq).reshape(bsz, s_len, X_HEADS, X_HEAD_DIM)
    kv = (mem @ wkv).reshape(bsz, mem.shape[1], 2, X_HEADS, X_HEAD_DIM)
    k, v = kv[:, :, 0], kv[:, :, 1]
    s = jnp.einsum('bshd,bmhd->bhsm', q, k).astype(jnp.float32) * (X_HEAD_DIM ** -0.5)
    p = jax.nn.softmax(s, axis=-1).astype(v.dtype)
    o = jnp.einsum('bhsm,bmhd->bshd', p, v).reshape(bsz, s_len, D_MODEL)
    return o @ wo

def grouped_moe(x, router_w, router_bias, w_gate, w_up, w_down):
    bsz, s_len, d = x.shape
    xt = x.reshape(-1, d)
    scores = jax.nn.softmax((xt @ router_w).astype(jnp.float32), axis=-1)
    biased = scores + router_bias.astype(jnp.float32)
    grouped = biased.reshape(-1, N_EXPERT_GROUPS, EXPERTS_PER_GROUP)
    group_score = jnp.sum(lax.top_k(grouped, TOP_K)[0], axis=-1)
    g_sel = jnp.argmax(group_score, axis=-1)
    in_group = jnp.take_along_axis(grouped, g_sel[:, None, None], axis=1)[:, 0]
    _, local_idx = lax.top_k(in_group, TOP_K)
    expert_idx = g_sel[:, None] * EXPERTS_PER_GROUP + local_idx
    sel = jnp.take_along_axis(scores, expert_idx, axis=1)
    weights = sel / jnp.sum(sel, axis=-1, keepdims=True)
    combine = jnp.sum(jax.nn.one_hot(expert_idx, N_EXPERTS, dtype=jnp.float32) * weights[..., None], axis=1)
    y = jnp.zeros(xt.shape, dtype=jnp.float32)
    for e in range(N_EXPERTS):
        he = jax.nn.silu(xt @ w_gate[e]) * (xt @ w_up[e])
        y = y + combine[:, e:e + 1] * (he @ w_down[e]).astype(jnp.float32)
    return y.astype(x.dtype).reshape(bsz, s_len, d)

def second_inputs(seed: int = 0) -> dict:
    key = jax.random.key(seed)
    keys = iter(jax.random.split(key, 64))
    f32 = jnp.float32

    def nrm(shape, scale):
        return jax.random.normal(next(keys), shape, f32) * scale

    def gain(n):
        return 1.0 + nrm((n,), 0.05)

    def bias(n):
        return nrm((n,), 0.02)

    inp = {}
    inp["x"] = nrm((BATCH, SEQ, D_MODEL), 1.0)
    inp["mem"] = nrm((BATCH, MEM_LEN, D_MODEL), 1.0)
    offset = jax.random.randint(next(keys), (BATCH, 1), 0, 4096, dtype=jnp.int32)
    inp["positions"] = (offset + jnp.arange(SEQ, dtype=jnp.int32)[None, :]).astype(jnp.int32)
    inp["router_w"] = nrm((D_MODEL, N_EXPERTS), D_MODEL ** -0.5)
    inp["router_bias"] = nrm((N_EXPERTS,), 0.01)

    def common(prefix):
        inp[prefix + "ln1_g"] = gain(D_MODEL)
        inp[prefix + "ln1_b"] = bias(D_MODEL)
        inp[prefix + "xq"] = nrm((D_MODEL, D_MODEL), D_MODEL ** -0.5)
        inp[prefix + "xkv"] = nrm((D_MODEL, 2 * D_MODEL), D_MODEL ** -0.5)
        inp[prefix + "xo"] = nrm((D_MODEL, D_MODEL), BETA * D_MODEL ** -0.5)
        inp[prefix + "ln2_g"] = gain(D_MODEL)
        inp[prefix + "ln2_b"] = bias(D_MODEL)
        inp[prefix + "e_gate"] = nrm((N_EXPERTS, D_MODEL, D_EXPERT), D_MODEL ** -0.5)
        inp[prefix + "e_up"] = nrm((N_EXPERTS, D_MODEL, D_EXPERT), D_MODEL ** -0.5)
        inp[prefix + "e_down"] = nrm((N_EXPERTS, D_EXPERT, D_MODEL), BETA * D_EXPERT ** -0.5)
        inp[prefix + "ln3_g"] = gain(D_MODEL)
        inp[prefix + "ln3_b"] = bias(D_MODEL)

    inp["l0_w_in"] = nrm((D_MODEL, EVEN_IN_WIDTH), D_MODEL ** -0.5)
    inp["l0_sinks"] = nrm((A_Q_HEADS,), 0.5)
    inp["l0_sgu_ln_g"] = gain(B_WIDTH)
    inp["l0_sgu_ln_b"] = bias(B_WIDTH)
    inp["l0_sgu_w"] = nrm((B_GROUPS, CHUNK_2, CHUNK_2), CHUNK_2 ** -0.5)
    inp["l0_sgu_b"] = 1.0 + nrm((B_GROUPS, CHUNK_2), 0.1)
    inp["l0_w_out"] = nrm((EVEN_MIX_WIDTH, D_MODEL), BETA * EVEN_MIX_WIDTH ** -0.5)
    common("l0_")
    inp["l1_w_in"] = nrm((D_MODEL, POOL_WIDTH), D_MODEL ** -0.5)
    inp["l1_pool_w"] = nrm((POOL_GROUPS, POOL_GROUP_DIM, POOL_GROUP_DIM), POOL_GROUP_DIM ** -0.5)
    inp["l1_pool_scale"] = 1.0 + nrm((POOL_WIDTH,), 0.1)
    inp["l1_w_out"] = nrm((POOL_WIDTH, D_MODEL), BETA * POOL_WIDTH ** -0.5)
    common("l1_")

    order = ["x", "mem", "positions", "router_w", "router_bias",
             "l0_w_in", "l0_sinks", "l0_sgu_ln_g", "l0_sgu_ln_b", "l0_sgu_w", "l0_sgu_b", "l0_w_out",
             "l0_ln1_g", "l0_ln1_b", "l0_xq", "l0_xkv", "l0_xo", "l0_ln2_g", "l0_ln2_b",
             "l0_e_gate", "l0_e_up", "l0_e_down", "l0_ln3_g", "l0_ln3_b",
             "l1_w_in", "l1_pool_w", "l1_pool_scale", "l1_w_out",
             "l1_ln1_g", "l1_ln1_b", "l1_xq", "l1_xkv", "l1_xo", "l1_ln2_g", "l1_ln2_b",
             "l1_e_gate", "l1_e_up", "l1_e_down", "l1_ln3_g", "l1_ln3_b"]
    return {name: inp[name] for name in order}

def second_block(x, mem, positions, router_w, router_bias,
              l0_w_in, l0_sinks, l0_sgu_ln_g, l0_sgu_ln_b, l0_sgu_w, l0_sgu_b, l0_w_out,
              l0_ln1_g, l0_ln1_b, l0_xq, l0_xkv, l0_xo, l0_ln2_g, l0_ln2_b,
              l0_e_gate, l0_e_up, l0_e_down, l0_ln3_g, l0_ln3_b,
              l1_w_in, l1_pool_w, l1_pool_scale, l1_w_out,
              l1_ln1_g, l1_ln1_b, l1_xq, l1_xkv, l1_xo, l1_ln2_g, l1_ln2_b,
              l1_e_gate, l1_e_up, l1_e_down, l1_ln3_g, l1_ln3_b):
    mixer_params = [
        (l0_w_in, l0_sinks, l0_sgu_ln_g, l0_sgu_ln_b, l0_sgu_w, l0_sgu_b, l0_w_out),
        (l1_w_in, l1_pool_w, l1_pool_scale, l1_w_out),
    ]
    layer_params = [
        (l0_ln1_g, l0_ln1_b, l0_xq, l0_xkv, l0_xo, l0_ln2_g, l0_ln2_b,
         l0_e_gate, l0_e_up, l0_e_down, l0_ln3_g, l0_ln3_b),
        (l1_ln1_g, l1_ln1_b, l1_xq, l1_xkv, l1_xo, l1_ln2_g, l1_ln2_b,
         l1_e_gate, l1_e_up, l1_e_down, l1_ln3_g, l1_ln3_b),
    ]
    for layer in range(DEPTH):
        if layer % 2 == 0:
            mix = even_mixer(x, positions, *mixer_params[layer])
        else:
            mix = odd_mixer(x, *mixer_params[layer])
        (ln1_g, ln1_b, xq, xkv, xo, ln2_g, ln2_b,
         e_gate, e_up, e_down, ln3_g, ln3_b) = layer_params[layer]
        x = layer_norm(ALPHA * x + mix, ln1_g, ln1_b)
        x = layer_norm(ALPHA * x + memory_cross_attention(x, mem, xq, xkv, xo), ln2_g, ln2_b)
        x = layer_norm(ALPHA * x + grouped_moe(x, router_w, router_bias, e_gate, e_up, e_down), ln3_g, ln3_b)
    return x


def setup_inputs(seed=0):
    out = dict(first_inputs(seed))
    for name, value in second_inputs(seed + 1).items():
        if name != "x":
            out[name + "_2"] = value
    return out


def reference(
    x, ffn1_norm, ffn1_w_gate, ffn1_w_up, ffn1_w_down, mix_norm, w_in, shift_mu, w0, w_lora_up,
    a0, a_lora_up, g_lora_up, k_k, k_a, r_k, ln_x_w, ln_x_b, w_out, ffn2_norm, ffn2_w_gate,
    ffn2_w_up, ffn2_w_down, final_norm, mem_2, positions_2, router_w_2, router_bias_2,
    l0_w_in_2, l0_sinks_2, l0_sgu_ln_g_2, l0_sgu_ln_b_2, l0_sgu_w_2, l0_sgu_b_2, l0_w_out_2,
    l0_ln1_g_2, l0_ln1_b_2, l0_xq_2, l0_xkv_2, l0_xo_2, l0_ln2_g_2, l0_ln2_b_2, l0_e_gate_2,
    l0_e_up_2, l0_e_down_2, l0_ln3_g_2, l0_ln3_b_2, l1_w_in_2, l1_pool_w_2, l1_pool_scale_2,
    l1_w_out_2, l1_ln1_g_2, l1_ln1_b_2, l1_xq_2, l1_xkv_2, l1_xo_2, l1_ln2_g_2, l1_ln2_b_2,
    l1_e_gate_2, l1_e_up_2, l1_e_down_2, l1_ln3_g_2, l1_ln3_b_2,
):
    x = first_block(
        x, ffn1_norm, ffn1_w_gate, ffn1_w_up, ffn1_w_down, mix_norm, w_in, shift_mu, w0,
        w_lora_up, a0, a_lora_up, g_lora_up, k_k, k_a, r_k, ln_x_w, ln_x_b, w_out, ffn2_norm,
        ffn2_w_gate, ffn2_w_up, ffn2_w_down, final_norm,
    )
    return second_block(
        x, mem_2, positions_2, router_w_2, router_bias_2, l0_w_in_2, l0_sinks_2, l0_sgu_ln_g_2,
        l0_sgu_ln_b_2, l0_sgu_w_2, l0_sgu_b_2, l0_w_out_2, l0_ln1_g_2, l0_ln1_b_2, l0_xq_2,
        l0_xkv_2, l0_xo_2, l0_ln2_g_2, l0_ln2_b_2, l0_e_gate_2, l0_e_up_2, l0_e_down_2,
        l0_ln3_g_2, l0_ln3_b_2, l1_w_in_2, l1_pool_w_2, l1_pool_scale_2, l1_w_out_2, l1_ln1_g_2,
        l1_ln1_b_2, l1_xq_2, l1_xkv_2, l1_xo_2, l1_ln2_g_2, l1_ln2_b_2, l1_e_gate_2, l1_e_up_2,
        l1_e_down_2, l1_ln3_g_2, l1_ln3_b_2,
    )


_drawn_inputs = setup_inputs


def setup_inputs(seed=0):
    import zlib

    import numpy as np

    out = dict(_drawn_inputs(seed))
    spreads = {}
    factors = {'ln_x_b': 2.745,
     'l0_sinks_2': 8.0,
     'l0_sgu_ln_g_2': 2.97,
     'l0_sgu_ln_b_2': 8.0,
     'l1_ln3_b_2': 2.861}
    for name, (base, spread) in spreads.items():
        noise = np.random.default_rng([zlib.crc32(name.encode()), seed]).standard_normal(out[name].shape)
        drawn = base * np.exp(spread * noise) if base else spread * noise
        out[name] = __import__('jax').numpy.asarray(drawn.astype(out[name].dtype))
    for name, factor in factors.items():
        out[name] = (out[name] * factor).astype(out[name].dtype)
    return out
```

```python
from contextlib import ExitStack

import numpy as np

import concourse.bass as bass
from concourse import mybir

F32 = mybir.dt.float32
F32R = mybir.dt.float32r
BF16 = mybir.dt.bfloat16
I32 = mybir.dt.int32
ALU = mybir.AluOpType
ACT = mybir.ActivationFunctionType
AX = mybir.AxisListType
ds = bass.ds

P = 128
D = 1024
S = 256
NT = S // P
KB = D // P
DEPTH = 2
FF = 2816
CHUNK = 64
RH, RN = 8, 64
RW = RH * RN
LORA = 256
RWKV_IN = 3 * RW + LORA
RET_IN = 1536
PROJ = RWKV_IN + RET_IN
QCOL = RWKV_IN
VCOL = QCOL + 512
GCOL = VCOL + 512
RETH = 4
DECAY = -float(np.exp(-0.5))
GW = 416

STEPS_FFN = FF // P
TURNS_FFN = STEPS_FFN // 2

T_IDENT, T_CUMI, T_CUMX, T_TOT, T_LMASK, T_LEV, T_ROT, T_DIST = 0, 128, 256, 384, 392, 904, 1672, 1800
T_RES = T_DIST
T_DW = 384
T2 = T_DIST + RETH * T_DW
T_SWA, T_TRI, T_INV, T_LT = 0, 384, 512, 520
T2_SMALL = 536
T_POOL = T2 + T2_SMALL
T_ALL = T_POOL + 4 * NT * S

ALPHA = (2.0 * DEPTH) ** 0.25
W0 = 448
QH, HD = 8, 64
SW = 384
SG = 8
XH = 4
NE = 16
TURNS_E = 2
POOLS = (2, 4, 8, 16)


def tables():
    t = np.zeros((P, T_ALL), np.float64)
    j = np.arange(P)[:, None]
    i = np.arange(P)[None, :]
    same = j // CHUNK == i // CHUNK
    t[:, T_IDENT:T_IDENT + P] = j == i
    t[:, T_CUMI:T_CUMI + P] = DECAY * (same & (j <= i))
    t[:, T_CUMX:T_CUMX + P] = DECAY * (same & (j < i))
    t[:, T_TOT:T_TOT + 2] = DECAY * (j // CHUNK == np.arange(2)[None, :])
    for n in range(4):
        t[:, T_LMASK + n * P:T_LMASK + (n + 1) * P] = same & ((j < i) if n % 2 == 0 else (j <= i))
    for n in range(6):
        s = 2 ** n
        t[:, T_LEV + n * P:T_LEV + (n + 1) * P] = (j // (2 * s) == i // (2 * s)) & (j % (2 * s) < s) & (i % (2 * s) >= s)
    half = 32
    inv = (1.0 / (np.float32(10000.0) ** np.linspace(0.0, 1.0, half, dtype=np.float32))).astype(np.float32)
    for n in range(NT):
        ang = ((np.arange(P) + n * P).astype(np.float32)[:, None] * inv[None, :]).astype(np.float32).astype(np.float64)
        t[:, T_ROT + n * 32:T_ROT + (n + 1) * 32] = np.cos(ang)
        t[:, T_ROT + 64 + n * 32:T_ROT + 64 + (n + 1) * 32] = np.sin(ang)
    for h in range(RETH):
        lg = np.log(1.0 - 2.0 ** (-5.0 - h))
        for c0, js, qs in ((0, np.arange(P), np.arange(S)), (S, np.arange(P) + P, np.arange(P) + P)):
            w = np.exp(lg * np.abs(qs[None, :] - js[:, None])) * (js[:, None] // CHUNK <= qs[None, :] // CHUNK) / 8.0
            t[:, T_DIST + h * T_DW + c0:T_DIST + h * T_DW + c0 + len(qs)] = w
    q = np.arange(P)[:, None]
    t[:, T2:T2 + P] = np.where(i <= q, 0.0, -1e30)
    t[:, T2 + P:T2 + 2 * P] = np.where(i > q, 0.0, -1e30)
    t[:, T2 + 2 * P:T2 + 3 * P] = np.where(i <= q, 0.0, -1e30)
    t[:, T2 + T_TRI:T2 + T_TRI + P] = j <= i
    t[:, T2 + T_INV:T2 + T_INV + 8] = (np.float32(500000.0) ** (-(np.arange(8, dtype=np.float32) * 2.0 / 16))).astype(np.float32)
    t[:, T2 + T_LT:T2 + T_LT + 16] = [b < a for a in range(4) for b in range(4)]
    to = np.arange(S)[None, :]
    for g, win in enumerate(POOLS):
        for n in range(NT):
            js = np.arange(P)[:, None] + n * P
            c0 = T_POOL + (g * NT + n) * S
            t[:, c0:c0 + S] = ((js <= to) & (js > to - win)) / np.minimum(to + 1, win) - (js == to)
    return t.astype(np.float32)


VEC_LAYER = 48

CR = 2


def both_blocks(nc, A, out):
    ctx = ExitStack()
    with ctx:
        def sb(name, shape, dt=F32):
            return ctx.enter_context(nc.sbuf_tensor(name, shape, dt))

        def sem(name):
            return ctx.enter_context(nc.semaphore(name))

        PS = ctx.enter_context(nc.psum_tensor("PS", [P, 8, 512], F32))
        tab = sb("tab", [P, T_RES])
        x = sb("x", [P, NT, D])
        xn = sb("xn", [P, NT, D])
        xTh = sb("xTh", [P, KB, S], F32R)
        xTl = sb("xTl", [P, KB, S], F32R)
        gain = sb("gain", [P, 2, D])
        raw = sb("raw", [P, 3, 2, 1024])
        whi = sb("whi", [P, 3, 1024], F32R)
        wlo = sb("wlo", [P, 3, 1024], F32R)
        gs = sb("gs", [P, 2, S])
        h32 = sb("h32", [P, 2, S])
        hTh = sb("hTh", [P, 2, S], F32R)
        hTl = sb("hTl", [P, 2, S], F32R)
        rwh = sb("rwh", [P, KB, NE], F32R)
        rwl = sb("rwl", [P, KB, NE], F32R)
        zero = sb("zero", [P, 512], BF16)
        rs_in = sb("rs_in", [P, 16])
        rs_out = sb("rs_out", [P, 16])
        neg_half = sb("neg_half", [P, 16])
        bonus = sb("bonus", [P, 16])
        decC = sb("decC", [P, 16])
        proj = sb("proj", [P, NT, PROJ])
        par = sb("par", [P, 5, RW])
        RA = sb("RA", [P, 5376])
        RB = sb("RB", [P, 5888])
        gt = sb("gt", [P, NT, RW])
        tl = sb("tl", [P, 4, NT, RW])

        ident = tab[:, T_IDENT:T_IDENT + P]
        acc = PS[:, 0:4, :].rearrange("p b n -> p (b n)")

        prev = RA[:, 0:3584].rearrange("p (t n) -> p t n", t=NT)
        mu = RA[:, 3584:5376]

        def two(base, n):
            return base[:, 1024 * n:1024 * (n + 1)].rearrange("p (t c) -> p t c", t=NT)

        sw, av, W1, W2, W3 = (two(RA, n) for n in range(5))
        Lm = RA[:, 0:4096].rearrange("p (h n) -> p h n", h=RH)
        ART = RA[:, 4096:5120].rearrange("p (q n) -> p q n", q=4)
        WL = RB[:, 0:512]
        GL = RB[:, 512:1024]
        lT = RB[:, 1024:1536].rearrange("p (b s) -> p b s", b=2)
        kk = RB[:, 1536:2560].rearrange("p (t c) -> p t c", t=NT)
        tmp = RB[:, 2560:3584].rearrange("p (t c) -> p t c", t=NT)
        dist = RB[:, 1536:3072].rearrange("p (h n) -> p h n", h=RETH)
        qk = RB[:, 3072:4096].rearrange("p (t h n) -> p t h n", t=NT, h=8)
        qkT = RB[:, 4096:5120].rearrange("p (q t n) -> p q t n", q=4, t=NT)
        PT = RB[:, 5120:5888].rearrange("p (b n) -> p b n", b=2)
        TM = RB[:, 0:1024].rearrange("p (h n) -> p h n", h=RH)
        TT = RB[:, 1024:2048].rearrange("p (h n) -> p h n", h=RH)
        Aoff = RB[:, 2048:3072].rearrange("p (h n) -> p h n", h=RH)
        QM = RB[:, 3072:4096].rearrange("p (h n) -> p h n", h=RH)
        Zs = RB[:, 4096:5632].rearrange("p (c q n) -> p c q n", c=3, q=4)
        Ztmp = RB[:, 5632:5888].rearrange("p (q n) -> p q n", q=4)
        xTf = raw[:, 2].rearrange("p s n -> p (s n)")
        xT1 = RA[:, 0:2048].rearrange("p (k s) -> p k s", k=KB)
        BT = xTf[:, 0:512].rearrange("p (q n) -> p q n", q=4)
        KT = xTf[:, 512:1024].rearrange("p (q n) -> p q n", q=4)
        U = xTf[:, 1024:1536]
        AV = xTf[:, 1536:2048]

        h2 = proj[:].rearrange("p t n -> p (t n)")
        hid = h2[:, 0:3584].rearrange("p (t n) -> p t n", t=NT)
        Sc = h2[:, 3584:6656].rearrange("p (h n) -> p h n", h=QH)
        hid1 = h2[:, 0:2048].rearrange("p (t n) -> p t n", t=NT)
        pool_t = h2[:, 2048:4096].rearrange("p (g t n) -> p g t n", g=4, t=NT)
        pf = par[:].rearrange("p a n -> p (a n)")
        swa_mask = pf[:, T_SWA:T_SWA + SW]
        tri = pf[:, T_TRI:T_TRI + P]
        inv = pf[:, T_INV:T_INV + 8]
        lt = pf[:, T_LT:T_LT + 16]
        sinks = pf[:, 536:544]
        rbias = pf[:, 544:560]
        pscale = pf[:, 560:568]
        sgb = pf[:, 568:576]
        rw = pf[:, 576:704].rearrange("p (k e) -> p k e", k=KB)
        sgu_g, sgu_bb = pf[:, 704:1216], pf[:, 1216:1728]
        pos_i = pf[:, 1728:1730].bitcast(I32)
        posf = pf[:, 1730:1732]
        ang, turns, red = (pf[:, 1732 + 32 * n:1764 + 32 * n] for n in range(3))
        mrow = pf[:, 1828:1844]
        srow = pf[:, 1844:1860]
        den = pf[:, 1860:1876]
        mean = pf[:, 1876:1892]
        stats = pf[:, 1892:1904].rearrange("p (c n) -> p c n", c=2)
        aggr = pf[:, 1904:1908].rearrange("p (t n) -> p t n", t=NT)
        lg, score, bi, comb, sel, wsel = (pf[:, 1908 + 32 * n:1940 + 32 * n] for n in range(6))
        gsum, grank = pf[:, 2100:2108], pf[:, 2108:2116]
        cmp_, eqs = pf[:, 2120:2248], pf[:, 2248:2376]
        ropet = pf[:, 2376:2536].rearrange("p (t h n) -> p t h n", t=NT, h=10)
        tlf = tl[:].rearrange("p a t n -> p (a t n)")
        memT = tlf[:, 0:2048].rearrange("p (k s) -> p k s", k=KB)
        kT = tlf[:, 2048:4096].rearrange("p (k s) -> p k s", k=KB)
        vM = RA[:, 0:2048].rearrange("p (t n) -> p t n", t=NT)
        qT = RA[:, 2048:4096].rearrange("p (k s) -> p k s", k=KB)
        mem = RA[:, 2048:4096].rearrange("p (t n) -> p t n", t=NT)
        tmpA = RA[:, 2048:3072].rearrange("p (t n) -> p t n", t=NT)
        mixg = RA[:, 4096:5120].rearrange("p (g t n) -> p g t n", g=SG, t=NT)
        pTw = RB[:, 0:3072].rearrange("p (h b n) -> p h b n", h=QH, b=3)
        qT2 = RB[:, 3072:4096].rearrange("p (q t n) -> p q t n", q=4, t=NT)
        kT2 = RB[:, 4096:4608].rearrange("p (g t n) -> p g t n", g=2, t=NT)
        kdup = RA[:, 4608:5120].rearrange("p (t g c n) -> p t g c n", t=NT, g=2, c=2)
        sgw = RB[:, 4608:5632].rearrange("p (g n) -> p g n", g=SG)
        sgT = gt[:].rearrange("p t n -> p (t n)").rearrange("p (g n) -> p g n", g=SG)
        xT2 = RB[:, 0:2048].rearrange("p (k s) -> p k s", k=KB)
        px = RB[:, 0:2048].rearrange("p (a n) -> p a n", a=2 * XH)
        pxT = RB[:, 2048:4096].rearrange("p (h m s) -> p h m s", h=XH, m=NT)
        mapT = xn[:].rearrange("p t n -> p (t n)").rearrange("p (k s) -> p k s", k=KB)

        tab_in = sem("tab_in")
        gain_in = [sem(f"gain_in{n}") for n in range(2)]
        norm_done = sem("norm_done")
        rs_asked = sem("rs_asked")
        rs_given = sem("rs_given")
        xn_ready = sem("xn_ready")
        xT_psum = sem("xT_psum")
        xT_act = sem("xT_act")
        xT_dve = sem("xT_dve")
        rw_split = sem("rw_split")
        raw_in = [[sem(f"{m}_in{n}") for n in range(2)] for m in ("gate", "up", "down")]
        hi_done = [sem(f"{m}_hi") for m in ("gate", "up", "down")]
        lo_done = [sem(f"{m}_lo") for m in ("gate", "up", "down")]
        used = [sem(f"{m}_used") for m in ("gate", "up", "down")]
        silu_ready = sem("silu_ready")
        h_ready = sem("h_ready")
        hT_ready = sem("hT_ready")
        chunk_in = [sem(f"chunk_in{n}") for n in range(4)]
        chunk_used = sem("chunk_used")
        group_done = sem("group_done")
        group_out = sem("group_out")
        vec = sem("vec")
        setup = sem("setup")
        param_in = sem("param_in")
        ln_in = sem("ln_in")
        zero_row = sem("zero_row")
        shift_in = sem("shift_in")
        qk_rot = sem("qk_rot")
        qkT_psum = sem("qkT_psum")
        qkT_ready = sem("qkT_ready")
        ret_s = sem("ret_s")
        ret_p = sem("ret_p")
        ret_o = sem("ret_o")
        ret_oc = sem("ret_oc")
        ret_g = sem("ret_g")
        shifted = sem("shifted")
        lora_act = sem("lora_act")
        lT_psum = sem("lT_psum")
        lT_ready = sem("lT_ready")
        lora_out = sem("lora_out")
        z_ready = sem("z_ready")
        sig_ready = sem("sig_ready")
        g_ready = sem("g_ready")
        cum_psum = sem("cum_psum")
        exp_ready = sem("exp_ready")
        tilde = sem("tilde")
        tr_psum = sem("tr_psum")
        tr_act = sem("tr_act")
        tr_dve = sem("tr_dve")
        L_psum = sem("L_psum")
        L_ready = sem("L_ready")
        av_psum = sem("av_psum")
        av_ready = sem("av_ready")
        aoff_ready = sem("aoff_ready")
        q_psum = sem("q_psum")
        q_ready = sem("q_ready")
        t_psum = sem("t_psum")
        t_ready = sem("t_ready")
        gT_psum = sem("gT_psum")
        gT_ready = sem("gT_ready")
        u_psum = sem("u_psum")
        u_ready = sem("u_ready")
        z_psum = sem("z_psum")
        z_state = sem("z_state")
        y_psum = sem("y_psum")
        y_ready = sem("y_ready")
        out_done = sem("out_done")
        paces = {nc.sync.engine: sem("pace_sp"), nc.tensor.engine: sem("pace_pe")}

        par2_in = sem("par2_in")
        pool_in = sem("pool_in")
        ang_ready = sem("ang_ready")
        sin_ready = sem("sin_ready")
        rope_ready = sem("rope_ready")
        gelu_ready = sem("gelu_ready")
        swT_psum = sem("swT_psum")
        swT_ready = sem("swT_ready")
        sc_psum = sem("sc_psum")
        sc_read = sem("sc_read")
        ex_asked = sem("ex_asked")
        ex_ready = sem("ex_ready")
        p_ready = sem("p_ready")
        pT_psum = sem("pT_psum")
        pT_ready = sem("pT_ready")
        pv_psum = sem("pv_psum")
        pv_ready = sem("pv_ready")
        sgT_psum = sem("sgT_psum")
        sgT_ready = sem("sgT_ready")
        vg_ready = sem("vg_ready")
        sgu_psum = sem("sgu_psum")
        gate_read = sem("gate_read")
        xs_psum = sem("xs_psum")
        xe_asked = sem("xe_asked")
        xe_ready = sem("xe_ready")
        xp_ready = sem("xp_ready")
        xpT_psum = sem("xpT_psum")
        xpT_ready = sem("xpT_ready")
        rt_psum = sem("rt_psum")
        re_asked = sem("re_asked")
        re_ready = sem("re_ready")
        acc_free = sem("acc_free")

        def chunk_raw(q, k, width):
            return raw[:, (q % 4) // 2, q % 2, 0:k * width].rearrange("p (k n) -> p k n", k=k)

        def hold(eng, signal, value):
            eng.wait_ge(signal, value)
            eng.sem_inc(paces[eng.engine], 1)

        def chain(eng, signal, start):
            def step(ins):
                step.n += 1
                ins.then_inc(signal, 1)
                eng.wait_ge(signal, start + step.n)
            step.n = 0
            return step

        block = ctx.enter_context(nc.Block())

        @block.sync
        def _(sp):
            sp.dma_start(tab[:], A["tables"][:, 0:T_RES]).then_inc(tab_in, 16)
            sp.dma_start(x[:], A["x"][0].rearrange("(t p) d -> p t d", p=P)).then_inc(tab_in, 16)

            def chunk_load(q, n4, src):
                hold(sp, chunk_used, 4 * n4 + q % 4 + 1)
                sp.dma_start(chunk_raw(q, src.shape[1], src.shape[2]), src).then_inc(chunk_in[q % 4], 16)

            def step_load(m, turn, j, src):
                hold(sp, lo_done[m], 2 * turn + j + 1)
                dst = raw[:, m, j]
                if m < 2:
                    dst = dst.rearrange("p (k f) -> p k f", k=KB)
                sp.dma_start(dst, src).then_inc(raw_in[m][j], 16)

            def ffn_load(wg, wu, wd, l, t0):
                with sp.Fori(0, TURNS_FFN) as g:
                    for j in range(2):
                        cols = ds((2 * g + j) * P, P)
                        step_load(0, t0 + g, j, wg[l].rearrange("(k p) f -> p k f", p=P)[:, :, cols])
                        step_load(1, t0 + g, j, wu[l].rearrange("(k p) f -> p k f", p=P)[:, :, cols])
                        step_load(2, t0 + g, j, wd[l, cols, :])

            def steps_split(steps):
                for m in range(2):
                    hold(sp, lo_done[m], steps + CR)

            def chunks_multiplied(chunks):
                hold(sp, chunk_used, chunks + 4)

            with sp.Fori(0, DEPTH) as l:
                hold(sp, norm_done, 3 * l + 1)
                sp.dma_start(gain[:, 0], A["ffn1_norm"][l].partition_broadcast(P)).then_inc(gain_in[0], 16)
                sp.dma_start(gain[:, 1], A["mix_norm"][l].partition_broadcast(P)).then_inc(gain_in[1], 16)
                w_in = A["w_in"][l].rearrange("(k p) n -> p k n", p=P)
                ffn_load(A["ffn1_w_gate"], A["ffn1_w_up"], A["ffn1_w_down"], l, 2 * TURNS_FFN * l)
                steps_split(2 * STEPS_FFN * l + STEPS_FFN)
                for c in range(4):
                    chunk_load(c, 10 * l, w_in[:, 2 * c:2 * c + 2, 0:GW])
                hold(sp, norm_done, 3 * l + 2)
                sp.dma_start(gain[:, 0], A["ffn2_norm"][l].partition_broadcast(P)).then_inc(gain_in[0], 16)
                sp.dma_start(mu, A["shift_mu"][l].partition_broadcast(P)).then_inc(param_in, 16)
                for n, name in enumerate(("w0", "a0", "k_k", "k_a")):
                    sp.dma_start(par[:, n], A[name][l].partition_broadcast(P)).then_inc(param_in, 16)
                sp.dma_start(par[:, 4], A["r_k"][l].rearrange("h n -> (h n)").partition_broadcast(P)).then_inc(param_in, 16)
                sp.dma_start(WL[0:64], A["w_lora_up"][l]).then_inc(param_in, 16)
                sp.dma_start(WL[64:128], A["a_lora_up"][l]).then_inc(param_in, 16)
                sp.dma_start(GL, A["g_lora_up"][l]).then_inc(param_in, 16)
                sp.dma_start(dist, A["tables"][:, T_DIST:T2].rearrange("p (h n) -> p h n", h=RETH)).then_inc(param_in, 16)
                with sp.Fori(1, 8) as g:
                    for c in range(4):
                        chunk_load(c, 10 * l + g, w_in[:, 2 * c:2 * c + 2, ds(g * GW, GW)])
                hold(sp, group_out, 10 * l + 8 + CR)
                sp.wait_ge(zero_row, l + 1)
                sp.dma_start(prev[1:P], proj[0:P - 1, :, 0:RWKV_IN]).then_inc(shift_in, 16)
                sp.dma_start(prev[0:1, 1], proj[P - 1:P, 0, 0:RWKV_IN]).then_inc(shift_in, 16)
                w_out = A["w_out"][l].rearrange("(k p) n -> p k n", p=P)
                for c in range(4):
                    chunk_load(c, 10 * l + 8, w_out[:, 2 * c:2 * c + 2, 0:512])
                hold(sp, tilde, l + 1)
                sp.dma_start(par[:, 0], A["ln_x_w"][l].partition_broadcast(P)).then_inc(ln_in, 16)
                sp.dma_start(par[:, 1], A["ln_x_b"][l].partition_broadcast(P)).then_inc(ln_in, 16)
                for c in range(4):
                    chunk_load(c, 10 * l + 9, w_out[:, 2 * c:2 * c + 2, 512:1024])
                chunks_multiplied(40 * l + 40)
                ffn_load(A["ffn2_w_gate"], A["ffn2_w_up"], A["ffn2_w_down"], l, 2 * TURNS_FFN * l + TURNS_FFN)
            hold(sp, norm_done, 3 * DEPTH + 1)
            sp.dma_start(gain[:, 0], A["final_norm"].partition_broadcast(P)).then_inc(gain_in[0], 16)

            def by_row(w):
                return w.rearrange("(k p) n -> p k n", p=P)

            q = 40 * DEPTH

            def load2(w, c0, width):
                nonlocal q
                for c in range(4):
                    chunk_load(q, q // 4, by_row(w)[:, 2 * c:2 * c + 2, c0:c0 + width])
                    q += 1

            for dst, src in (
                (pf[:, 0:T2_SMALL], A["tables"][:, T2:T2 + T2_SMALL]),
                (sinks, A["l0_sinks_2"].partition_broadcast(P)),
                (rbias, A["router_bias_2"].partition_broadcast(P)),
                (pscale, A["l1_pool_scale_2"].rearrange("(k p) -> p k", p=P)),
                (sgb, A["l0_sgu_b_2"].rearrange("g t -> t g")),
                (rw, by_row(A["router_w_2"])),
                (sgu_g, A["l0_sgu_ln_g_2"].partition_broadcast(P)),
                (sgu_bb, A["l0_sgu_ln_b_2"].partition_broadcast(P)),
                (pos_i, A["positions_2"][0].rearrange("(t p) -> p t", p=P)),
                (sgw, A["l0_sgu_w_2"].rearrange("g t s -> t g s")),
                (mem, A["mem_2"][0].rearrange("(t p) d -> p t d", p=P)),
            ):
                sp.dma_start(dst, src, allow_slow_non_contiguous=True).then_inc(par2_in, 16)
            for l in range(DEPTH):
                w = {n: A[f"l{l}_{n}_2"] for n in ("w_in", "w_out", "xq", "xkv", "xo", "e_gate", "e_up", "e_down")}
                steps_split(4 * STEPS_FFN + 2 * NE * TURNS_E * l)
                for j in range(4 if l == 0 else 2):
                    load2(w["w_in"], j * (W0 if l == 0 else 512), W0 if l == 0 else 512)
                if l:
                    sp.dma_start(pool_t.rearrange("p g t n -> p (g t n)"), A["tables"][:, T_POOL:T_ALL]).then_inc(pool_in, 16)
                for j in range(4):
                    load2(w["xkv"], j * 512, 512)
                if l == 1:
                    for g in range(4):
                        chunk_load(q, q // 4, A["l1_pool_w_2"][g].rearrange("(c p) d -> p c d", p=P))
                        q += 1
                for name in ("w_out", "xq", "xo"):
                    for j in range(2):
                        load2(w[name], j * 512, 512)
                chunks_multiplied(q)
                t0 = 4 * TURNS_FFN + NE * TURNS_E * l
                with sp.Fori(0, NE) as e:
                    for tt in range(TURNS_E):
                        for j in range(2):
                            turn = t0 + TURNS_E * e + tt
                            cols = slice((2 * tt + j) * P, (2 * tt + j + 1) * P)
                            step_load(0, turn, j, w["e_gate"][e].rearrange("(k p) f -> p k f", p=P)[:, :, cols])
                            step_load(1, turn, j, w["e_up"][e].rearrange("(k p) f -> p k f", p=P)[:, :, cols])
                            step_load(2, turn, j, w["e_down"][e, cols, :])
            sp.wait_ge(norm_done, 3 * DEPTH + 8)
            sp.dma_start(out[0].rearrange("(t p) d -> p t d", p=P), x[:]).then_inc(out_done, 16)
            sp.wait_ge(out_done, 16)

        @block.gpsimd
        def _(pool):
            pool.wait_ge(setup, 3)

            def rsqrt(n):
                pool.wait_ge(rs_asked, n + 1)
                nc.gpsimd.tensor_tensor(rs_out[:], rs_in[:], neg_half[:], ALU.pow).then_inc(rs_given, 1)

            with pool.Fori(0, DEPTH) as l:
                for n in range(4):
                    rsqrt(6 * l + n)
                for t in range(NT):
                    for lev in range(6):
                        for hf in range(2):
                            hs = slice(4 * hf, 4 * hf + 4)
                            if lev == 0:
                                pool.wait_ge(L_ready, 16 * l + 8 * t + 4 * hf + 4)
                                if t:
                                    pool.wait_ge(q_psum, 24 * l + 12)
                            else:
                                pool.wait_ge(q_psum, 24 * l + 12 * t + 2 * lev - 2 + hf + 1)
                                if lev == 1:
                                    pool.wait_ge(t_ready, 24 * l + 12 * t + hf + 1)
                            mask = tab[:, T_LEV + lev * P:T_LEV + (lev + 1) * P]
                            nc.gpsimd.tensor_tensor(Aoff[:, hs], Lm[:, hs, 0:P], mask.unsqueeze(1).to_broadcast([P, 4, P]),
                                                    ALU.mult).then_inc(aoff_ready, 1)
                for n in range(4, 6):
                    rsqrt(6 * l + n)
            with pool.Fori(6 * DEPTH, 6 * DEPTH + 8) as n:
                rsqrt(n)

        @block.scalar
        def _(act):
            def turn_rows(r, dst):
                for b in (0, 2):
                    act.wait_ge(xT_psum, 4 * r + b + 1)
                    nc.scalar.activation(dst[:, 2 * b:2 * b + 2, :], PS[:, 4 + b, :], ACT.Copy).then_inc(xT_act, 2)

            def turn_split(r):
                for b in range(4):
                    act.wait_ge(xT_psum, 4 * r + b + 1)
                    nc.scalar.activation(xTh[:, 2 * b:2 * b + 2, :].rearrange("p k s -> p (k s)"), PS[:, 4 + b, :], ACT.Copy).then_inc(xT_act, 1)

            def split(m, turn, j):
                act.wait_ge(raw_in[m][j], 16 * turn + 16)
                act.wait_ge(used[m], 2 * turn + j + 1)
                nc.scalar.activation(whi[:, m], raw[:, m, j], ACT.Copy).then_inc(hi_done[m], 1)

            def first_split(turn):
                for m in range(2):
                    split(m, turn, 0)

            def step(turn, j, more=True):
                if more:
                    for m in range(2):
                        split(m, turn + j, 1 - j)
                act.wait_ge(used[1], 2 * turn + j + 1 + 1)
                nc.scalar.activation(gs[:, j], PS[:, 4 + j, 0:S], ACT.Silu).then_inc(silu_ready, 1)
                split(2, turn, j)

            def ffn(t0):
                with act.Fori(0, TURNS_FFN - 1) as g:
                    for j in range(2):
                        step(t0 + g, j)
                step(t0 + TURNS_FFN - 1, 0)
                step(t0 + TURNS_FFN - 1, 1, False)

            def experts(t0):
                step(t0, 0)
                with act.Fori(0, NE - 1) as e:
                    t = t0 + TURNS_E * e
                    step(t, 1)
                    step(t + 1, 0)
                    step(t + 1, 1)
                    step(t + 2, 0)
                t = t0 + TURNS_E * (NE - 1)
                step(t, 1)
                step(t + 1, 0)
                step(t + 1, 1, False)

            act.wait_ge(setup, 3)
            with act.Fori(0, DEPTH) as l:
                first_split(2 * TURNS_FFN * l)
                turn_split(4 * l)
                ffn(2 * TURNS_FFN * l)
                turn_rows(4 * l + 1, xT1)
                with act.Fori(0, 4) as g:
                    for j in range(2):
                        act.wait_ge(group_done, 10 * l + 2 * g + j + 1 + CR)
                        nc.scalar.activation(proj[:, :, ds((2 * g + j) * GW, GW)], PS[:, 2 * j:2 * j + 2, 0:GW],
                                             ACT.Copy).then_inc(group_out, 1)
                act.wait_ge(group_out, 10 * l + 8 + CR)
                nc.scalar.activation(proj[:, :, GCOL:PROJ], proj[:, :, GCOL:PROJ], ACT.Silu).then_inc(ret_g, 1)
                act.wait_ge(qkT_psum, l + 1)
                nc.scalar.activation(qkT.rearrange("p q t n -> p (q t n)"), PS[:, 4:6, :].rearrange("p b n -> p (b n)"),
                                     ACT.Copy).then_inc(qkT_ready, 1)
                act.wait_ge(ret_o, l + 1)
                nc.scalar.activation(xn[:, :, RW:2 * RW], PS[:, 0:2, :], ACT.Copy).then_inc(ret_oc, 1)
                act.wait_ge(shifted, l + 1)
                nc.scalar.activation(proj[:, :, 1536:1600], proj[:, :, 1536:1600], ACT.Tanh).then_inc(lora_act, 1)
                nc.scalar.activation(proj[:, :, 1664:1792], proj[:, :, 1664:1792], ACT.Sigmoid).then_inc(lora_act, 1)
                act.wait_ge(lT_psum, l + 1)
                nc.scalar.activation(lT.rearrange("p b s -> p (b s)"), PS[:, 4, :], ACT.Copy).then_inc(lT_ready, 1)
                act.wait_ge(lora_out, l + 1)
                nc.scalar.activation(gt[:], PS[:, 6:8, :], ACT.Copy).then_inc(g_ready, 1)
                act.wait_ge(z_ready, 2 * l + 1)
                nc.scalar.activation(sw, sw, ACT.Sigmoid).then_inc(sig_ready, 1)
                act.wait_ge(z_ready, 2 * l + 2)
                nc.scalar.activation(av, av, ACT.Sigmoid).then_inc(sig_ready, 1)
                act.wait_ge(cum_psum, l + 1)
                nc.scalar.activation(W1, PS[:, 0:2, :], ACT.Exp)
                nc.scalar.activation(W2, PS[:, 0:2, :], ACT.Exp, scale=-1.0)
                nc.scalar.activation(W3, PS[:, 2:4, :], ACT.Exp)
                nc.scalar.activation(decC[:], PS[:, 5, 0:16], ACT.Exp).then_inc(exp_ready, 1)
                for t in range(NT):
                    act.wait_ge(tr_psum, 2 * l + t + 1)
                    nc.scalar.activation(ART.rearrange("p q n -> p (q n)"), PS[:, 0:2, :].rearrange("p b n -> p (b n)"),
                                         ACT.Copy).then_inc(tr_act, 1)
                    act.wait_ge(av_psum, 2 * l + t + 1)
                    nc.scalar.activation(AV, PS[:, 0, :], ACT.Copy).then_inc(av_ready, 1)
                    for lev in range(1, 6):
                        for hf in range(2):
                            act.wait_ge(q_psum, 24 * l + 12 * t + 2 * lev + hf + 1)
                            if lev > 1:
                                act.wait_ge(t_psum, 20 * l + 10 * t + 2 * (lev - 2) + hf + 1)
                            nc.scalar.activation(QM[:, 4 * hf:4 * hf + 4, :].rearrange("p h n -> p (h n)"), PS[:, 2 + hf, :],
                                                 ACT.Copy).then_inc(q_ready, 1)
                    act.wait_ge(gT_psum, 2 * l + t + 1)
                    nc.scalar.activation(tl[:, 3, t], PS[:, 1, :], ACT.Copy).then_inc(gT_ready, 1)
                    for hf in range(2):
                        rows = slice(64 * hf, 64 * hf + 64)
                        act.wait_ge(u_psum, 4 * l + 2 * t + hf + 1)
                        nc.scalar.activation(U[rows], PS[rows, 2, :], ACT.Copy).then_inc(u_ready, 1)
                    act.wait_ge(y_psum, 2 * l + t + 1)
                    nc.scalar.activation(xn[:, t, 0:RW], PS[:, 1, :], ACT.Copy).then_inc(y_ready, 1)
                turn_rows(4 * l + 2, xT1)
                first_split(2 * TURNS_FFN * l + TURNS_FFN)
                turn_split(4 * l + 3)
                ffn(2 * TURNS_FFN * l + TURNS_FFN)

            def gains(k, g, b):
                act.wait_ge(norm_done, 3 * DEPTH + k + 2)
                act.dma_start(gain[:, 0], g.partition_broadcast(P)).then_inc(gain_in[0], 16)
                act.dma_start(gain[:, 1], b.partition_broadcast(P)).then_inc(gain_in[1], 16)

            def evac(n, dst):
                act.wait_ge(group_done, n + 1 + CR)
                b = 2 * (n % 2)
                nc.scalar.activation(dst, PS[:, b:b + 2, 0:dst.shape[2]] if len(dst.shape) == 3 else PS[:, b:b + 2, :], ACT.Copy)\
                    .then_inc(group_out, 1)

            def evac_turned(n, dst, j):
                act.wait_ge(group_done, n + 1 + CR)
                b = 2 * (n % 2)
                nc.scalar.activation(dst[:, 4 * j:4 * j + 4, :].rearrange("p k s -> p (k s)"), PS[:, b:b + 2, :].rearrange("p b n -> p (b n)"),
                                     ACT.Copy).then_inc(group_out, 1)

            turn_rows(8, xT2)
            turn_rows(9, memT)
            act.wait_ge(par2_in, 176)
            nc.scalar.activation(rwh[:], rw, ACT.Copy).then_inc(rw_split, 1)
            for l in range(DEPTH):
                gains(3 * l, A[f"l{l}_ln1_g_2"], A[f"l{l}_ln1_b_2"])
                n = 20 + 14 * l
                r = 10 if l == 0 else 15
                if l == 0:
                    act.wait_ge(ang_ready, 1)
                    nc.scalar.activation(red, red, ACT.Sin).then_inc(sin_ready, 1)
                    for j in range(4):
                        evac(n + j, hid[:, :, j * W0:(j + 1) * W0])
                    n += 4
                    act.wait_ge(group_out, n + CR)
                    nc.scalar.activation(hid[:, :, 768:1792], hid[:, :, 768:1792], ACT.Gelu_apprx_tanh).then_inc(gelu_ready, 1)
                else:
                    for j in range(2):
                        evac(n + j, hid1[:, :, j * 512:(j + 1) * 512])
                    n += 2
                for j in range(2):
                    evac_turned(n + j, kT, j)
                if l == 0:
                    act.wait_ge(swT_psum, 1)
                    nc.scalar.activation(qT2.rearrange("p q t n -> p (q t n)"), PS[:, 4:6, :].rearrange("p b n -> p (b n)"), ACT.Copy)
                    nc.scalar.activation(kT2.rearrange("p g t n -> p (g t n)"), PS[:, 6, :], ACT.Copy).then_inc(swT_ready, 1)
                for j in range(2):
                    evac(n + 2 + j, vM[:, :, j * 512:(j + 1) * 512])
                n += 4
                if l == 0:
                    act.wait_ge(ex_asked, 1)
                    nc.scalar.activation(Sc, Sc, ACT.Exp)
                    nc.scalar.activation(srow, srow, ACT.Exp).then_inc(ex_ready, 1)
                    for half in range(2):
                        act.wait_ge(pT_psum, half + 1)
                        nc.scalar.activation(pTw[:, 4 * half:4 * half + 4].rearrange("p h b n -> p (h b n)"),
                                             PS[:, 3 * half:3 * half + 3, :].rearrange("p b n -> p (b n)"), ACT.Copy).then_inc(pT_ready, 1)
                    act.wait_ge(pv_psum, 1)
                    nc.scalar.activation(xn[:, :, 0:512], PS[:, 6:8, :], ACT.Copy).then_inc(pv_ready, 1)
                else:
                    turn_rows(r, xT2)
                    n += 2
                    r += 1
                if l == 0:
                    turn_rows(r, xT2)
                    r += 1
                n += 2
                turn_rows(r, xT2)
                gains(3 * l + 1, A[f"l{l}_ln2_g_2"], A[f"l{l}_ln2_b_2"])
                for j in range(2):
                    evac_turned(n + j, qT, j)
                act.wait_ge(xe_asked, l + 1)
                nc.scalar.activation(px, px, ACT.Exp, scale=1.0 / 16).then_inc(xe_ready, 1)
                act.wait_ge(xpT_psum, l + 1)
                nc.scalar.activation(pxT.rearrange("p h m s -> p (h m s)"), PS[:, 0:4, :].rearrange("p b n -> p (b n)"), ACT.Copy)\
                    .then_inc(xpT_ready, 1)
                turn_rows(r + 1, xT2)
                t0 = 4 * TURNS_FFN + NE * TURNS_E * l
                first_split(t0)
                turn_split(r + 2)
                gains(3 * l + 2, A[f"l{l}_ln3_g_2"], A[f"l{l}_ln3_b_2"])
                act.wait_ge(re_asked, l + 1)
                nc.scalar.activation(lg, lg, ACT.Exp).then_inc(re_ready, 1)
                experts(t0)
                if l == 0:
                    turn_rows(14, xT2)

        @block.vector
        def _(dve):
            nc.vector.memset(zero[:], 0.0).then_inc(setup, 1)
            nc.vector.memset(rs_in[:], 1.0).then_inc(setup, 1)
            nc.vector.memset(neg_half[:], -0.5).then_inc(setup, 1)
            dve.wait_ge(setup, 3)
            dve.sem_inc(hT_ready, CR)
            dve.sem_inc(norm_done, 1)
            for m in range(3):
                dve.sem_inc(lo_done[m], CR)

            def rsqrt(n):
                dve.wait_ge(rs_given, n + 1)

            def rms(own, n, g, g_value, ask, dst=xn):
                for t in range(NT):
                    own(nc.vector.tensor_tensor_reduce(xn[:, t], x[:, t], x[:, t], 1.0, 0.0, ALU.mult, ALU.add, rs_in[:, t:t + 1]))
                nc.vector.tensor_scalar(rs_in[:, 0:2], rs_in[:, 0:2], 1.0 / D, 1e-6, ALU.mult, ALU.add).then_inc(rs_asked, 1)
                rsqrt(ask)
                dve.wait_ge(gain_in[g], g_value)
                for t in range(NT):
                    last = nc.vector.scalar_tensor_tensor(out=dst[:, t], in0=x[:, t], scalar=rs_out[:, t:t + 1], in1=gain[:, g],
                                                          op0=ALU.mult, op1=ALU.mult)
                last.then_inc(norm_done, 1)
                dve.wait_ge(norm_done, n + 2)

            def turn_rows(r, dst):
                dve.sem_inc(xn_ready, 1)
                for b in (1, 3):
                    dve.wait_ge(xT_psum, 4 * r + b + 1)
                    nc.vector.tensor_copy(dst[:, 2 * b:2 * b + 2, :].rearrange("p k s -> p (k s)"), PS[:, 4 + b, :]).then_inc(xT_dve, 2)

            def turn_split(r, turn):
                dve.sem_inc(xn_ready, 1)
                for m in range(2):
                    split(m, turn, 0)
                for b in range(4):
                    dve.wait_ge(xT_act, 4 * r + b + 1)
                    f = slice(2 * b, 2 * b + 2)
                    nc.vector.tensor_tensor(xTl[:, f, :].rearrange("p k s -> p (k s)"), PS[:, 4 + b, :],
                                            xTh[:, f, :].rearrange("p k s -> p (k s)").bitcast(F32), ALU.subtract).then_inc(xT_dve, 1)

            def split(m, turn, j):
                dve.wait_ge(hi_done[m], 2 * turn + j + 1)
                nc.vector.tensor_tensor(wlo[:, m], raw[:, m, j], whi[:, m].bitcast(F32), ALU.subtract).then_inc(lo_done[m], 1)

            def step(turn, j, more=True, between=None):
                if more:
                    for m in range(2):
                        split(m, turn + j, 1 - j)
                if between:
                    between()
                dve.wait_ge(silu_ready, 2 * turn + j + 1)
                nc.vector.tensor_tensor(h32[:, j], gs[:, j], PS[:, 4 + j, S:2 * S], ALU.mult)
                nc.vector.tensor_tensor(hTh[:, j], gs[:, j], PS[:, 4 + j, S:2 * S], ALU.mult).then_inc(h_ready, 1)
                dve.wait_ge(h_ready, 2 * turn + j + 1)
                nc.vector.tensor_tensor(hTl[:, j], h32[:, j], hTh[:, j].bitcast(F32), ALU.subtract).then_inc(hT_ready, 1)
                split(2, turn, j)

            def ffn(own, t0):
                with dve.Fori(0, TURNS_FFN - 1) as g:
                    for j in range(2):
                        step(t0 + g, j)
                step(t0 + TURNS_FFN - 1, 0)
                step(t0 + TURNS_FFN - 1, 1, False)
                dve.wait_ge(used[2], 2 * (t0 + TURNS_FFN) + 1)
                xf = x[:].rearrange("p t d -> p (t d)")
                own(nc.vector.scalar_tensor_tensor(out=xf, in0=acc, scalar=0.5, in1=xf, op0=ALU.mult, op1=ALU.add))

            def heads(ap):
                return ap.rearrange("p t (h n) -> p t h n", h=RH)

            def per_head(ap):
                return ap.rearrange("p (t h) -> p t h", t=NT).unsqueeze(3).to_broadcast([P, NT, RH, RN])

            def row(ap):
                return ap.unsqueeze(1).to_broadcast([P, NT, ap.shape[1]])

            dve.wait_ge(tab_in, 32)
            TTop = nc.vector.tensor_tensor
            with dve.Fori(0, DEPTH) as l:
                own = chain(dve, vec, l * VEC_LAYER)
                rms(own, 3 * l, 0, 32 * l + 16, 6 * l)
                turn_split(4 * l, 2 * TURNS_FFN * l)
                ffn(own, 2 * TURNS_FFN * l)
                rms(own, 3 * l + 1, 1, 16 * l + 16, 6 * l + 1)
                turn_rows(4 * l + 1, xT1)
                dve.wait_ge(param_in, 160 * l + 160)
                dve.wait_ge(group_out, 10 * l + 8 + CR)
                nc.vector.memset(prev[0:1, 0], 0.0).then_inc(zero_row, 1)
                pq = proj[:, :, QCOL:VCOL].rearrange("p t (h n) -> p t h n", h=8)
                c = tab[:, T_ROT:T_ROT + 64].rearrange("p (t n) -> p t n", t=NT).unsqueeze(2).to_broadcast([P, NT, 8, 32])
                s = tab[:, T_ROT + 64:T_ROT + 128].rearrange("p (t n) -> p t n", t=NT).unsqueeze(2).to_broadcast([P, NT, 8, 32])
                ta = xn[:, :, 512:768].rearrange("p t (h n) -> p t h n", h=8)
                x1, x2 = pq[:, :, :, 0:32], pq[:, :, :, 32:64]
                dve.wait_ge(xT_psum, 16 * l + 8)
                nc.vector.tensor_tensor(qk[:, :, :, 0:32], x1, c, ALU.mult)
                own(TTop(ta, x2, s, ALU.mult))
                own(TTop(qk[:, :, :, 0:32], qk[:, :, :, 0:32], ta, ALU.subtract))
                nc.vector.tensor_tensor(qk[:, :, :, 32:64], x1, s, ALU.mult)
                own(TTop(ta, x2, c, ALU.mult))
                TTop(qk[:, :, :, 32:64], qk[:, :, :, 32:64], ta, ALU.add).then_inc(qk_rot, 1)
                for h in range(RETH):
                    dve.wait_ge(ret_s, 4 * l + h + 1)
                    if h >= 2:
                        dve.wait_ge(ret_s, 4 * l + 4)
                    TTop(PT[:, h % 2], PS[:, 6 + h % 2, 0:T_DW], dist[:, h], ALU.mult).then_inc(ret_p, 1)
                dve.wait_ge(shift_in, 32 * l + 32)
                pr = proj[:, :, 0:RWKV_IN]
                own(TTop(prev, prev, pr, ALU.subtract))
                own(TTop(prev, prev, row(mu), ALU.mult))
                TTop(pr, pr, prev, ALU.add).then_inc(shifted, 1)
                dve.wait_ge(shifted, l + 1)
                dve.wait_ge(ret_oc, l + 1)
                dve.wait_ge(ret_g, l + 1)
                o = xn[:, :, RW:2 * RW]
                oh = o.rearrange("p t (h n) -> p t h n", h=RETH)
                sq = qk.rearrange("p t h n -> p t (h n)")
                own(TTop(sq, o, o, ALU.mult))
                own(nc.vector.tensor_reduce(rs_in[:, 0:8], sq.rearrange("p t (h n) -> p (t h) n", h=RETH), AX.X, ALU.add))
                nc.vector.tensor_scalar(rs_in[:, 0:8], rs_in[:, 0:8], 1.0 / 128, 1e-6, ALU.mult, ALU.add).then_inc(rs_asked, 1)
                rsqrt(6 * l + 2)
                own(TTop(oh, oh, rs_out[:, 0:8].rearrange("p (t h) -> p t h", t=NT).unsqueeze(3).to_broadcast([P, NT, RETH, 128]), ALU.mult))
                own(TTop(o, o, proj[:, :, GCOL:PROJ], ALU.mult))
                r_, k_, v_ = (proj[:, :, n * RW:(n + 1) * RW] for n in range(3))
                own(TTop(kk, k_, row(par[:, 2]), ALU.mult))
                own(TTop(tmp, kk, kk, ALU.mult))
                own(nc.vector.tensor_reduce(rs_in[:], tmp.rearrange("p t (h n) -> p (t h) n", h=RH), AX.X, ALU.add))
                nc.vector.tensor_scalar(rs_in[:], rs_in[:], 1e-24, None, ALU.max).then_inc(rs_asked, 1)
                dve.wait_ge(lora_out, l + 1)
                TTop(sw, PS[:, 0:2, :], row(par[:, 0]), ALU.add).then_inc(z_ready, 1)
                TTop(av, PS[:, 2:4, :], row(par[:, 1]), ALU.add).then_inc(z_ready, 1)
                rsqrt(6 * l + 3)
                own(TTop(heads(kk), heads(kk), per_head(rs_out[:]), ALU.mult))
                dve.wait_ge(sig_ready, 2 * l + 2)
                dve.wait_ge(exp_ready, l + 1)
                nc.vector.scalar_tensor_tensor(out=tl[:, 0], in0=kk, scalar=-1.0, in1=W3, op0=ALU.mult, op1=ALU.mult)
                own(TTop(tmp, kk, av, ALU.mult))
                TTop(tl[:, 1], tmp, W2, ALU.mult)
                own(nc.vector.scalar_tensor_tensor(out=av, in0=av, scalar=-1.0, in1=row(par[:, 3]), op0=ALU.add, op1=ALU.mult))
                own(nc.vector.scalar_tensor_tensor(out=av, in0=av, scalar=1.0, in1=k_, op0=ALU.add, op1=ALU.mult))
                TTop(tl[:, 2], av, W2, ALU.mult)
                TTop(tl[:, 3], r_, W1, ALU.mult)
                own(TTop(tmp, r_, av, ALU.mult))
                own(TTop(tmp, tmp, row(par[:, 4]), ALU.mult))
                nc.vector.tensor_reduce(bonus[:], tmp.rearrange("p t (h n) -> p (t h) n", h=RH), AX.X, ALU.add).then_inc(tilde, 1)
                dve.wait_ge(tilde, l + 1)
                own(nc.vector.memset(Zs, 0.0))
                lmask = tab[:, T_LMASK:T_LMASK + 512]
                for t in range(NT):
                    dve.wait_ge(tr_psum, 2 * l + t + 1)
                    if t:
                        dve.wait_ge(y_psum, 2 * l + t)
                    nc.vector.tensor_copy(BT.rearrange("p q n -> p (q n)"), PS[:, 2, :])
                    nc.vector.tensor_copy(KT.rearrange("p q n -> p (q n)"), PS[:, 3, :]).then_inc(tr_dve, 1)
                    for h in range(RH):
                        dve.wait_ge(L_psum, 16 * l + 8 * t + h + 1)
                        TTop(Lm[:, h], PS[:, 4 + h % 4, :], lmask, ALU.mult).then_inc(L_ready, 1)
                    for lev in range(6):
                        for hf in range(2):
                            hs = slice(4 * hf, 4 * hf + 4)
                            fl = lambda ap: ap[:, hs].rearrange("p h n -> p (h n)")
                            base = 24 * l + 12 * t + 2 * lev + hf
                            if lev == 0:
                                idb = ident.unsqueeze(1).to_broadcast([P, 4, P])
                                dve.wait_ge(q_psum, base + 1)
                                dve.wait_ge(aoff_ready, base + 1)
                                TTop(TM[:, hs], PS[:, 2 + hf, :].rearrange("p (h n) -> p h n", h=4), idb, ALU.add)
                                TTop(TT[:, hs], Aoff[:, hs], idb, ALU.add).then_inc(t_ready, 1)
                                continue
                            dve.wait_ge(t_psum, 20 * l + 10 * t + 2 * (lev - 1) + hf + 1)
                            dve.wait_ge(t_ready, base - 1)
                            if lev < 5:
                                TTop(fl(TM), fl(TM), PS[:, 4 + hf, :], ALU.add)
                            TTop(fl(TT), fl(TT), PS[:, 6 + hf, :], ALU.add).then_inc(t_ready, 1)
                    for hf in range(2):
                        ch = 2 * t + hf
                        if ch == 3:
                            break
                        dve.wait_ge(z_psum, 3 * l + ch + 1)
                        for b in (0, 64):
                            rows, cols = slice(b, b + 64), slice(b, b + 64)
                            src = PS[rows, 3, :].rearrange("p (q n) -> p q n", q=4)[:, :, cols]
                            dec = decC[rows].rearrange("p (t q f) -> p t q f", t=NT, q=4)[:, t, :, hf].unsqueeze(2).to_broadcast([64, 4, 64])
                            if ch:
                                own(TTop(Ztmp[rows], src, Zs[rows, ch - 1, :, cols], ALU.add))
                                src = Ztmp[rows]
                            own(TTop(Zs[rows, ch, :, cols], src, dec, ALU.mult))
                        dve.sem_inc(z_state, 1)
                dve.wait_ge(y_ready, 2 * l + 2)
                dve.wait_ge(ln_in, 32 * l + 32)
                y = xn[:, :, 0:RW]
                yh = heads(y)
                t1 = tl[:, 3]
                own(nc.vector.tensor_reduce(rs_in[:].rearrange("p (t h) -> p t h", t=NT), yh, AX.X, ALU.add))
                own(nc.vector.tensor_scalar(rs_in[:], rs_in[:], -1.0 / RN, None, ALU.mult))
                own(TTop(yh, yh, per_head(rs_in[:]), ALU.add))
                own(TTop(t1, y, y, ALU.mult))
                own(nc.vector.tensor_reduce(rs_in[:], t1.rearrange("p t (h n) -> p (t h) n", h=RH), AX.X, ALU.add))
                nc.vector.tensor_scalar(rs_in[:], rs_in[:], 1.0 / RN, 64e-5, ALU.mult, ALU.add).then_inc(rs_asked, 1)
                own(TTop(heads(t1), heads(v_), per_head(bonus[:]), ALU.mult))
                rsqrt(6 * l + 4)
                own(TTop(yh, yh, per_head(rs_out[:]), ALU.mult))
                own(TTop(y, y, row(par[:, 0]), ALU.mult))
                own(TTop(y, y, row(par[:, 1]), ALU.add))
                own(TTop(y, y, t1, ALU.add))
                dve.wait_ge(g_ready, l + 1)
                own(TTop(y, y, gt[:], ALU.mult))
                turn_rows(4 * l + 2, xT1)
                for j in range(2):
                    dve.wait_ge(group_done, 10 * l + 8 + j + 1 + CR)
                    xs = x[:, :, j * 512:(j + 1) * 512]
                    TTop(xs, xs, PS[:, 2 * j:2 * j + 2, :], ALU.add).then_inc(group_out, 1)
                dve.wait_ge(group_out, 10 * l + 10 + CR)
                rms(own, 3 * l + 2, 0, 32 * l + 32, 6 * l + 5)
                turn_split(4 * l + 3, 2 * TURNS_FFN * l + TURNS_FFN)
                ffn(own, 2 * TURNS_FFN * l + TURNS_FFN)
                assert own.n == VEC_LAYER, own.n
            own = chain(dve, vec, DEPTH * VEC_LAYER)
            rms(own, 3 * DEPTH, 0, 32 * DEPTH + 16, 6 * DEPTH, x)

            def layer_norm(k, ask):
                for t in range(NT):
                    for c in range(2):
                        own(nc.vector.bn_stats(stats[:, c], x[:, t, c * 512:(c + 1) * 512]))
                    own(nc.vector.bn_aggr(aggr[:, t], stats))
                nc.vector.tensor_scalar(rs_in[:, 0:2], aggr[:, :, 1], 1e-5, None, ALU.add).then_inc(rs_asked, 1)
                dve.wait_ge(gain_in[0], 16 * (2 * DEPTH + 2 + k))
                for t in range(NT):
                    own(nc.vector.scalar_tensor_tensor(out=x[:, t], in0=x[:, t], scalar=aggr[:, t, 0:1], in1=gain[:, 0], op0=ALU.subtract, op1=ALU.mult))
                rsqrt(ask)
                dve.wait_ge(gain_in[1], 16 * (DEPTH + 1 + k))
                for t in range(NT):
                    last = nc.vector.scalar_tensor_tensor(out=x[:, t], in0=x[:, t], scalar=rs_out[:, t:t + 1], in1=gain[:, 1], op0=ALU.mult, op1=ALU.add)
                last.then_inc(norm_done, 1)
                dve.wait_ge(norm_done, 3 * DEPTH + k + 3)

            def residual(n):
                for j in range(2):
                    dve.wait_ge(group_done, n + j + 1 + CR)
                    xs = x[:, :, j * 512:(j + 1) * 512]
                    nc.vector.scalar_tensor_tensor(out=xs, in0=xs, scalar=ALPHA, in1=PS[:, 2 * j:2 * j + 2, :], op0=ALU.mult, op1=ALU.add)\
                        .then_inc(group_out, 1)
                dve.wait_ge(group_out, n + 2 + CR)

            def bc(ap, n):
                return ap.unsqueeze(len(ap.shape)).to_broadcast([*ap.shape, n])

            def pair(ap):
                return ap.rearrange("p (t n) -> p t n", t=NT)

            def window_attention():
                dve.wait_ge(par2_in, 176)
                dve.wait_ge(rw_split, 1)
                nc.vector.tensor_tensor(rwl[:], rw, rwh[:].bitcast(F32), ALU.subtract).then_inc(rw_split, 1)
                own(nc.vector.tensor_copy(posf, pos_i))
                a3 = ang.rearrange("p (k t n) -> p k t n", k=2, t=NT)
                for k in range(2):
                    own(TTop(a3[:, k], bc(posf, 8), inv.unsqueeze(1).to_broadcast([P, NT, 8]), ALU.mult))
                    own(nc.vector.tensor_scalar(turns[:, 16 * k:16 * k + 16], ang[:, 16 * k:16 * k + 16], 1.0 / (2 * np.pi), 0.25 * k, ALU.mult, ALU.add))
                own(nc.vector.tensor_scalar(turns, turns, 12582912.0, None, ALU.add))
                own(nc.vector.tensor_scalar(turns, turns, -12582912.0, None, ALU.add))
                c1 = 6.28125
                c2 = float(np.array(int(np.float32(2 * np.pi - c1).view(np.int32)) & -4096, np.int32).view(np.float32))
                c3 = float(2 * np.pi - c1 - c2)
                src = ang
                for c in (c1, c2, c3):
                    own(nc.vector.scalar_tensor_tensor(out=red, in0=turns, scalar=-c, in1=src, op0=ALU.mult, op1=ALU.add))
                    src = red
                own(nc.vector.tensor_scalar(red[:, 16:32], red[:, 16:32], float(np.pi / 2), None, ALU.add))
                nc.vector.tensor_scalar(red, red, 3.1415925, -3.1415925, ALU.min, ALU.max).then_inc(ang_ready, 1)
                dve.wait_ge(group_out, 24 + CR)
                dve.wait_ge(sin_ready, 1)
                hv = hid[:, :, 0:640].rearrange("p t (h n) -> p t h n", h=10)
                x1, x2 = hv[:, :, :, 0:8], hv[:, :, :, 8:16]
                s, c = (pair(red[:, 16 * k:16 * k + 16]).unsqueeze(2).to_broadcast([P, NT, 10, 8]) for k in range(2))
                ra = RA[:, 4096:4256].rearrange("p (t h n) -> p t h n", t=NT, h=10)
                rb = RA[:, 4256:4416].rearrange("p (t h n) -> p t h n", t=NT, h=10)
                rc = RA[:, 4416:4576].rearrange("p (t h n) -> p t h n", t=NT, h=10)
                TTop(ra, x1, c, ALU.mult)
                TTop(rb, x2, s, ALU.mult)
                TTop(rc, x1, s, ALU.mult)
                own(TTop(ropet, x2, c, ALU.mult))
                own(TTop(x1, ra, rb, ALU.subtract))
                own(TTop(x2, rc, ropet, ALU.add))
                for g in range(2):
                    last = nc.vector.tensor_copy(kdup[:, :, g], hid[:, :, 512 + 64 * g:576 + 64 * g].unsqueeze(2).to_broadcast([P, NT, 2, 64]))
                    last.then_inc(rope_ready, 1)
                dve.wait_ge(gelu_ready, 1)
                v = hid[:, :, 1280:1792]
                vh = v.rearrange("p t (g n) -> p t g n", g=SG)
                own(nc.vector.tensor_reduce(pair(mean), vh, AX.X, ALU.add))
                own(nc.vector.tensor_scalar(mean, mean, -1.0 / 64, None, ALU.mult))
                own(TTop(vh, vh, bc(pair(mean), 64), ALU.add))
                dve.wait_ge(xT_psum, 40)
                own(TTop(tmpA, v, v, ALU.mult))
                own(nc.vector.tensor_reduce(rs_in[:], tmpA.rearrange("p t (g n) -> p (t g) n", g=SG), AX.X, ALU.add))
                nc.vector.tensor_scalar(rs_in[:], rs_in[:], 1.0 / 64, 1e-5, ALU.mult, ALU.add).then_inc(rs_asked, 1)
                rsqrt(6 * DEPTH + 1)
                own(TTop(vh, vh, bc(pair(rs_out[:]), 64), ALU.mult))
                own(TTop(v, v, row(sgu_g), ALU.mult))
                TTop(v, v, row(sgu_bb), ALU.add).then_inc(vg_ready, 1)
                for h in range(QH):
                    dve.wait_ge(sc_psum, h + 1)
                    nc.vector.scalar_tensor_tensor(out=Sc[:, h], in0=PS[:, 4 + h % 4, 0:SW], scalar=HD ** -0.5, in1=swa_mask,
                                                   op0=ALU.mult, op1=ALU.add).then_inc(sc_read, 1)
                dve.wait_ge(sc_read, QH)
                SA, SB = Sc[:, :, 0:P], Sc[:, :, P:SW]
                nc.vector.tensor_reduce(mrow[:, 0:8], SA, AX.X, ALU.max)
                own(nc.vector.tensor_reduce(mrow[:, 8:16], SB, AX.X, ALU.max))
                own(TTop(pair(mrow), pair(mrow), row(sinks), ALU.max))
                TTop(SA, SA, bc(mrow[:, 0:8], P), ALU.subtract)
                TTop(SB, SB, bc(mrow[:, 8:16], 256), ALU.subtract)
                TTop(pair(srow), row(sinks), pair(mrow), ALU.subtract).then_inc(ex_asked, 1)
                dve.wait_ge(sgT_psum, 1)
                TTop(sgT, PS[:, 4:6, :].rearrange("p b (g n) -> p (b g) n", g=4), tri.unsqueeze(1).to_broadcast([P, SG, P]), ALU.mult)\
                    .then_inc(sgT_ready, 1)
                dve.wait_ge(ex_ready, 1)
                nc.vector.tensor_reduce(den[:, 0:8], SA, AX.X, ALU.add)
                own(nc.vector.tensor_reduce(den[:, 8:16], SB, AX.X, ALU.add))
                own(TTop(den, den, srow, ALU.add))
                own(nc.vector.reciprocal(den, den))
                TTop(SA, SA, bc(den[:, 0:8], P), ALU.mult)
                TTop(SB, SB, bc(den[:, 8:16], 256), ALU.mult).then_inc(p_ready, 1)
                dve.wait_ge(sgu_psum, 1)
                TTop(mixg.rearrange("p g t n -> p g (t n)"), PS[:, 6:8, :].rearrange("p b (g n) -> p (b g) n", g=4), bc(sgb, P), ALU.add)\
                    .then_inc(gate_read, 1)
                dve.wait_ge(gate_read, 1)
                for t in range(NT):
                    own(TTop(xn[:, t, 512:1024].rearrange("p (g n) -> p g n", g=SG), mixg[:, :, t], hid[:, t, 768:1280].rearrange("p (g n) -> p g n", g=SG), ALU.mult))
                dve.wait_ge(pv_ready, 1)

            def memory_attention(l):
                dve.wait_ge(xs_psum, l + 1)
                ps = PS[:, 4:8, :].rearrange("p h (t n) -> p (h t) n", t=NT)
                own(nc.vector.tensor_reduce(mrow[:, 0:8], ps, AX.X, ALU.max))
                TTop(px, ps, bc(mrow[:, 0:8], 256), ALU.subtract).then_inc(xe_asked, 1)
                dve.wait_ge(xe_ready, l + 1)
                own(nc.vector.tensor_reduce(den[:, 0:8], px, AX.X, ALU.add))
                own(nc.vector.reciprocal(den[:, 0:8], den[:, 0:8]))
                TTop(px, px, bc(den[:, 0:8], 256), ALU.mult).then_inc(xp_ready, 1)

            def first_of(rank, values, groups):
                n = groups
                v3 = values.rearrange("p (g j) -> p g j", j=4)
                c4 = cmp_[:, 0:16 * n].rearrange("p (g i j) -> p g i j", i=4, j=4)
                e4 = eqs[:, 0:16 * n].rearrange("p (g i j) -> p g i j", i=4, j=4)
                of_j = v3.unsqueeze(2).to_broadcast([P, n, 4, 4])
                of_i = v3.unsqueeze(3).to_broadcast([P, n, 4, 4])
                TTop(c4, of_j, of_i, ALU.is_gt)
                own(TTop(e4, of_j, of_i, ALU.is_equal))
                own(TTop(eqs[:, 0:16 * n].rearrange("p (g k) -> p g k", k=16), eqs[:, 0:16 * n].rearrange("p (g k) -> p g k", k=16),
                         lt.unsqueeze(1).to_broadcast([P, n, 16]), ALU.mult))
                own(TTop(cmp_[:, 0:16 * n], cmp_[:, 0:16 * n], eqs[:, 0:16 * n], ALU.add))
                own(nc.vector.tensor_reduce(rank, cmp_[:, 0:16 * n].rearrange("p (g j) -> p g j", j=4), AX.X, ALU.add))

            def experts(l):
                dve.wait_ge(rt_psum, l + 1)
                own(nc.vector.tensor_reduce(mrow[:, 0:2], pair(PS[:, 0, 0:32]), AX.X, ALU.max))
                own(TTop(pair(lg), pair(PS[:, 0, 0:32]), bc(mrow[:, 0:2], NE), ALU.subtract))
                dve.sem_inc(acc_free, 1)
                dve.sem_inc(re_asked, 1)
                own(nc.vector.tensor_scalar(x[:], x[:], ALPHA, None, ALU.mult))
                t0 = 4 * TURNS_FFN + NE * TURNS_E * l
                step(t0, 0)
                dve.wait_ge(re_ready, l + 1)
                own(nc.vector.tensor_reduce(den[:, 0:2], pair(lg), AX.X, ALU.add))
                own(nc.vector.reciprocal(den[:, 0:2], den[:, 0:2]))
                own(TTop(pair(score), pair(lg), bc(den[:, 0:2], NE), ALU.mult))
                own(TTop(pair(bi), pair(score), row(rbias), ALU.add))
                first_of(wsel, bi, 8)
                own(nc.vector.tensor_scalar(sel, wsel, 1.5, None, ALU.is_lt))
                own(TTop(wsel, sel, bi, ALU.mult))
                own(nc.vector.tensor_reduce(gsum, wsel.rearrange("p (g j) -> p g j", j=4), AX.X, ALU.add))
                first_of(grank, gsum, 2)
                own(nc.vector.tensor_scalar(grank, grank, 0.5, None, ALU.is_lt))
                own(TTop(sel.rearrange("p (g j) -> p g j", j=4), sel.rearrange("p (g j) -> p g j", j=4), bc(grank, 4), ALU.mult))
                own(TTop(sel, sel, score, ALU.mult))
                own(nc.vector.tensor_reduce(den[:, 0:2], pair(sel), AX.X, ALU.add))
                own(nc.vector.reciprocal(den[:, 0:2], den[:, 0:2]))
                own(TTop(pair(comb), pair(sel), bc(den[:, 0:2], NE), ALU.mult))

                def add(e):
                    dve.wait_ge(used[2], 2 * (t0 + TURNS_E * e + TURNS_E) + 1)
                    dve.wait_ge(acc_free, 17 * l + 1 + e)
                    for t in range(NT):
                        last = nc.vector.scalar_tensor_tensor(out=x[:, t], in0=acc[:, t * D:(t + 1) * D], scalar=comb[:, ds(t * NE + e, 1)],
                                                              in1=x[:, t], op0=ALU.mult, op1=ALU.add)
                    last.then_inc(acc_free, 1)

                with dve.Fori(0, NE - 1) as e:
                    t = t0 + TURNS_E * e
                    step(t, 1)
                    step(t + 1, 0)
                    step(t + 1, 1)
                    step(t + 2, 0, between=lambda: add(e))
                t = t0 + TURNS_E * (NE - 1)
                step(t, 1)
                step(t + 1, 0)
                step(t + 1, 1, False)
                add(NE - 1)
                dve.wait_ge(acc_free, 17 * (l + 1))

            turn_rows(8, xT2)
            turn_rows(9, memT)
            for l in range(DEPTH):
                n = 28 if l == 0 else 42
                r = 10 if l == 0 else 16
                if l == 0:
                    window_attention()
                    turn_rows(10, xT2)
                    r = 11
                else:
                    turn_rows(15, xT2)
                    for j in range(2):
                        dve.wait_ge(group_done, 40 + j + 1 + CR)
                        TTop(mapT[:, 4 * j:4 * j + 4], PS[:, 2 * j:2 * j + 2, :].rearrange("p b (k s) -> p (b k) s", k=2),
                             bc(pscale[:, 4 * j:4 * j + 4], S), ALU.mult).then_inc(group_out, 1)
                residual(n)
                layer_norm(3 * l, 6 * DEPTH + 2 + 3 * l)
                turn_rows(r, xT2)
                memory_attention(l)
                turn_rows(r + 1, xT2)
                residual(n + 4)
                layer_norm(3 * l + 1, 6 * DEPTH + 3 + 3 * l)
                turn_split(r + 2, 4 * TURNS_FFN + NE * TURNS_E * l)
                experts(l)
                layer_norm(3 * l + 2, 6 * DEPTH + 4 + 3 * l)
                if l == 0:
                    turn_rows(14, xT2)

        @block.tensor
        def _(pe):
            mm = nc.tensor.matmul
            pe.wait_ge(tab_in, 32)
            pe.wait_ge(setup, 3)
            for m in range(3):
                pe.sem_inc(used[m], 1)
            pe.sem_inc(chunk_used, 4)
            pe.sem_inc(group_done, CR)
            pe.sem_inc(group_out, CR)

            def turn_rows(r, src=xn):
                pe.wait_ge(xn_ready, r + 1)
                for b in range(4):
                    for n in range(4):
                        last = nc.tensor.transpose(PS[:, 4 + b, n * P:(n + 1) * P], src[:, n % 2, (2 * b + n // 2) * P:(2 * b + n // 2 + 1) * P], ident)
                    last.then_inc(xT_psum, 1)
                turned(r)

            def turned(r):
                pe.wait_ge(xT_act, 4 * r + 4)
                hold(pe, xT_dve, 4 * r + 4)

            def gate_up(turn, j):
                for m in range(2):
                    pe.wait_ge(lo_done[m], 2 * turn + j + 1 + CR)
                    if m == 0:
                        pe.wait_ge(hT_ready, 2 * turn + j + 1)
                    for k in range(KB):
                        out_, ks = PS[:, 4 + j, m * S:(m + 1) * S], slice(k * P, (k + 1) * P)
                        mm(out_, whi[:, m, ks], xTh[:, k, :], start=(k == 0), stop=False)
                        mm(out_, whi[:, m, ks], xTl[:, k, :], start=False, stop=False)
                        last = mm(out_, wlo[:, m, ks], xTh[:, k, :], start=False, stop=(k == KB - 1))
                    last.then_inc(used[m], 1)

            def down(turn, j, opens=None):
                pe.wait_ge(lo_done[2], 2 * turn + j + 1 + CR)
                pe.wait_ge(hT_ready, 2 * turn + j + 1 + CR)
                if opens is not None:
                    pe.wait_ge(acc_free, opens)
                for t in range(NT):
                    ts = slice(t * P, (t + 1) * P)
                    for n in range(2):
                        out_, ns = PS[:, 2 * t + n, :], slice(n * 512, (n + 1) * 512)
                        mm(out_, hTh[:, j, ts], whi[:, 2, ns], start=(opens is not None), stop=False, skip_group_check=True)
                        mm(out_, hTh[:, j, ts], wlo[:, 2, ns], start=False, stop=False, skip_group_check=True)
                        last = mm(out_, hTl[:, j, ts], whi[:, 2, ns], start=False, stop=False, skip_group_check=True)
                last.then_inc(used[2], 1)

            def step(turn, j, opens=None):
                gate_up(turn + j, 1 - j)
                down(turn, j, opens)

            def ffn(t0):
                for b in range(4):
                    mm(PS[:, b, :], zero[:, 0:P], zero[:], start=True, stop=False, skip_group_check=True)
                gate_up(t0, 0)
                with pe.Fori(0, TURNS_FFN - 1) as g:
                    for j in range(2):
                        step(t0 + g, j)
                step(t0 + TURNS_FFN - 1, 0)
                down(t0 + TURNS_FFN - 1, 1)

            def experts(t0, free):
                gate_up(t0, 0)
                step(t0, 0, free)
                with pe.Fori(0, NE - 1) as e:
                    t = t0 + TURNS_E * e
                    step(t, 1)
                    step(t + 1, 0)
                    step(t + 1, 1)
                    step(t + 2, 0, free + 1 + e)
                t = t0 + TURNS_E * (NE - 1)
                step(t, 1)
                step(t + 1, 0)
                down(t + 1, 1)

            def group(n, n4, slot, width, lhs):
                pe.wait_ge(group_out, n + 1)
                for c in range(4):
                    pe.wait_ge(chunk_in[c], 16 * n4 + 16)
                    w = chunk_raw(c, 2, width)
                    for t in range(NT):
                        for i in range(2):
                            last = mm(PS[:, 2 * slot + t, 0:width], lhs[:, 2 * c + i, t * P:(t + 1) * P], w[:, i, :],
                                      start=(c == 0 and i == 0), stop=(c == 3 and i == 1))
                    last.then_inc(chunk_used, 1)
                pe.wait_ge(chunk_used, 4 * n4 + 4 + 4)
                pe.sem_inc(group_done, 1)

            with pe.Fori(0, DEPTH) as l:
                turn_rows(4 * l)
                ffn(2 * TURNS_FFN * l)
                turn_rows(4 * l + 1)
                with pe.Fori(0, 4) as g:
                    for j in range(2):
                        n = 10 * l + 2 * g + j
                        group(n, n, j, GW, xT1)
                pe.wait_ge(qk_rot, l + 1)
                for q in range(4):
                    for t in range(NT):
                        n = 2 * q + t
                        last = nc.tensor.transpose(PS[:, 4 + n // 4, (n % 4) * P:(n % 4 + 1) * P],
                                                   qk[:, t, 2 * q:2 * q + 2, :].rearrange("p h n -> p (h n)"), ident)
                last.then_inc(qkT_psum, 1)
                pe.wait_ge(qkT_ready, l + 1)
                pe.wait_ge(group_out, 10 * l + 8 + CR)

                def scores(h):
                    b, q = 64 * (h % 2), h // 2
                    if h >= 2:
                        pe.wait_ge(ret_p, 4 * l + h - 1)
                    mm(PS[:, 6 + h % 2, 0:S], qkT[b:b + 64, 2 + q, 0, :], qkT[b:b + 64, q, :, :].rearrange("p t n -> p (t n)"), start=True, stop=True)
                    mm(PS[:, 6 + h % 2, S:S + P], qkT[b:b + 64, 2 + q, 1, :], qkT[b:b + 64, q, 1, :], start=True, stop=True).then_inc(ret_s, 1)

                def values(h):
                    pe.wait_ge(ret_p, 4 * l + h + 1)
                    v = [proj[:, t, VCOL + h * P:VCOL + (h + 1) * P] for t in range(NT)]
                    o = [PS[:, t, h * P:(h + 1) * P] for t in range(NT)]
                    mm(o[0], PT[:, h % 2, 0:P], v[0], start=True, stop=True)
                    mm(o[1], PT[:, h % 2, P:2 * P], v[0], start=True, stop=False)
                    return mm(o[1], PT[:, h % 2, 2 * P:3 * P], v[1], start=False, stop=True)

                scores(0)
                scores(1)
                values(0)
                scores(2)
                values(1)
                scores(3)
                values(2)
                values(3).then_inc(ret_o, 1)
                pe.wait_ge(lora_act, 2 * l + 2)
                pe.wait_ge(shifted, l + 1)
                for b in range(2):
                    for t in range(NT):
                        last = nc.tensor.transpose(PS[:, 4, (2 * b + t) * P:(2 * b + t + 1) * P], proj[:, t, 1536 + b * P:1536 + (b + 1) * P], ident)
                last.then_inc(lT_psum, 1)
                pe.wait_ge(lT_ready, l + 1)
                pe.wait_ge(ret_oc, l + 1)
                pe.wait_ge(param_in, 160 * l + 160)
                for t in range(NT):
                    ts = slice(t * P, (t + 1) * P)
                    mm(PS[:, t, :], lT[0:64, 0, ts], WL[0:64], start=True, stop=True)
                    mm(PS[:, 2 + t, :], lT[64:128, 0, ts], WL[64:128], start=True, stop=True)
                    last = mm(PS[:, 6 + t, :], lT[:, 1, ts], GL, start=True, stop=True)
                last.then_inc(lora_out, 1)
                pe.wait_ge(z_ready, 2 * l + 2)
                pe.wait_ge(sig_ready, 2 * l + 1)
                for t in range(NT):
                    mm(PS[:, t, :], tab[:, T_CUMI:T_CUMI + P], sw[:, t], start=True, stop=True)
                    mm(PS[:, 2 + t, :], tab[:, T_CUMX:T_CUMX + P], sw[:, t], start=True, stop=True)
                    for q in range(4):
                        c0 = (4 * t + q) * 2
                        last = mm(PS[:, 5, c0:c0 + 2], sw[:, t, q * P:(q + 1) * P], tab[:, T_TOT:T_TOT + 2], start=True, stop=True)
                last.then_inc(cum_psum, 1)
                pe.wait_ge(tilde, l + 1)
                for t in range(NT):
                    if t:
                        pe.wait_ge(y_ready, 2 * l + t)
                        pe.wait_ge(z_state, 3 * l + 2)
                    for q in range(4):
                        qs = slice(q * P, (q + 1) * P)
                        nc.tensor.transpose(PS[:, q // 2, (q % 2) * 256:(q % 2) * 256 + P], tl[:, 0, t, qs], ident)
                        nc.tensor.transpose(PS[:, q // 2, (q % 2) * 256 + P:(q % 2) * 256 + 256], tl[:, 3, t, qs], ident)
                        nc.tensor.transpose(PS[:, 2, qs], tl[:, 1, t, qs], ident)
                        last = nc.tensor.transpose(PS[:, 3, qs], tl[:, 2, t, qs], ident)
                    last.then_inc(tr_psum, 1)
                    pe.wait_ge(tr_act, 2 * l + t + 1)
                    pe.wait_ge(tr_dve, 2 * l + t + 1)
                    for h in range(RH):
                        b, q = 64 * (h % 2), h // 2
                        if h >= 4:
                            pe.wait_ge(L_ready, 16 * l + 8 * t + h - 3)
                        mm(PS[:, 4 + h % 4, 0:256], BT[b:b + 64, q, :], ART[b:b + 64, q, :], start=True, stop=True)
                        mm(PS[:, 4 + h % 4, 256:512], KT[b:b + 64, q, :], ART[b:b + 64, q, :], start=True, stop=True).then_inc(L_psum, 1)
                    v = [proj[:, t, 2 * RW + h * RN:2 * RW + (h + 1) * RN] for h in range(RH)]
                    for h in range(RH):
                        pe.wait_ge(L_ready, 16 * l + 8 * t + h + 1)
                        last = mm(PS[:, 0, h * RN:(h + 1) * RN], Lm[:, h, 256:384], v[h], start=True, stop=True)
                    last.then_inc(av_psum, 1)
                    for lev in range(6):
                        for hf in range(2):
                            base = 24 * l + 12 * t + 2 * lev + hf
                            pe.wait_ge(aoff_ready, base + 1)
                            if lev:
                                pe.wait_ge(t_ready, base - 1)
                                if lev > 1:
                                    pe.wait_ge(q_ready, 20 * l + 10 * t + 2 * (lev - 2) + hf + 1)
                            for h in range(4 * hf, 4 * hf + 4):
                                last = mm(PS[:, 2 + hf, (h % 4) * P:(h % 4 + 1) * P], Aoff[:, h], TM[:, h] if lev else ident, start=True, stop=True)
                            last.then_inc(q_psum, 1)
                        if lev == 0:
                            continue
                        for hf in range(2):
                            pe.wait_ge(q_ready, 20 * l + 10 * t + 2 * (lev - 1) + hf + 1)
                            for h in range(4 * hf, 4 * hf + 4):
                                hs = slice((h % 4) * P, (h % 4 + 1) * P)
                                if lev < 5:
                                    mm(PS[:, 4 + hf, hs], TT[:, h], QM[:, h], start=True, stop=True)
                                last = mm(PS[:, 6 + hf, hs], QM[:, h], TT[:, h], start=True, stop=True)
                            last.then_inc(t_psum, 1)
                    pe.wait_ge(t_ready, 24 * l + 12 * t + 12)
                    for h in range(RH):
                        b, q = 64 * (h % 2), h // 2
                        last = mm(PS[b:b + 64, 1, q * P:(q + 1) * P], tl[:, 0, t, h * RN:(h + 1) * RN], TT[:, h], start=True, stop=True)
                    last.then_inc(gT_psum, 1)
                    pe.wait_ge(av_ready, 2 * l + t + 1)
                    for hf in range(2):
                        ch = 2 * t + hf
                        rows = slice(64 * hf, 64 * hf + 64)
                        if hf == 0:
                            for h in range(RH):
                                last = mm(PS[:, 2, h * RN:(h + 1) * RN], TT[:, h], AV[:, h * RN:(h + 1) * RN],
                                          start=(h == 0), stop=False, skip_group_check=True)
                            pe.wait_ge(gT_ready, 2 * l + t + 1)
                        if ch:
                            pe.wait_ge(z_state, 3 * l + ch)
                            for q in range(4):
                                last = mm(PS[rows, 2, q * P:(q + 1) * P], tl[:, 3, t, q * P + 64 * hf:q * P + 64 * hf + 64],
                                          Zs[:, ch - 1, q, :], start=False, stop=False, skip_group_check=True)
                        last.then_inc(u_psum, 1)
                        pe.wait_ge(u_ready, 4 * l + ch + 1)
                        if ch == 3:
                            break
                        for q in range(4):
                            qs = slice(q * P, (q + 1) * P)
                            mm(PS[:, 3, qs], tl[rows, 1, t, qs], U[rows, qs], start=True, stop=False)
                            last = mm(PS[:, 3, qs], tl[rows, 2, t, qs], proj[rows, t, 2 * RW + q * P:2 * RW + (q + 1) * P], start=False, stop=True)
                        last.then_inc(z_psum, 1)
                    for h in range(RH):
                        b, q = 64 * (h % 2), h // 2
                        hs = slice(h * RN, (h + 1) * RN)
                        mm(PS[:, 1, hs], Lm[:, h, 128:256], U[:, hs], start=(h == 0), stop=False, skip_group_check=True)
                        mm(PS[:, 1, hs], Lm[:, h, 384:512], v[h], start=False, stop=False, skip_group_check=True)
                    for q in range(4):
                        for hf in range(2):
                            ch = 2 * t + hf
                            if ch:
                                last = mm(PS[64 * hf:64 * hf + 64, 1, q * P:(q + 1) * P], ART[:, q, P + 64 * hf:P + 64 * hf + 64],
                                          Zs[:, ch - 1, q, :], start=False, stop=False, skip_group_check=True)
                    last.then_inc(y_psum, 1)
                turn_rows(4 * l + 2)
                for j in range(2):
                    group(10 * l + 8 + j, 10 * l + 8 + j, j, 512, xT1)
                turn_rows(4 * l + 3)
                ffn(2 * TURNS_FFN * l + TURNS_FFN)
            n4 = 10 * DEPTH

            def group2(n, width, lhs):
                nonlocal n4
                group(n, n4, n % 2, width, lhs)
                n4 += 1

            def group_turned(n, rhs):
                nonlocal n4
                slot = n % 2
                pe.wait_ge(group_out, n + 1)
                for c in range(4):
                    pe.wait_ge(chunk_in[c], 16 * n4 + 16)
                    w = chunk_raw(c, 2, 512)
                    for f in range(4):
                        for i in range(2):
                            last = mm(PS[:, 2 * slot + f // 2, (f % 2) * S:(f % 2 + 1) * S], w[:, i, f * P:(f + 1) * P], rhs[:, 2 * c + i, :],
                                      start=(c == 0 and i == 0 and f % 2 == 0), stop=(c == 3 and i == 1), skip_group_check=True)
                    last.then_inc(chunk_used, 1)
                pe.wait_ge(chunk_used, 4 * n4 + 4 + 4)
                pe.sem_inc(group_done, 1)
                n4 += 1

            turn_rows(8, x)
            pe.wait_ge(par2_in, 176)
            turn_rows(9, mem)
            for l in range(DEPTH):
                n = 20 + 14 * l
                for j in range(4 if l == 0 else 2):
                    group2(n + j, W0 if l == 0 else 512, xT2)
                n += 4 if l == 0 else 2
                for j in range(2):
                    group_turned(n + j, memT)
                if l == 0:
                    pe.wait_ge(rope_ready, 2)
                    for q in range(4):
                        for t in range(NT):
                            i = 2 * q + t
                            nc.tensor.transpose(PS[:, 4 + i // 4, (i % 4) * P:(i % 4 + 1) * P], hid[:, t, q * P:(q + 1) * P], ident)
                    for g in range(2):
                        for t in range(NT):
                            i = 2 * g + t
                            last = nc.tensor.transpose(PS[:, 6, i * P:(i + 1) * P], kdup[:, t, g].rearrange("p c n -> p (c n)"), ident)
                    last.then_inc(swT_psum, 1)
                    pe.wait_ge(swT_ready, 1)
                    for h in range(QH):
                        b, q, g = 64 * (h % 2), h // 2, h // 4
                        if h >= 4:
                            pe.wait_ge(sc_read, h - 3)
                        mm(PS[:, 4 + h % 4, 0:P], qT2[b:b + 64, q, 0], kT2[b:b + 64, g, 0], start=True, stop=True)
                        mm(PS[:, 4 + h % 4, P:SW], qT2[b:b + 64, q, 1], kT2[b:b + 64, g].rearrange("p t n -> p (t n)"), start=True, stop=True)\
                            .then_inc(sc_psum, 1)
                    pe.wait_ge(sc_read, QH)
                    for g in range(SG):
                        last = nc.tensor.transpose(PS[:, 4 + g // 4, (g % 4) * P:(g % 4 + 1) * P], sgw[:, g], ident)
                    last.then_inc(sgT_psum, 1)
                for j in range(2):
                    group2(n + 2 + j, 512, memT)
                n += 4
                if l == 0:
                    pe.wait_ge(sgT_ready, 1)
                    pe.wait_ge(vg_ready, 1)
                    vg = hid[:, :, 1280:1792]
                    for g in range(SG):
                        last = mm(PS[:, 6 + g // 4, (g % 4) * P:(g % 4 + 1) * P], sgT[:, g], vg[:, :, g * 64:(g + 1) * 64], start=True, stop=True)
                    last.then_inc(sgu_psum, 1)
                    pe.wait_ge(p_ready, 1)
                    pe.wait_ge(group_out, n + CR)
                    for half in range(2):
                        for i in range(12):
                            h, b3 = 4 * half + i // 3, i % 3
                            last = nc.tensor.transpose(PS[:, 3 * half + i // 4, (i % 4) * P:(i % 4 + 1) * P], Sc[:, h, b3 * P:(b3 + 1) * P], ident)
                        last.then_inc(pT_psum, 1)
                    pe.wait_ge(pT_ready, 2)
                    pe.wait_ge(gate_read, 1)
                    for h in range(QH):
                        ks = slice(640 + 64 * (h // 4), 704 + 64 * (h // 4))
                        os_ = slice(h * HD, (h + 1) * HD)
                        mm(PS[:, 6, os_], pTw[:, h, 0], hid[:, 0, ks], start=True, stop=True)
                        mm(PS[:, 7, os_], pTw[:, h, 1], hid[:, 0, ks], start=True, stop=False)
                        last = mm(PS[:, 7, os_], pTw[:, h, 2], hid[:, 1, ks], start=False, stop=True)
                    last.then_inc(pv_psum, 1)
                    turn_rows(10)
                    lhs = xT2
                    r = 11
                else:
                    pe.wait_ge(pool_in, 16)
                    for k in range(KB):
                        for t in range(NT):
                            last = mm(PS[:, 4 + k // 2, (k % 2) * S:(k % 2 + 1) * S], hid1[:, t, k * P:(k + 1) * P], pool_t[:, k // 2, t],
                                      start=(t == 0), stop=(t == NT - 1))
                        if k % 2:
                            last.then_inc(xT_psum, 1)
                    turned(15)
                    for j in range(2):
                        pe.wait_ge(group_out, n + 1)
                        for g in range(2):
                            pe.wait_ge(chunk_in[2 * j + g], 16 * n4 + 16)
                            w = chunk_raw(2 * j + g, 2, S)
                            for d in range(2):
                                for c in range(2):
                                    last = mm(PS[:, 2 * j + g, d * S:(d + 1) * S], w[:, c, d * P:(d + 1) * P],
                                              xT2[:, 2 * (2 * j + g) + c, :], start=(c == 0), stop=(c == 1))
                            last.then_inc(chunk_used, 1)
                        pe.wait_ge(chunk_used, 4 * n4 + 2 * j + 2 + 4)
                        pe.sem_inc(group_done, 1)
                        n += 1
                    n4 += 1
                    pe.wait_ge(group_out, n + CR)
                    lhs = mapT
                    r = 16
                for j in range(2):
                    group2(n + j, 512, lhs)
                n += 2
                turn_rows(r, x)
                for j in range(2):
                    group_turned(n + j, xT2)
                n += 2
                pe.wait_ge(group_out, n + CR)
                for h in range(XH):
                    for t in range(NT):
                        for d in range(2):
                            last = mm(PS[:, 4 + h, t * S:(t + 1) * S], qT[:, 2 * h + d, t * P:(t + 1) * P], kT[:, 2 * h + d, :],
                                      start=(d == 0), stop=(d == 1))
                last.then_inc(xs_psum, 1)
                pe.wait_ge(xp_ready, l + 1)
                for h in range(XH):
                    for m in range(NT):
                        for t in range(NT):
                            last = nc.tensor.transpose(PS[:, h, m * S + t * P:m * S + (t + 1) * P], px[:, 2 * h + t, m * P:(m + 1) * P], ident)
                last.then_inc(xpT_psum, 1)
                pe.wait_ge(xpT_ready, l + 1)
                for h in range(XH):
                    for d in range(2):
                        for m in range(NT):
                            last = mm(PS[:, 4 + h, d * S:(d + 1) * S], vM[:, m, (2 * h + d) * P:(2 * h + d + 1) * P], pxT[:, h, m, :],
                                      start=(m == 0), stop=(m == NT - 1))
                    last.then_inc(xT_psum, 1)
                turned(r + 1)
                for j in range(2):
                    group2(n + j, 512, xT2)
                turn_rows(r + 2, x)
                pe.wait_ge(rw_split, 2)
                for t in range(NT):
                    for k in range(KB):
                        out_, ts = PS[:, 0, t * NE:(t + 1) * NE], slice(t * P, (t + 1) * P)
                        mm(out_, xTh[:, k, ts], rwh[:, k, :], start=(k == 0), stop=False)
                        mm(out_, xTh[:, k, ts], rwl[:, k, :], start=False, stop=False)
                        last = mm(out_, xTl[:, k, ts], rwh[:, k, :], start=False, stop=(k == KB - 1))
                last.then_inc(rt_psum, 1)
                experts(4 * TURNS_FFN + NE * TURNS_E * l, 17 * l + 1)
                if l == 0:
                    turn_rows(14, x)


_INS = ["x", "ffn1_norm", "ffn1_w_gate", "ffn1_w_up", "ffn1_w_down", "mix_norm", "w_in", "shift_mu", "w0", "w_lora_up",
        "a0", "a_lora_up", "g_lora_up", "k_k", "k_a", "r_k", "ln_x_w", "ln_x_b", "w_out", "ffn2_norm", "ffn2_w_gate",
        "ffn2_w_up", "ffn2_w_down", "final_norm", "mem_2", "positions_2", "router_w_2", "router_bias_2",
        "l0_w_in_2", "l0_sinks_2", "l0_sgu_ln_g_2", "l0_sgu_ln_b_2", "l0_sgu_w_2", "l0_sgu_b_2", "l0_w_out_2",
        "l0_ln1_g_2", "l0_ln1_b_2", "l0_xq_2", "l0_xkv_2", "l0_xo_2", "l0_ln2_g_2", "l0_ln2_b_2", "l0_e_gate_2",
        "l0_e_up_2", "l0_e_down_2", "l0_ln3_g_2", "l0_ln3_b_2", "l1_w_in_2", "l1_pool_w_2", "l1_pool_scale_2",
        "l1_w_out_2", "l1_ln1_g_2", "l1_ln1_b_2", "l1_xq_2", "l1_xkv_2", "l1_xo_2", "l1_ln2_g_2", "l1_ln2_b_2",
        "l1_e_gate_2", "l1_e_up_2", "l1_e_down_2", "l1_ln3_g_2", "l1_ln3_b_2"]


def kernel(**inputs):
    import concourse.bacc as bacc
    from concourse.bass_utils import run_bass_kernel_spmd as run

    nc = bacc.Bacc("TRN2", target_bir_lowering=False, num_devices=1)
    arrays, args = {}, {}
    for name in _INS + ["tables"]:
        a = tables() if name == "tables" else np.ascontiguousarray(inputs[name])
        arrays[f"in_{name}_dram"] = a
        args[name] = nc.dram_tensor(f"in_{name}_dram", a.shape, mybir.dt.from_np(a.dtype), kind="ExternalInput").ap()
    out = nc.dram_tensor("out_0_dram", (1, S, D), F32, kind="ExternalOutput").ap()
    both_blocks(nc, args, out)
    r = run(nc, [arrays], core_ids=[0])
    return r.results[0]["out_0_dram"]
```

```python
from contextlib import ExitStack

import numpy as np

import concourse.bass as bass
from concourse import mybir

F32 = mybir.dt.float32
F32R = mybir.dt.float32r
BF16 = mybir.dt.bfloat16
I32 = mybir.dt.int32
ALU = mybir.AluOpType
ACT = mybir.ActivationFunctionType
AX = mybir.AxisListType
ds = bass.ds

P = 128
D = 1024
S = 256
NT = S // P
KB = D // P
DEPTH = 2
FF = 2816
CHUNK = 64
RH, RN = 8, 64
RW = RH * RN
LORA = 256
RWKV_IN = 3 * RW + LORA
RET_IN = 1536
PROJ = RWKV_IN + RET_IN
QCOL = RWKV_IN
VCOL = QCOL + 512
GCOL = VCOL + 512
RETH = 4
DECAY = -float(np.exp(-0.5))
GW = 416

STEPS_FFN = FF // P
TURNS_FFN = STEPS_FFN // 2

T_IDENT, T_CUMI, T_CUMX, T_TOT, T_LMASK, T_LEV, T_ROT, T_DIST = 0, 128, 256, 384, 392, 904, 1672, 1800
T_RES = T_DIST
T_DW = 384
T2 = T_DIST + RETH * T_DW
T_SWA, T_TRI, T_INV, T_LT = 0, 384, 512, 520
T2_SMALL = 536
T_POOL = T2 + T2_SMALL
T_ALL = T_POOL + 4 * NT * S

ALPHA = (2.0 * DEPTH) ** 0.25
W0 = 448
QH, HD = 8, 64
SW = 384
SG = 8
XH = 4
NE = 16
TURNS_E = 2
POOLS = (2, 4, 8, 16)


def tables():
    t = np.zeros((P, T_ALL), np.float64)
    j = np.arange(P)[:, None]
    i = np.arange(P)[None, :]
    same = j // CHUNK == i // CHUNK
    t[:, T_IDENT:T_IDENT + P] = j == i
    t[:, T_CUMI:T_CUMI + P] = DECAY * (same & (j <= i))
    t[:, T_CUMX:T_CUMX + P] = DECAY * (same & (j < i))
    t[:, T_TOT:T_TOT + 2] = DECAY * (j // CHUNK == np.arange(2)[None, :])
    for n in range(4):
        t[:, T_LMASK + n * P:T_LMASK + (n + 1) * P] = same & ((j < i) if n % 2 == 0 else (j <= i))
    for n in range(6):
        s = 2 ** n
        t[:, T_LEV + n * P:T_LEV + (n + 1) * P] = (j // (2 * s) == i // (2 * s)) & (j % (2 * s) < s) & (i % (2 * s) >= s)
    half = 32
    inv = (1.0 / (np.float32(10000.0) ** np.linspace(0.0, 1.0, half, dtype=np.float32))).astype(np.float32)
    for n in range(NT):
        ang = ((np.arange(P) + n * P).astype(np.float32)[:, None] * inv[None, :]).astype(np.float32).astype(np.float64)
        t[:, T_ROT + n * 32:T_ROT + (n + 1) * 32] = np.cos(ang)
        t[:, T_ROT + 64 + n * 32:T_ROT + 64 + (n + 1) * 32] = np.sin(ang)
    for h in range(RETH):
        lg = np.log(1.0 - 2.0 ** (-5.0 - h))
        for c0, js, qs in ((0, np.arange(P), np.arange(S)), (S, np.arange(P) + P, np.arange(P) + P)):
            w = np.exp(lg * np.abs(qs[None, :] - js[:, None])) * (js[:, None] // CHUNK <= qs[None, :] // CHUNK) / 8.0
            t[:, T_DIST + h * T_DW + c0:T_DIST + h * T_DW + c0 + len(qs)] = w
    q = np.arange(P)[:, None]
    t[:, T2:T2 + P] = np.where(i <= q, 0.0, -1e30)
    t[:, T2 + P:T2 + 2 * P] = np.where(i > q, 0.0, -1e30)
    t[:, T2 + 2 * P:T2 + 3 * P] = np.where(i <= q, 0.0, -1e30)
    t[:, T2 + T_TRI:T2 + T_TRI + P] = j <= i
    t[:, T2 + T_INV:T2 + T_INV + 8] = (np.float32(500000.0) ** (-(np.arange(8, dtype=np.float32) * 2.0 / 16))).astype(np.float32)
    t[:, T2 + T_LT:T2 + T_LT + 16] = [b < a for a in range(4) for b in range(4)]
    to = np.arange(S)[None, :]
    for g, win in enumerate(POOLS):
        for n in range(NT):
            js = np.arange(P)[:, None] + n * P
            c0 = T_POOL + (g * NT + n) * S
            t[:, c0:c0 + S] = ((js <= to) & (js > to - win)) / np.minimum(to + 1, win) - (js == to)
    return t.astype(np.float32)


VEC_LAYER = 65

RSQ = 7
SPLIT_AT = (0, 1, 2, 1)
CR = 2


def both_blocks(nc, A, out):
    ctx = ExitStack()
    with ctx:
        def sb(name, shape, dt=F32):
            return ctx.enter_context(nc.sbuf_tensor(name, shape, dt))

        def sem(name):
            return ctx.enter_context(nc.semaphore(name))

        PS = ctx.enter_context(nc.psum_tensor("PS", [P, 8, 512], F32))
        tab = sb("tab", [P, T_RES])
        x = sb("x", [P, NT, D])
        xn = sb("xn", [P, NT, D])
        xTh = sb("xTh", [P, KB, S], F32R)
        xTl = sb("xTl", [P, KB, S], F32R)
        gain = sb("gain", [P, 2, D])
        raw = sb("raw", [P, 3, 2, 1024])
        whi = sb("whi", [P, 3, 1024], F32R)
        wlo = sb("wlo", [P, 3, 1024], F32R)
        gs = sb("gs", [P, 2, S])
        h32 = sb("h32", [P, 2, S])
        hTh = sb("hTh", [P, 2, S], F32R)
        hTl = sb("hTl", [P, 2, S], F32R)
        rws = sb("rws", [P, KB, 2, NE], F32R)
        zero = sb("zero", [P, 512], BF16)
        rs_in = sb("rs_in", [P, 16])
        rs_out = sb("rs_out", [P, 16])
        neg_half = sb("neg_half", [P, 16])
        bonus = sb("bonus", [P, 16])
        decC = sb("decC", [P, 16])
        proj = sb("proj", [P, NT, PROJ])
        par = sb("par", [P, 5, RW])
        RA = sb("RA", [P, 5376])
        RB = sb("RB", [P, 5888])
        gt = sb("gt", [P, NT, RW])
        tl = sb("tl", [P, 4, NT, RW])

        ident = tab[:, T_IDENT:T_IDENT + P]
        acc = PS[:, 0:4, :].rearrange("p b n -> p (b n)")

        prev = RA[:, 0:3584].rearrange("p (t n) -> p t n", t=NT)
        mu = RA[:, 3584:5376]

        def two(base, n):
            return base[:, 1024 * n:1024 * (n + 1)].rearrange("p (t c) -> p t c", t=NT)

        sw, av, W1, W2, W3 = (two(RA, n) for n in range(5))
        Lm = RA[:, 0:4096].rearrange("p (h n) -> p h n", h=RH)
        ART = RA[:, 4096:5120].rearrange("p (q n) -> p q n", q=4)
        WL = RB[:, 0:512]
        GL = RB[:, 512:1024]
        lT = RB[:, 1024:1536].rearrange("p (b s) -> p b s", b=2)
        kk = RB[:, 1536:2560].rearrange("p (t c) -> p t c", t=NT)
        tmp = RB[:, 2560:3584].rearrange("p (t c) -> p t c", t=NT)
        dist = RB[:, 1536:3072].rearrange("p (h n) -> p h n", h=RETH)
        qk = RB[:, 3072:4096].rearrange("p (t h n) -> p t h n", t=NT, h=8)
        qkT = RB[:, 4096:5120].rearrange("p (q t n) -> p q t n", q=4, t=NT)
        PT = RB[:, 5120:5888].rearrange("p (b n) -> p b n", b=2)
        TM = RB[:, 0:1024].rearrange("p (h n) -> p h n", h=RH)
        TT = RB[:, 1024:2048].rearrange("p (h n) -> p h n", h=RH)
        Aoff = RB[:, 2048:3072].rearrange("p (h n) -> p h n", h=RH)
        QM = RB[:, 3072:4096].rearrange("p (h n) -> p h n", h=RH)
        Zs = RB[:, 4096:5632].rearrange("p (c q n) -> p c q n", c=3, q=4)
        Ztmp = RB[:, 5632:5888].rearrange("p (q n) -> p q n", q=4)
        xTf = raw[:, 2].rearrange("p s n -> p (s n)")
        BT = xTf[:, 0:512].rearrange("p (q n) -> p q n", q=4)
        KT = xTf[:, 512:1024].rearrange("p (q n) -> p q n", q=4)
        U = xTf[:, 1024:1536]
        AV = xTf[:, 1536:2048]

        h2 = proj[:].rearrange("p t n -> p (t n)")
        hid = h2[:, 0:3584].rearrange("p (t n) -> p t n", t=NT)
        Sc = h2[:, 3584:6656].rearrange("p (h n) -> p h n", h=QH)
        hid1 = h2[:, 0:2048].rearrange("p (t n) -> p t n", t=NT)
        pool_t = h2[:, 2048:4096].rearrange("p (g t n) -> p g t n", g=4, t=NT)
        pf = par[:].rearrange("p a n -> p (a n)")
        swa_mask = pf[:, T_SWA:T_SWA + SW]
        tri = pf[:, T_TRI:T_TRI + P]
        inv = pf[:, T_INV:T_INV + 8]
        lt = pf[:, T_LT:T_LT + 16]
        sinks = pf[:, 536:544]
        rbias = pf[:, 544:560]
        pscale = pf[:, 560:568]
        sgb = pf[:, 568:576]
        rw = pf[:, 576:704].rearrange("p (k e) -> p k e", k=KB)
        sgu_g, sgu_bb = pf[:, 704:1216], pf[:, 1216:1728]
        pos_i = pf[:, 1728:1730].bitcast(I32)
        posf = pf[:, 1730:1732]
        ang, turns, red = (pf[:, 1732 + 32 * n:1764 + 32 * n] for n in range(3))
        mrow = pf[:, 1828:1844]
        srow = pf[:, 1844:1860]
        den = pf[:, 1860:1876]
        mean = pf[:, 1876:1892]
        stats = pf[:, 2536:2560].rearrange("p (t c n) -> p t c n", t=NT, c=2)
        aggr = pf[:, 1904:1908].rearrange("p (t n) -> p t n", t=NT)
        lg, score, bi, comb, sel, wsel = (pf[:, 1908 + 32 * n:1940 + 32 * n] for n in range(6))
        gsum, grank = pf[:, 2100:2108], pf[:, 2108:2116]
        cmp_, eqs = pf[:, 2120:2248], pf[:, 2248:2376]
        ropet = pf[:, 2376:2536].rearrange("p (t h n) -> p t h n", t=NT, h=10)
        tlf = tl[:].rearrange("p a t n -> p (a t n)")
        memT = tlf[:, 0:2048].rearrange("p (k s) -> p k s", k=KB)
        kT = tlf[:, 2048:4096].rearrange("p (k s) -> p k s", k=KB)
        vM = RA[:, 0:2048].rearrange("p (t n) -> p t n", t=NT)
        qT = RA[:, 2048:4096].rearrange("p (k s) -> p k s", k=KB)
        mem = RA[:, 2048:4096].rearrange("p (t n) -> p t n", t=NT)
        tmpA = RA[:, 2048:3072].rearrange("p (t n) -> p t n", t=NT)
        mixg = RA[:, 4096:5120].rearrange("p (g t n) -> p g t n", g=SG, t=NT)
        pTw = RB[:, 0:3072].rearrange("p (h b n) -> p h b n", h=QH, b=3)
        qT2 = RB[:, 3072:4096].rearrange("p (q t n) -> p q t n", q=4, t=NT)
        kT2 = RB[:, 4096:4608].rearrange("p (g t n) -> p g t n", g=2, t=NT)
        kdup = RA[:, 4608:5120].rearrange("p (t g c n) -> p t g c n", t=NT, g=2, c=2)
        sgw = RB[:, 4608:5632].rearrange("p (g n) -> p g n", g=SG)
        sgT = gt[:].rearrange("p t n -> p (t n)").rearrange("p (g n) -> p g n", g=SG)
        px = RB[:, 0:2048].rearrange("p (a n) -> p a n", a=2 * XH)
        pxT = RB[:, 2048:4096].rearrange("p (h m s) -> p h m s", h=XH, m=NT)
        mapT = xn[:].rearrange("p t n -> p (t n)").rearrange("p (k s) -> p k s", k=KB)

        x_in = sem("x_in")
        tab_in = sem("tab_in")
        gain_in = [sem(f"gain_in{n}") for n in range(2)]
        norm_done = sem("norm_done")
        rs_asked = sem("rs_asked")
        rs_given = sem("rs_given")
        xn_ready = sem("xn_ready")
        xT_psum = sem("xT_psum")
        xT_act = sem("xT_act")
        xT_dve = sem("xT_dve")
        rw_split = sem("rw_split")
        mem_split = sem("mem_split")
        raw_in = [[sem(f"{m}_in{n}") for n in range(2)] for m in ("gate", "up", "down")]
        hi_done = [sem(f"{m}_hi") for m in ("gate", "up", "down")]
        lo_done = [sem(f"{m}_lo") for m in ("gate", "up", "down")]
        used = [sem(f"{m}_used") for m in ("gate", "up", "down")]
        tile_done = sem("tile_done")
        silu_ready = sem("silu_ready")
        h_ready = sem("h_ready")
        hT_ready = sem("hT_ready")
        chunk_in = [sem(f"chunk_in{n}") for n in range(4)]
        chunk_hi = sem("chunk_hi")
        chunk_lo = sem("chunk_lo")
        chunk_used = sem("chunk_used")
        group_done = sem("group_done")
        group_out = sem("group_out")
        vec = sem("vec")
        setup = sem("setup")
        param_in = sem("param_in")
        ln_in = sem("ln_in")
        zero_row = sem("zero_row")
        shift_in = sem("shift_in")
        qk_rot = sem("qk_rot")
        qkT_psum = sem("qkT_psum")
        qkT_ready = sem("qkT_ready")
        ret_s = sem("ret_s")
        ret_p = sem("ret_p")
        ret_o = sem("ret_o")
        ret_oc = sem("ret_oc")
        ret_g = sem("ret_g")
        shifted = sem("shifted")
        lora_act = sem("lora_act")
        lT_psum = sem("lT_psum")
        lT_ready = sem("lT_ready")
        lora_out = sem("lora_out")
        z_ready = sem("z_ready")
        sig_ready = sem("sig_ready")
        g_ready = sem("g_ready")
        cum_psum = sem("cum_psum")
        exp_ready = sem("exp_ready")
        tilde = sem("tilde")
        tr_psum = sem("tr_psum")
        tr_act = sem("tr_act")
        tr_dve = sem("tr_dve")
        L_psum = sem("L_psum")
        L_ready = sem("L_ready")
        av_psum = sem("av_psum")
        av_ready = sem("av_ready")
        aoff_ready = sem("aoff_ready")
        q_psum = sem("q_psum")
        q_ready = sem("q_ready")
        t_psum = sem("t_psum")
        t_ready = sem("t_ready")
        gT_psum = sem("gT_psum")
        gT_ready = sem("gT_ready")
        u_psum = sem("u_psum")
        u_ready = sem("u_ready")
        z_psum = sem("z_psum")
        z_state = sem("z_state")
        y_psum = sem("y_psum")
        y_ready = sem("y_ready")
        out_done = sem("out_done")
        paces = {nc.sync.engine: sem("pace_sp"), nc.tensor.engine: sem("pace_pe")}

        par2_in = sem("par2_in")
        pool_in = sem("pool_in")
        ang_ready = sem("ang_ready")
        sin_ready = sem("sin_ready")
        rope_ready = sem("rope_ready")
        gelu_ready = sem("gelu_ready")
        swT_psum = sem("swT_psum")
        swT_ready = sem("swT_ready")
        sc_psum = sem("sc_psum")
        sc_read = sem("sc_read")
        ex_asked = sem("ex_asked")
        ex_ready = sem("ex_ready")
        p_ready = sem("p_ready")
        pT_psum = sem("pT_psum")
        pT_ready = sem("pT_ready")
        pv_psum = sem("pv_psum")
        pv_ready = sem("pv_ready")
        sgT_psum = sem("sgT_psum")
        sgT_ready = sem("sgT_ready")
        vg_ready = sem("vg_ready")
        sgu_psum = sem("sgu_psum")
        gate_read = sem("gate_read")
        xs_psum = sem("xs_psum")
        xe_asked = sem("xe_asked")
        xe_ready = sem("xe_ready")
        xp_ready = sem("xp_ready")
        xpT_psum = sem("xpT_psum")
        xpT_ready = sem("xpT_ready")
        rt_psum = sem("rt_psum")
        re_asked = sem("re_asked")
        re_ready = sem("re_ready")
        acc_free = sem("acc_free")

        def chunk_raw(q, k, width):
            return raw[:, (q % 4) // 2, q % 2, 0:k * width].rearrange("p (k n) -> p k n", k=k)

        def hold(eng, signal, value):
            eng.wait_ge(signal, value)
            eng.sem_inc(paces[eng.engine], 1)

        def chain(eng, signal, start):
            def step(ins):
                step.n += 1
                ins.then_inc(signal, 1)
                eng.wait_ge(signal, start + step.n)
            step.n = 0
            return step

        block = ctx.enter_context(nc.Block())

        @block.sync
        def _(sp):
            sp.dma_start(x[:], A["x"][0].rearrange("(t p) d -> p t d", p=P)).then_inc(x_in, 16)
            sp.dma_start(tab[:], A["tables"][:, 0:T_RES]).then_inc(tab_in, 16)

            def chunk_load(q, n4, src, free=chunk_lo):
                hold(sp, free, 4 * n4 + q % 4 + 1)
                sp.dma_start(chunk_raw(q, src.shape[1], src.shape[2]), src).then_inc(chunk_in[q % 4], 16)

            def step_load(m, turn, j, src):
                hold(sp, lo_done[m], 2 * turn + j + 1)
                dst = raw[:, m, j]
                if m < 2:
                    dst = dst.rearrange("p (k f) -> p k f", k=KB)
                sp.dma_start(dst, src).then_inc(raw_in[m][j], 16)

            def ffn_load(wg, wu, wd, l, t0):
                with sp.Fori(0, TURNS_FFN) as g:
                    for j in range(2):
                        cols = ds((2 * g + j) * P, P)
                        step_load(0, t0 + g, j, wg[l].rearrange("(k p) f -> p k f", p=P)[:, :, cols])
                        step_load(1, t0 + g, j, wu[l].rearrange("(k p) f -> p k f", p=P)[:, :, cols])
                        step_load(2, t0 + g, j, wd[l, cols, :])

            def steps_split(steps):
                for m in range(2):
                    hold(sp, lo_done[m], steps + CR)

            def chunks_multiplied(chunks):
                hold(sp, chunk_used, chunks + 4)

            with sp.Fori(0, DEPTH) as l:
                hold(sp, norm_done, 3 * l + 1)
                sp.dma_start(gain[:, 0], A["ffn1_norm"][l].partition_broadcast(P)).then_inc(gain_in[0], 16)
                sp.dma_start(gain[:, 1], A["mix_norm"][l].partition_broadcast(P)).then_inc(gain_in[1], 16)
                w_in = A["w_in"][l].rearrange("(k p) n -> p k n", p=P)
                ffn_load(A["ffn1_w_gate"], A["ffn1_w_up"], A["ffn1_w_down"], l, 2 * TURNS_FFN * l)
                steps_split(2 * STEPS_FFN * l + STEPS_FFN)
                for c in range(4):
                    chunk_load(c, 10 * l, w_in[:, 2 * c:2 * c + 2, 0:GW])
                hold(sp, norm_done, 3 * l + 2)
                sp.dma_start(gain[:, 0], A["ffn2_norm"][l].partition_broadcast(P)).then_inc(gain_in[0], 16)
                sp.dma_start(mu, A["shift_mu"][l].partition_broadcast(P)).then_inc(param_in, 16)
                for n, name in enumerate(("w0", "a0", "k_k", "k_a")):
                    sp.dma_start(par[:, n], A[name][l].partition_broadcast(P)).then_inc(param_in, 16)
                sp.dma_start(par[:, 4], A["r_k"][l].rearrange("h n -> (h n)").partition_broadcast(P)).then_inc(param_in, 16)
                sp.dma_start(WL[0:64], A["w_lora_up"][l]).then_inc(param_in, 16)
                sp.dma_start(WL[64:128], A["a_lora_up"][l]).then_inc(param_in, 16)
                sp.dma_start(GL, A["g_lora_up"][l]).then_inc(param_in, 16)
                sp.dma_start(dist, A["tables"][:, T_DIST:T2].rearrange("p (h n) -> p h n", h=RETH)).then_inc(param_in, 16)
                with sp.Fori(1, 8) as g:
                    for c in range(4):
                        chunk_load(c, 10 * l + g, w_in[:, 2 * c:2 * c + 2, ds(g * GW, GW)])
                hold(sp, group_out, 10 * l + 8 + CR)
                sp.wait_ge(zero_row, l + 1)
                sp.dma_start(prev[1:P], proj[0:P - 1, :, 0:RWKV_IN]).then_inc(shift_in, 16)
                sp.dma_start(prev[0:1, 1], proj[P - 1:P, 0, 0:RWKV_IN]).then_inc(shift_in, 16)
                w_out = A["w_out"][l].rearrange("(k p) n -> p k n", p=P)
                for c in range(4):
                    chunk_load(c, 10 * l + 8, w_out[:, 2 * c:2 * c + 2, 0:512])
                hold(sp, tilde, l + 1)
                sp.dma_start(par[:, 0], A["ln_x_w"][l].partition_broadcast(P)).then_inc(ln_in, 16)
                sp.dma_start(par[:, 1], A["ln_x_b"][l].partition_broadcast(P)).then_inc(ln_in, 16)
                for c in range(4):
                    chunk_load(c, 10 * l + 9, w_out[:, 2 * c:2 * c + 2, 512:1024])
                chunks_multiplied(40 * l + 40)
                ffn_load(A["ffn2_w_gate"], A["ffn2_w_up"], A["ffn2_w_down"], l, 2 * TURNS_FFN * l + TURNS_FFN)
            hold(sp, norm_done, 3 * DEPTH + 1)
            sp.dma_start(gain[:, 0], A["final_norm"].partition_broadcast(P)).then_inc(gain_in[0], 16)

            def by_row(w):
                return w.rearrange("(k p) n -> p k n", p=P)

            q = 40 * DEPTH
            unsplit = 0
            last_split = True

            def load2(w, c0, width, split=True):
                nonlocal q, unsplit, last_split
                for c in range(4):
                    if last_split:
                        chunk_load(q, (q - unsplit) // 4, by_row(w)[:, 2 * c:2 * c + 2, c0:c0 + width])
                    else:
                        chunk_load(q, q // 4, by_row(w)[:, 2 * c:2 * c + 2, c0:c0 + width], chunk_used)
                    q += 1
                if not split:
                    unsplit += 4
                last_split = split

            for dst, src in (
                (pf[:, 0:T2_SMALL], A["tables"][:, T2:T2 + T2_SMALL]),
                (sinks, A["l0_sinks_2"].partition_broadcast(P)),
                (rbias, A["router_bias_2"].partition_broadcast(P)),
                (pscale, A["l1_pool_scale_2"].rearrange("(k p) -> p k", p=P)),
                (sgb, A["l0_sgu_b_2"].rearrange("g t -> t g")),
                (rw, by_row(A["router_w_2"])),
                (sgu_g, A["l0_sgu_ln_g_2"].partition_broadcast(P)),
                (sgu_bb, A["l0_sgu_ln_b_2"].partition_broadcast(P)),
                (pos_i, A["positions_2"][0].rearrange("(t p) -> p t", p=P)),
                (sgw, A["l0_sgu_w_2"].rearrange("g t s -> t g s")),
                (mem, A["mem_2"][0].rearrange("(t p) d -> p t d", p=P)),
            ):
                sp.dma_start(dst, src, allow_slow_non_contiguous=True).then_inc(par2_in, 16)
            for l in range(DEPTH):
                w = {n: A[f"l{l}_{n}_2"] for n in ("w_in", "w_out", "xq", "xkv", "xo", "e_gate", "e_up", "e_down")}
                steps_split(4 * STEPS_FFN + 2 * NE * TURNS_E * l)
                if l == 0:
                    for j in range(4):
                        load2(w["w_in"], j * W0, W0)
                for j in range(4):
                    load2(w["xkv"], j * 512, 512, split=l == 1)
                if l == 1:
                    for j in range(2):
                        load2(w["w_in"], j * 512, 512)
                    sp.dma_start(pool_t.rearrange("p g t n -> p (g t n)"), A["tables"][:, T_POOL:T_ALL]).then_inc(pool_in, 16)
                    for g in range(4):
                        chunk_load(q, (q - unsplit) // 4, A["l1_pool_w_2"][g].rearrange("(c p) d -> p c d", p=P))
                        q += 1
                for name in ("w_out", "xq", "xo"):
                    for j in range(2):
                        load2(w[name], j * 512, 512)
                chunks_multiplied(q)
                t0 = 4 * TURNS_FFN + NE * TURNS_E * l
                with sp.Fori(0, NE) as e:
                    for tt in range(TURNS_E):
                        for j in range(2):
                            turn = t0 + TURNS_E * e + tt
                            cols = slice((2 * tt + j) * P, (2 * tt + j + 1) * P)
                            step_load(0, turn, j, w["e_gate"][e].rearrange("(k p) f -> p k f", p=P)[:, :, cols])
                            step_load(1, turn, j, w["e_up"][e].rearrange("(k p) f -> p k f", p=P)[:, :, cols])
                            step_load(2, turn, j, w["e_down"][e, cols, :])
            sp.wait_ge(norm_done, 3 * DEPTH + 8)
            sp.dma_start(out[0].rearrange("(t p) d -> p t d", p=P), x[:]).then_inc(out_done, 16)
            sp.wait_ge(out_done, 16)

        @block.gpsimd
        def _(pool):
            pool.wait_ge(setup, 3)

            def rsqrt(n):
                pool.wait_ge(rs_asked, n + 1)
                nc.gpsimd.tensor_tensor(rs_out[:], rs_in[:], neg_half[:], ALU.pow).then_inc(rs_given, 1)

            with pool.Fori(0, DEPTH) as l:
                for n in range(4):
                    rsqrt(RSQ * l + n)
                for t in range(NT):
                    for lev in range(6):
                        for hf in range(2):
                            hs = slice(4 * hf, 4 * hf + 4)
                            if lev == 0:
                                pool.wait_ge(L_ready, 16 * l + 8 * t + 4 * hf + 4)
                                if t:
                                    pool.wait_ge(q_psum, 24 * l + 12)
                            else:
                                pool.wait_ge(q_psum, 24 * l + 12 * t + 2 * lev - 2 + hf + 1)
                                if lev == 1:
                                    pool.wait_ge(t_ready, 24 * l + 12 * t + hf + 1)
                            mask = tab[:, T_LEV + lev * P:T_LEV + (lev + 1) * P]
                            nc.gpsimd.tensor_tensor(Aoff[:, hs], Lm[:, hs, 0:P], mask.unsqueeze(1).to_broadcast([P, 4, P]),
                                                    ALU.mult).then_inc(aoff_ready, 1)
                for n in range(4, RSQ):
                    rsqrt(RSQ * l + n)
            with pool.Fori(RSQ * DEPTH, RSQ * DEPTH + 8) as n:
                rsqrt(n)

        @block.scalar
        def _(act):
            def turn_rows(r, dst):
                for b in (0, 2):
                    act.wait_ge(xT_psum, 4 * r + b + 1)
                    nc.scalar.activation(dst[:, 2 * b:2 * b + 2, :], PS[:, 4 + b, :], ACT.Copy).then_inc(xT_act, 2)

            def turn_split(r):
                for b in range(4):
                    act.wait_ge(xT_psum, 4 * r + b + 1)
                    nc.scalar.activation(xTh[:, 2 * b:2 * b + 2, :].rearrange("p k s -> p (k s)"), PS[:, 4 + b, :], ACT.Copy).then_inc(xT_act, 1)

            def split(m, turn, j):
                act.wait_ge(raw_in[m][j], 16 * turn + 16)
                act.wait_ge(used[m], 2 * turn + j + 1)
                nc.scalar.activation(whi[:, m], raw[:, m, j], ACT.Copy).then_inc(hi_done[m], 1)

            def first_split(turn):
                for m in range(2):
                    split(m, turn, 0)

            def split_chunk(n4, c, width):
                act.wait_ge(chunk_in[c], 16 * n4 + 16)
                act.wait_ge(chunk_used, 4 * n4 + c + (3 if c % 2 else 1))
                nc.scalar.activation(whi[:, SPLIT_AT[c], 0:2 * width], raw[:, c // 2, c % 2, 0:2 * width], ACT.Copy).then_inc(chunk_hi, 1)

            def step(turn, j, more=True):
                if more:
                    for m in range(2):
                        split(m, turn + j, 1 - j)
                act.wait_ge(used[1], 2 * turn + j + 1 + 1)
                nc.scalar.activation(gs[:, j], PS[:, 4 + j, 0:S], ACT.Silu).then_inc(silu_ready, 1)
                split(2, turn, j)

            def ffn(t0):
                with act.Fori(0, TURNS_FFN - 1) as g:
                    for j in range(2):
                        step(t0 + g, j)
                step(t0 + TURNS_FFN - 1, 0)
                step(t0 + TURNS_FFN - 1, 1, False)

            def experts(t0):
                step(t0, 0)
                with act.Fori(0, NE - 1) as e:
                    t = t0 + TURNS_E * e
                    step(t, 1)
                    step(t + 1, 0)
                    step(t + 1, 1)
                    step(t + 2, 0)
                t = t0 + TURNS_E * (NE - 1)
                step(t, 1)
                step(t + 1, 0)
                step(t + 1, 1, False)

            act.wait_ge(setup, 3)
            with act.Fori(0, DEPTH) as l:
                first_split(2 * TURNS_FFN * l)
                turn_split(4 * l)
                ffn(2 * TURNS_FFN * l)
                for c in range(2):
                    split_chunk(10 * l, c, GW)
                turn_split(4 * l + 1)
                for c in range(2, 4):
                    split_chunk(10 * l, c, GW)

                def evac_in(g, j):
                    act.wait_ge(group_done, 10 * l + g + 1 + CR)
                    nc.scalar.activation(proj[:, :, ds(g * GW, GW)], PS[:, 2 * j:2 * j + 2, 0:GW], ACT.Copy).then_inc(group_out, 1)

                def in_step(g, j):
                    for c in range(4):
                        split_chunk(10 * l + g, c, GW)
                        if c == 1:
                            evac_in(g - 1, 1 - j)

                with act.Fori(0, 3) as g:
                    in_step(2 * g + 1, 1)
                    in_step(2 * g + 2, 0)
                in_step(7, 1)
                evac_in(7, 1)
                act.wait_ge(group_out, 10 * l + 8 + CR)
                nc.scalar.activation(proj[:, :, GCOL:PROJ], proj[:, :, GCOL:PROJ], ACT.Silu).then_inc(ret_g, 1)
                act.wait_ge(qkT_psum, l + 1)
                nc.scalar.activation(qkT.rearrange("p q t n -> p (q t n)"), PS[:, 4:6, :].rearrange("p b n -> p (b n)"),
                                     ACT.Copy).then_inc(qkT_ready, 1)
                act.wait_ge(ret_o, l + 1)
                nc.scalar.activation(xn[:, :, RW:2 * RW], PS[:, 0:2, :], ACT.Copy).then_inc(ret_oc, 1)
                act.wait_ge(shifted, l + 1)
                nc.scalar.activation(proj[:, :, 1536:1600], proj[:, :, 1536:1600], ACT.Tanh).then_inc(lora_act, 1)
                nc.scalar.activation(proj[:, :, 1664:1792], proj[:, :, 1664:1792], ACT.Sigmoid).then_inc(lora_act, 1)
                act.wait_ge(lT_psum, l + 1)
                nc.scalar.activation(lT.rearrange("p b s -> p (b s)"), PS[:, 4, :], ACT.Copy).then_inc(lT_ready, 1)
                act.wait_ge(lora_out, l + 1)
                nc.scalar.activation(gt[:], PS[:, 6:8, :], ACT.Copy).then_inc(g_ready, 1)
                act.wait_ge(z_ready, 2 * l + 1)
                nc.scalar.activation(sw, sw, ACT.Sigmoid).then_inc(sig_ready, 1)
                act.wait_ge(z_ready, 2 * l + 2)
                nc.scalar.activation(av, av, ACT.Sigmoid).then_inc(sig_ready, 1)
                act.wait_ge(cum_psum, l + 1)
                nc.scalar.activation(W1, PS[:, 0:2, :], ACT.Exp)
                nc.scalar.activation(W2, PS[:, 0:2, :], ACT.Exp, scale=-1.0)
                nc.scalar.activation(W3, PS[:, 2:4, :], ACT.Exp)
                nc.scalar.activation(decC[:], PS[:, 5, 0:16], ACT.Exp).then_inc(exp_ready, 1)
                for t in range(NT):
                    act.wait_ge(tr_psum, 2 * l + t + 1)
                    nc.scalar.activation(ART.rearrange("p q n -> p (q n)"), PS[:, 0:2, :].rearrange("p b n -> p (b n)"),
                                         ACT.Copy).then_inc(tr_act, 1)
                    act.wait_ge(av_psum, 2 * l + t + 1)
                    nc.scalar.activation(AV, PS[:, 0, :], ACT.Copy).then_inc(av_ready, 1)
                    for lev in range(1, 6):
                        for hf in range(2):
                            act.wait_ge(q_psum, 24 * l + 12 * t + 2 * lev + hf + 1)
                            if lev > 1:
                                act.wait_ge(t_psum, 20 * l + 10 * t + 2 * (lev - 2) + hf + 1)
                            nc.scalar.activation(QM[:, 4 * hf:4 * hf + 4, :].rearrange("p h n -> p (h n)"), PS[:, 2 + hf, :],
                                                 ACT.Copy).then_inc(q_ready, 1)
                    act.wait_ge(gT_psum, 2 * l + t + 1)
                    nc.scalar.activation(tl[:, 3, t], PS[:, 1, :], ACT.Copy).then_inc(gT_ready, 1)
                    for hf in range(2):
                        rows = slice(64 * hf, 64 * hf + 64)
                        act.wait_ge(u_psum, 4 * l + 2 * t + hf + 1)
                        nc.scalar.activation(U[rows], PS[rows, 2, :], ACT.Copy).then_inc(u_ready, 1)
                    act.wait_ge(y_psum, 2 * l + t + 1)
                    nc.scalar.activation(xn[:, t, 0:RW], PS[:, 1, :], ACT.Copy).then_inc(y_ready, 1)
                for c in range(2):
                    split_chunk(10 * l + 8, c, 512)
                turn_split(4 * l + 2)
                for c in range(2, 8):
                    split_chunk(10 * l + 8 + c // 4, c % 4, 512)
                first_split(2 * TURNS_FFN * l + TURNS_FFN)
                turn_split(4 * l + 3)
                ffn(2 * TURNS_FFN * l + TURNS_FFN)

            def gains(k, g, b):
                act.wait_ge(norm_done, 3 * DEPTH + k + 2)
                act.dma_start(gain[:, 0], g.partition_broadcast(P)).then_inc(gain_in[0], 16)
                act.dma_start(gain[:, 1], b.partition_broadcast(P)).then_inc(gain_in[1], 16)

            def evac(n, dst):
                act.wait_ge(group_done, n + 1 + CR)
                b = 2 * (n % 2)
                nc.scalar.activation(dst, PS[:, b:b + 2, 0:dst.shape[2]] if len(dst.shape) == 3 else PS[:, b:b + 2, :], ACT.Copy)\
                    .then_inc(group_out, 1)

            def evac_turned(n, dst, j):
                act.wait_ge(group_done, n + 1 + CR)
                b = 2 * (n % 2)
                nc.scalar.activation(dst[:, 4 * j:4 * j + 4, :].rearrange("p k s -> p (k s)"), PS[:, b:b + 2, :].rearrange("p b n -> p (b n)"),
                                     ACT.Copy).then_inc(group_out, 1)

            q = 40 * DEPTH

            def split_chunks(count, width=512):
                nonlocal q
                for _ in range(count):
                    split_chunk(q // 4, q % 4, width)
                    q += 1

            split_chunks(2, W0)
            turn_split(8)
            turn_rows(9, memT)
            act.wait_ge(par2_in, 176)
            nc.scalar.activation(rws[:, :, 0], rw, ACT.Copy).then_inc(rw_split, 1)
            for l in range(DEPTH):
                gains(3 * l, A[f"l{l}_ln1_g_2"], A[f"l{l}_ln1_b_2"])
                n = 20 + 14 * l
                r = 10 if l == 0 else 15
                if l == 0:
                    for j in range(4):
                        split_chunks(4 if j < 3 else 2, W0)
                        evac(n + j, hid[:, :, j * W0:(j + 1) * W0])
                    n += 4
                    act.wait_ge(ang_ready, 1)
                    nc.scalar.activation(red, red, ACT.Sin).then_inc(sin_ready, 1)
                    act.wait_ge(group_out, n + CR)
                    nc.scalar.activation(hid[:, :, 768:1792], hid[:, :, 768:1792], ACT.Gelu_apprx_tanh).then_inc(gelu_ready, 1)
                else:
                    n += 4
                    for j in range(2):
                        split_chunks(4 if j == 0 else 2)
                        evac(n + j, hid1[:, :, j * 512:(j + 1) * 512])
                    n += 2
                if l == 0:
                    q += 16
                    for j in range(2):
                        evac_turned(n + j, kT, j)
                    act.wait_ge(swT_psum, 1)
                    nc.scalar.activation(qT2.rearrange("p q t n -> p (q t n)"), PS[:, 4:6, :].rearrange("p b n -> p (b n)"), ACT.Copy)
                    nc.scalar.activation(kT2.rearrange("p g t n -> p (g t n)"), PS[:, 6, :], ACT.Copy).then_inc(swT_ready, 1)
                    for j in range(2):
                        evac(n + 2 + j, vM[:, :, j * 512:(j + 1) * 512])
                    n += 4
                    act.wait_ge(ex_asked, 1)
                    nc.scalar.activation(Sc, Sc, ACT.Exp)
                    nc.scalar.activation(srow, srow, ACT.Exp).then_inc(ex_ready, 1)
                    for half in range(2):
                        act.wait_ge(pT_psum, half + 1)
                        nc.scalar.activation(pTw[:, 4 * half:4 * half + 4].rearrange("p h b n -> p (h b n)"),
                                             PS[:, 3 * half:3 * half + 3, :].rearrange("p b n -> p (b n)"), ACT.Copy).then_inc(pT_ready, 1)
                    act.wait_ge(pv_psum, 1)
                    nc.scalar.activation(xn[:, :, 0:512], PS[:, 6:8, :], ACT.Copy).then_inc(pv_ready, 1)
                    split_chunks(2)
                    turn_split(r)
                    split_chunks(6)
                else:
                    split_chunks(2, S)
                    turn_split(r)
                    split_chunks(2, S)
                    split_chunks(8)
                    n += 2
                r += 1
                n += 2
                split_chunks(2)
                turn_split(r)
                gains(3 * l + 1, A[f"l{l}_ln2_g_2"], A[f"l{l}_ln2_b_2"])
                for j in range(2):
                    split_chunks(4 if j == 0 else 2)
                    evac_turned(n + j, qT, j)
                act.wait_ge(xe_asked, l + 1)
                nc.scalar.activation(px, px, ACT.Exp, scale=1.0 / 16).then_inc(xe_ready, 1)
                act.wait_ge(xpT_psum, l + 1)
                nc.scalar.activation(pxT.rearrange("p h m s -> p (h m s)"), PS[:, 0:4, :].rearrange("p b n -> p (b n)"), ACT.Copy)\
                    .then_inc(xpT_ready, 1)
                split_chunks(2)
                turn_split(r + 1)
                split_chunks(6)
                t0 = 4 * TURNS_FFN + NE * TURNS_E * l
                first_split(t0)
                turn_split(r + 2)
                gains(3 * l + 2, A[f"l{l}_ln3_g_2"], A[f"l{l}_ln3_b_2"])
                act.wait_ge(re_asked, l + 1)
                nc.scalar.activation(lg, lg, ACT.Exp).then_inc(re_ready, 1)
                experts(t0)
                if l == 0:
                    split_chunks(2)
                    nc.scalar.activation(xTh[:].rearrange("p k s -> p (k s)"), memT.rearrange("p k s -> p (k s)"), ACT.Copy).then_inc(mem_split, 1)
                    act.wait_ge(used[2], 2 * (t0 + NE * TURNS_E) + 1)
                    for j in range(2):
                        split_chunks(4)
                        evac_turned(34 + j, kT, j)
                    for j in range(2):
                        split_chunks(4)
                        evac(36 + j, vM[:, :, j * 512:(j + 1) * 512])
                    turn_split(14)

        @block.vector
        def _(dve):
            nc.vector.memset(zero[:], 0.0).then_inc(setup, 1)
            nc.vector.memset(rs_in[:], 1.0).then_inc(setup, 1)
            nc.vector.memset(neg_half[:], -0.5).then_inc(setup, 1)
            dve.wait_ge(setup, 3)
            dve.sem_inc(hT_ready, CR)
            dve.sem_inc(norm_done, 1)
            for m in range(3):
                dve.sem_inc(lo_done[m], CR)
            dve.sem_inc(chunk_lo, 4)

            def rsqrt(n):
                dve.wait_ge(rs_given, n + 1)

            def rms(own, n, g, g_value, ask, dst=xn):
                for t in range(NT):
                    own(nc.vector.tensor_tensor_reduce(xn[:, t], x[:, t], x[:, t], 1.0, 0.0, ALU.mult, ALU.add, rs_in[:, t:t + 1]))
                nc.vector.tensor_scalar(rs_in[:, 0:2], rs_in[:, 0:2], 1.0 / D, 1e-6, ALU.mult, ALU.add).then_inc(rs_asked, 1)
                rsqrt(ask)
                dve.wait_ge(gain_in[g], g_value)
                for t in range(NT):
                    last = nc.vector.scalar_tensor_tensor(out=dst[:, t], in0=x[:, t], scalar=rs_out[:, t:t + 1], in1=gain[:, g],
                                                          op0=ALU.mult, op1=ALU.mult)
                last.then_inc(norm_done, 1)
                dve.wait_ge(norm_done, n + 2)

            def turn_rows(r, dst):
                dve.sem_inc(xn_ready, 1)
                for b in (1, 3):
                    dve.wait_ge(xT_psum, 4 * r + b + 1)
                    nc.vector.tensor_copy(dst[:, 2 * b:2 * b + 2, :].rearrange("p k s -> p (k s)"), PS[:, 4 + b, :]).then_inc(xT_dve, 2)

            def turn_split(r):
                for b in range(4):
                    dve.wait_ge(xT_act, 4 * r + b + 1)
                    f = slice(2 * b, 2 * b + 2)
                    nc.vector.tensor_tensor(xTl[:, f, :].rearrange("p k s -> p (k s)"), PS[:, 4 + b, :],
                                            xTh[:, f, :].rearrange("p k s -> p (k s)").bitcast(F32), ALU.subtract).then_inc(xT_dve, 1)

            def turn_for_steps(r, turn):
                dve.sem_inc(xn_ready, 1)
                for m in range(2):
                    split(m, turn, 0)
                turn_split(r)

            def split_chunk(ns, c, width):
                dve.wait_ge(chunk_hi, 4 * ns + c + 1)
                nc.vector.tensor_tensor(wlo[:, SPLIT_AT[c], 0:2 * width], raw[:, c // 2, c % 2, 0:2 * width],
                                        whi[:, SPLIT_AT[c], 0:2 * width].bitcast(F32), ALU.subtract).then_inc(chunk_lo, 1)

            def split(m, turn, j):
                dve.wait_ge(hi_done[m], 2 * turn + j + 1)
                nc.vector.tensor_tensor(wlo[:, m], raw[:, m, j], whi[:, m].bitcast(F32), ALU.subtract).then_inc(lo_done[m], 1)

            def step(turn, j, more=True, between=None):
                if more:
                    for m in range(2):
                        split(m, turn + j, 1 - j)
                if between:
                    between()
                dve.wait_ge(silu_ready, 2 * turn + j + 1)
                nc.vector.tensor_tensor(h32[:, j], gs[:, j], PS[:, 4 + j, S:2 * S], ALU.mult)
                nc.vector.tensor_tensor(hTh[:, j], gs[:, j], PS[:, 4 + j, S:2 * S], ALU.mult).then_inc(h_ready, 1)
                dve.wait_ge(h_ready, 2 * turn + j + 1)
                nc.vector.tensor_tensor(hTl[:, j], h32[:, j], hTh[:, j].bitcast(F32), ALU.subtract).then_inc(hT_ready, 1)
                split(2, turn, j)

            def ffn(own, t0, n):
                with dve.Fori(0, TURNS_FFN - 1) as g:
                    for j in range(2):
                        step(t0 + g, j)
                step(t0 + TURNS_FFN - 1, 0)
                step(t0 + TURNS_FFN - 1, 1, False)
                dve.wait_ge(tile_done, n + 1)
                for t in range(NT):
                    if t:
                        dve.wait_ge(used[2], 2 * (t0 + TURNS_FFN) + 1)
                    own(nc.vector.scalar_tensor_tensor(out=x[:, t], in0=acc[:, t * D:(t + 1) * D], scalar=0.5, in1=x[:, t], op0=ALU.mult, op1=ALU.add))

            def heads(ap):
                return ap.rearrange("p t (h n) -> p t h n", h=RH)

            def per_head(ap):
                return ap.rearrange("p (t h) -> p t h", t=NT).unsqueeze(3).to_broadcast([P, NT, RH, RN])

            def row(ap):
                return ap.unsqueeze(1).to_broadcast([P, NT, ap.shape[1]])

            dve.wait_ge(x_in, 16)
            TTop = nc.vector.tensor_tensor
            with dve.Fori(0, DEPTH) as l:
                own = chain(dve, vec, l * VEC_LAYER)
                rms(own, 3 * l, 0, 32 * l + 16, RSQ * l)
                turn_for_steps(4 * l, 2 * TURNS_FFN * l)
                ffn(own, 2 * TURNS_FFN * l, 2 * l)
                rms(own, 3 * l + 1, 1, 16 * l + 16, RSQ * l + 1)
                dve.sem_inc(xn_ready, 1)
                for c in range(2):
                    split_chunk(10 * l, c, GW)
                turn_split(4 * l + 1)
                for c in range(2, 4):
                    split_chunk(10 * l, c, GW)
                with dve.Fori(1, 8) as g:
                    for c in range(4):
                        split_chunk(10 * l + g, c, GW)
                dve.wait_ge(tab_in, 16)
                dve.wait_ge(param_in, 160 * l + 160)
                dve.wait_ge(group_out, 10 * l + 8 + CR)
                nc.vector.memset(prev[0:1, 0], 0.0).then_inc(zero_row, 1)
                pq = proj[:, :, QCOL:VCOL].rearrange("p t (h n) -> p t h n", h=8)
                c = tab[:, T_ROT:T_ROT + 64].rearrange("p (t n) -> p t n", t=NT).unsqueeze(2).to_broadcast([P, NT, 8, 32])
                s = tab[:, T_ROT + 64:T_ROT + 128].rearrange("p (t n) -> p t n", t=NT).unsqueeze(2).to_broadcast([P, NT, 8, 32])
                ta = xn[:, :, 512:768].rearrange("p t (h n) -> p t h n", h=8)
                x1, x2 = pq[:, :, :, 0:32], pq[:, :, :, 32:64]
                dve.wait_ge(xT_psum, 16 * l + 8)
                nc.vector.tensor_tensor(qk[:, :, :, 0:32], x1, c, ALU.mult)
                own(TTop(ta, x2, s, ALU.mult))
                own(TTop(qk[:, :, :, 0:32], qk[:, :, :, 0:32], ta, ALU.subtract))
                nc.vector.tensor_tensor(qk[:, :, :, 32:64], x1, s, ALU.mult)
                own(TTop(ta, x2, c, ALU.mult))
                TTop(qk[:, :, :, 32:64], qk[:, :, :, 32:64], ta, ALU.add).then_inc(qk_rot, 1)
                for h in range(RETH):
                    dve.wait_ge(ret_s, 4 * l + h + 1)
                    if h >= 2:
                        dve.wait_ge(ret_s, 4 * l + 4)
                    TTop(PT[:, h % 2], PS[:, 6 + h % 2, 0:T_DW], dist[:, h], ALU.mult).then_inc(ret_p, 1)
                dve.wait_ge(shift_in, 32 * l + 32)

                def shift(cols, last):
                    pr, pv = proj[:, :, cols], prev[:, :, cols]
                    own(TTop(pv, pv, pr, ALU.subtract))
                    own(TTop(pv, pv, row(mu[:, cols]), ALU.mult))
                    last(TTop(pr, pr, pv, ALU.add))

                shift(slice(3 * RW, RWKV_IN), lambda ins: ins.then_inc(shifted, 1))
                shift(slice(0, 3 * RW), own)
                dve.wait_ge(lora_out, l + 1)
                TTop(sw, PS[:, 0:2, :], row(par[:, 0]), ALU.add).then_inc(z_ready, 1)
                TTop(av, PS[:, 2:4, :], row(par[:, 1]), ALU.add).then_inc(z_ready, 1)
                r_, k_, v_ = (proj[:, :, n * RW:(n + 1) * RW] for n in range(3))
                own(TTop(kk, k_, row(par[:, 2]), ALU.mult))
                own(TTop(tmp, kk, kk, ALU.mult))
                own(nc.vector.tensor_reduce(rs_in[:], tmp.rearrange("p t (h n) -> p (t h) n", h=RH), AX.X, ALU.add))
                nc.vector.tensor_scalar(rs_in[:], rs_in[:], 1e-24, None, ALU.max).then_inc(rs_asked, 1)
                dve.wait_ge(ret_oc, l + 1)
                o = xn[:, :, RW:2 * RW]
                oh = o.rearrange("p t (h n) -> p t h n", h=RETH)
                sq = qk.rearrange("p t h n -> p t (h n)")
                rsqrt(RSQ * l + 2)
                own(TTop(heads(kk), heads(kk), per_head(rs_out[:]), ALU.mult))
                own(TTop(sq, o, o, ALU.mult))
                own(nc.vector.tensor_reduce(rs_in[:, 0:8], sq.rearrange("p t (h n) -> p (t h) n", h=RETH), AX.X, ALU.add))
                nc.vector.tensor_scalar(rs_in[:, 0:8], rs_in[:, 0:8], 1.0 / 128, 1e-6, ALU.mult, ALU.add).then_inc(rs_asked, 1)
                dve.wait_ge(sig_ready, 2 * l + 2)
                dve.wait_ge(exp_ready, l + 1)
                nc.vector.scalar_tensor_tensor(out=tl[:, 0], in0=kk, scalar=-1.0, in1=W3, op0=ALU.mult, op1=ALU.mult)
                own(TTop(tmp, kk, av, ALU.mult))
                TTop(tl[:, 1], tmp, W2, ALU.mult)
                own(nc.vector.scalar_tensor_tensor(out=av, in0=av, scalar=-1.0, in1=row(par[:, 3]), op0=ALU.add, op1=ALU.mult))
                own(nc.vector.scalar_tensor_tensor(out=av, in0=av, scalar=1.0, in1=k_, op0=ALU.add, op1=ALU.mult))
                TTop(tl[:, 2], av, W2, ALU.mult)
                TTop(tl[:, 3], r_, W1, ALU.mult).then_inc(tilde, 1)
                dve.wait_ge(tilde, l + 1)
                own(TTop(tmp, r_, av, ALU.mult))
                own(TTop(tmp, tmp, row(par[:, 4]), ALU.mult))
                own(nc.vector.tensor_reduce(bonus[:], tmp.rearrange("p t (h n) -> p (t h) n", h=RH), AX.X, ALU.add))
                lmask = tab[:, T_LMASK:T_LMASK + 512]
                spare = h32[:].rearrange("p j s -> p (j s)")

                def head_norm(t):
                    dve.wait_ge(y_ready, 2 * l + t + 1)
                    dve.wait_ge(ln_in, 32 * l + 32)
                    y, t1, v = xn[:, t, 0:RW], spare, proj[:, t, 2 * RW:3 * RW]
                    hs = slice(t * RH, (t + 1) * RH)
                    ri, ro = rs_in[:, hs], rs_out[:, hs]
                    by_head = lambda ap: ap.rearrange("p (h n) -> p h n", h=RH)
                    each = lambda ap: ap.unsqueeze(2).to_broadcast([P, RH, RN])
                    own(nc.vector.tensor_reduce(ri, by_head(y), AX.X, ALU.add))
                    own(nc.vector.tensor_scalar(ri, ri, -1.0 / RN, None, ALU.mult))
                    own(TTop(by_head(y), by_head(y), each(ri), ALU.add))
                    own(TTop(t1, y, y, ALU.mult))
                    own(nc.vector.tensor_reduce(ri, by_head(t1), AX.X, ALU.add))
                    nc.vector.tensor_scalar(ri, ri, 1.0 / RN, 64e-5, ALU.mult, ALU.add).then_inc(rs_asked, 1)
                    own(TTop(by_head(t1), by_head(v), each(bonus[:, hs]), ALU.mult))
                    rsqrt(RSQ * l + 4 + t)
                    own(TTop(by_head(y), by_head(y), each(ro), ALU.mult))
                    own(TTop(y, y, par[:, 0], ALU.mult))
                    own(TTop(y, y, par[:, 1], ALU.add))
                    own(TTop(y, y, t1, ALU.add))
                    dve.wait_ge(g_ready, l + 1)
                    own(TTop(y, y, gt[:, t], ALU.mult))

                for t in range(NT):
                    dve.wait_ge(tr_psum, 2 * l + t + 1)
                    if t:
                        dve.wait_ge(y_psum, 2 * l + t)
                    nc.vector.tensor_copy(BT.rearrange("p q n -> p (q n)"), PS[:, 2, :])
                    nc.vector.tensor_copy(KT.rearrange("p q n -> p (q n)"), PS[:, 3, :]).then_inc(tr_dve, 1)
                    for h in range(RH):
                        dve.wait_ge(L_psum, 16 * l + 8 * t + h + 1)
                        TTop(Lm[:, h], PS[:, 4 + h % 4, :], lmask, ALU.mult).then_inc(L_ready, 1)
                    for lev in range(6):
                        for hf in range(2):
                            hs = slice(4 * hf, 4 * hf + 4)
                            fl = lambda ap: ap[:, hs].rearrange("p h n -> p (h n)")
                            base = 24 * l + 12 * t + 2 * lev + hf
                            if lev == 0:
                                idb = ident.unsqueeze(1).to_broadcast([P, 4, P])
                                dve.wait_ge(q_psum, base + 1)
                                dve.wait_ge(aoff_ready, base + 1)
                                TTop(TM[:, hs], PS[:, 2 + hf, :].rearrange("p (h n) -> p h n", h=4), idb, ALU.add)
                                TTop(TT[:, hs], Aoff[:, hs], idb, ALU.add).then_inc(t_ready, 1)
                                continue
                            dve.wait_ge(t_psum, 20 * l + 10 * t + 2 * (lev - 1) + hf + 1)
                            dve.wait_ge(t_ready, base - 1)
                            if lev < 5:
                                TTop(fl(TM), fl(TM), PS[:, 4 + hf, :], ALU.add)
                            TTop(fl(TT), fl(TT), PS[:, 6 + hf, :], ALU.add).then_inc(t_ready, 1)
                    if t == 0:
                        own(nc.vector.memset(Zs, 0.0))
                        rsqrt(RSQ * l + 3)
                        dve.wait_ge(ret_g, l + 1)
                        own(TTop(oh, oh, rs_out[:, 0:8].rearrange("p (t h) -> p t h", t=NT).unsqueeze(3).to_broadcast([P, NT, RETH, 128]), ALU.mult))
                        own(TTop(o, o, proj[:, :, GCOL:PROJ], ALU.mult))
                    for hf in range(2):
                        ch = 2 * t + hf
                        if ch == 3:
                            break
                        dve.wait_ge(z_psum, 3 * l + ch + 1)
                        for b in (0, 64):
                            rows, cols = slice(b, b + 64), slice(b, b + 64)
                            src = PS[rows, 3, :].rearrange("p (q n) -> p q n", q=4)[:, :, cols]
                            dec = decC[rows].rearrange("p (t q f) -> p t q f", t=NT, q=4)[:, t, :, hf].unsqueeze(2).to_broadcast([64, 4, 64])
                            if ch:
                                own(TTop(Ztmp[rows], src, Zs[rows, ch - 1, :, cols], ALU.add))
                                src = Ztmp[rows]
                            own(TTop(Zs[rows, ch, :, cols], src, dec, ALU.mult))
                        dve.sem_inc(z_state, 1)
                for t in range(NT):
                    head_norm(t)
                dve.sem_inc(xn_ready, 1)
                for c in range(2):
                    split_chunk(10 * l + 8, c, 512)
                turn_split(4 * l + 2)
                for j in range(2):
                    for c in range(4 * j + 2, 6 if j == 0 else 8):
                        split_chunk(10 * l + 8 + c // 4, c % 4, 512)
                    dve.wait_ge(group_done, 10 * l + 8 + j + 1 + CR)
                    xs = x[:, :, j * 512:(j + 1) * 512]
                    TTop(xs, xs, PS[:, 2 * j:2 * j + 2, :], ALU.add).then_inc(group_out, 1)
                dve.wait_ge(group_out, 10 * l + 10 + CR)
                rms(own, 3 * l + 2, 0, 32 * l + 32, RSQ * l + 6)
                turn_for_steps(4 * l + 3, 2 * TURNS_FFN * l + TURNS_FFN)
                ffn(own, 2 * TURNS_FFN * l + TURNS_FFN, 2 * l + 1)
                assert own.n == VEC_LAYER, own.n
            own = chain(dve, vec, DEPTH * VEC_LAYER)
            rms(own, 3 * DEPTH, 0, 32 * DEPTH + 16, RSQ * DEPTH, x)

            def layer_norm(k, ask, halves=False, chunks=False):
                for t in range(NT):
                    if halves:
                        for c in range(2):
                            last = nc.vector.bn_stats(stats[:, t, c], x[:, t, c * 512:(c + 1) * 512])
                        own(last)
                    own(nc.vector.bn_aggr(aggr[:, t], stats[:, t]))
                    split_chunks(chunks)
                nc.vector.tensor_scalar(rs_in[:, 0:2], aggr[:, :, 1], 1e-5, None, ALU.add).then_inc(rs_asked, 1)
                dve.wait_ge(gain_in[0], 16 * (2 * DEPTH + 2 + k))
                for t in range(NT):
                    own(nc.vector.scalar_tensor_tensor(out=x[:, t], in0=x[:, t], scalar=aggr[:, t, 0:1], in1=gain[:, 0], op0=ALU.subtract, op1=ALU.mult))
                    split_chunks(chunks)
                rsqrt(ask)
                dve.wait_ge(gain_in[1], 16 * (DEPTH + 1 + k))
                for t in range(NT):
                    last = nc.vector.scalar_tensor_tensor(out=x[:, t], in0=x[:, t], scalar=rs_out[:, t:t + 1], in1=gain[:, 1], op0=ALU.mult, op1=ALU.add)
                last.then_inc(norm_done, 1)
                dve.wait_ge(norm_done, 3 * DEPTH + k + 3)

            q = 40 * DEPTH

            def split_chunks(count, width=512):
                nonlocal q
                for _ in range(count):
                    split_chunk(q // 4, q % 4, width)
                    q += 1

            def turn_for_group(r, width=512):
                dve.sem_inc(xn_ready, 1)
                split_chunks(2, width)
                turn_split(r)

            def residual(n):
                for j in range(2):
                    split_chunks(4 if j == 0 else 2)
                    dve.wait_ge(group_done, n + j + 1 + CR)
                    xs = x[:, :, j * 512:(j + 1) * 512]
                    nc.vector.scalar_tensor_tensor(out=xs, in0=xs, scalar=ALPHA, in1=PS[:, 2 * j:2 * j + 2, :], op0=ALU.mult, op1=ALU.add)\
                        .then_inc(group_out, 1)
                    dve.wait_ge(group_out, n + j + 1 + CR)
                    for t in range(NT):
                        last = nc.vector.bn_stats(stats[:, t, j], xs[:, t])
                    own(last)

            def bc(ap, n):
                return ap.unsqueeze(len(ap.shape)).to_broadcast([*ap.shape, n])

            def pair(ap):
                return ap.rearrange("p (t n) -> p t n", t=NT)

            def window_attention():
                for j in range(4):
                    split_chunks(4 if j < 3 else 2, W0)
                dve.wait_ge(par2_in, 176)
                dve.wait_ge(rw_split, 1)
                nc.vector.tensor_tensor(rws[:, :, 1], rw, rws[:, :, 0].bitcast(F32), ALU.subtract).then_inc(rw_split, 1)
                own(nc.vector.tensor_copy(posf, pos_i))
                a3 = ang.rearrange("p (k t n) -> p k t n", k=2, t=NT)
                for k in range(2):
                    own(TTop(a3[:, k], bc(posf, 8), inv.unsqueeze(1).to_broadcast([P, NT, 8]), ALU.mult))
                    own(nc.vector.tensor_scalar(turns[:, 16 * k:16 * k + 16], ang[:, 16 * k:16 * k + 16], 1.0 / (2 * np.pi), 0.25 * k, ALU.mult, ALU.add))
                own(nc.vector.tensor_scalar(turns, turns, 12582912.0, None, ALU.add))
                own(nc.vector.tensor_scalar(turns, turns, -12582912.0, None, ALU.add))
                c1 = 6.28125
                c2 = float(np.array(int(np.float32(2 * np.pi - c1).view(np.int32)) & -4096, np.int32).view(np.float32))
                c3 = float(2 * np.pi - c1 - c2)
                src = ang
                for c in (c1, c2, c3):
                    own(nc.vector.scalar_tensor_tensor(out=red, in0=turns, scalar=-c, in1=src, op0=ALU.mult, op1=ALU.add))
                    src = red
                own(nc.vector.tensor_scalar(red[:, 16:32], red[:, 16:32], float(np.pi / 2), None, ALU.add))
                nc.vector.tensor_scalar(red, red, 3.1415925, -3.1415925, ALU.min, ALU.max).then_inc(ang_ready, 1)
                dve.wait_ge(group_out, 24 + CR)
                dve.wait_ge(sin_ready, 1)
                hv = hid[:, :, 0:640].rearrange("p t (h n) -> p t h n", h=10)
                x1, x2 = hv[:, :, :, 0:8], hv[:, :, :, 8:16]
                s, c = (pair(red[:, 16 * k:16 * k + 16]).unsqueeze(2).to_broadcast([P, NT, 10, 8]) for k in range(2))
                ra = RA[:, 4096:4256].rearrange("p (t h n) -> p t h n", t=NT, h=10)
                rb = RA[:, 4256:4416].rearrange("p (t h n) -> p t h n", t=NT, h=10)
                rc = RA[:, 4416:4576].rearrange("p (t h n) -> p t h n", t=NT, h=10)
                TTop(ra, x1, c, ALU.mult)
                TTop(rb, x2, s, ALU.mult)
                TTop(rc, x1, s, ALU.mult)
                own(TTop(ropet, x2, c, ALU.mult))
                own(TTop(x1, ra, rb, ALU.subtract))
                own(TTop(x2, rc, ropet, ALU.add))
                for g in range(2):
                    last = nc.vector.tensor_copy(kdup[:, :, g], hid[:, :, 512 + 64 * g:576 + 64 * g].unsqueeze(2).to_broadcast([P, NT, 2, 64]))
                    last.then_inc(rope_ready, 1)
                dve.wait_ge(gelu_ready, 1)
                v = hid[:, :, 1280:1792]
                vh = v.rearrange("p t (g n) -> p t g n", g=SG)
                own(nc.vector.tensor_reduce(pair(mean), vh, AX.X, ALU.add))
                own(nc.vector.tensor_scalar(mean, mean, -1.0 / 64, None, ALU.mult))
                own(TTop(vh, vh, bc(pair(mean), 64), ALU.add))
                dve.wait_ge(xT_psum, 40)
                own(TTop(tmpA, v, v, ALU.mult))
                own(nc.vector.tensor_reduce(rs_in[:], tmpA.rearrange("p t (g n) -> p (t g) n", g=SG), AX.X, ALU.add))
                nc.vector.tensor_scalar(rs_in[:], rs_in[:], 1.0 / 64, 1e-5, ALU.mult, ALU.add).then_inc(rs_asked, 1)
                rsqrt(RSQ * DEPTH + 1)
                own(TTop(vh, vh, bc(pair(rs_out[:]), 64), ALU.mult))
                own(TTop(v, v, row(sgu_g), ALU.mult))
                TTop(v, v, row(sgu_bb), ALU.add).then_inc(vg_ready, 1)
                for h in range(QH):
                    dve.wait_ge(sc_psum, h + 1)
                    nc.vector.scalar_tensor_tensor(out=Sc[:, h], in0=PS[:, 4 + h % 4, 0:SW], scalar=HD ** -0.5, in1=swa_mask,
                                                   op0=ALU.mult, op1=ALU.add).then_inc(sc_read, 1)
                dve.wait_ge(sc_read, QH)
                SA, SB = Sc[:, :, 0:P], Sc[:, :, P:SW]
                nc.vector.tensor_reduce(mrow[:, 0:8], SA, AX.X, ALU.max)
                own(nc.vector.tensor_reduce(mrow[:, 8:16], SB, AX.X, ALU.max))
                own(TTop(pair(mrow), pair(mrow), row(sinks), ALU.max))
                TTop(SA, SA, bc(mrow[:, 0:8], P), ALU.subtract)
                TTop(SB, SB, bc(mrow[:, 8:16], 256), ALU.subtract)
                TTop(pair(srow), row(sinks), pair(mrow), ALU.subtract).then_inc(ex_asked, 1)
                dve.wait_ge(sgT_psum, 1)
                TTop(sgT, PS[:, 4:6, :].rearrange("p b (g n) -> p (b g) n", g=4), tri.unsqueeze(1).to_broadcast([P, SG, P]), ALU.mult)\
                    .then_inc(sgT_ready, 1)
                dve.wait_ge(ex_ready, 1)
                nc.vector.tensor_reduce(den[:, 0:8], SA, AX.X, ALU.add)
                own(nc.vector.tensor_reduce(den[:, 8:16], SB, AX.X, ALU.add))
                own(TTop(den, den, srow, ALU.add))
                own(nc.vector.reciprocal(den, den))
                TTop(SA, SA, bc(den[:, 0:8], P), ALU.mult)
                TTop(SB, SB, bc(den[:, 8:16], 256), ALU.mult).then_inc(p_ready, 1)
                dve.wait_ge(sgu_psum, 1)
                TTop(mixg.rearrange("p g t n -> p g (t n)"), PS[:, 6:8, :].rearrange("p b (g n) -> p (b g) n", g=4), bc(sgb, P), ALU.add)\
                    .then_inc(gate_read, 1)
                dve.wait_ge(gate_read, 1)
                for t in range(NT):
                    own(TTop(xn[:, t, 512:1024].rearrange("p (g n) -> p g n", g=SG), mixg[:, :, t], hid[:, t, 768:1280].rearrange("p (g n) -> p g n", g=SG), ALU.mult))
                dve.wait_ge(pv_ready, 1)

            def memory_attention(l):
                dve.wait_ge(xs_psum, l + 1)
                ps = PS[:, 4:8, :].rearrange("p h (t n) -> p (h t) n", t=NT)
                own(nc.vector.tensor_reduce(mrow[:, 0:8], ps, AX.X, ALU.max))
                TTop(px, ps, bc(mrow[:, 0:8], 256), ALU.subtract).then_inc(xe_asked, 1)
                dve.wait_ge(xe_ready, l + 1)
                own(nc.vector.tensor_reduce(den[:, 0:8], px, AX.X, ALU.add))
                own(nc.vector.reciprocal(den[:, 0:8], den[:, 0:8]))
                TTop(px, px, bc(den[:, 0:8], 256), ALU.mult).then_inc(xp_ready, 1)

            def first_of(rank, values, groups):
                n = groups
                v3 = values.rearrange("p (g j) -> p g j", j=4)
                c4 = cmp_[:, 0:16 * n].rearrange("p (g i j) -> p g i j", i=4, j=4)
                e4 = eqs[:, 0:16 * n].rearrange("p (g i j) -> p g i j", i=4, j=4)
                of_j = v3.unsqueeze(2).to_broadcast([P, n, 4, 4])
                of_i = v3.unsqueeze(3).to_broadcast([P, n, 4, 4])
                TTop(c4, of_j, of_i, ALU.is_gt)
                own(TTop(e4, of_j, of_i, ALU.is_equal))
                own(TTop(eqs[:, 0:16 * n].rearrange("p (g k) -> p g k", k=16), eqs[:, 0:16 * n].rearrange("p (g k) -> p g k", k=16),
                         lt.unsqueeze(1).to_broadcast([P, n, 16]), ALU.mult))
                own(TTop(cmp_[:, 0:16 * n], cmp_[:, 0:16 * n], eqs[:, 0:16 * n], ALU.add))
                own(nc.vector.tensor_reduce(rank, cmp_[:, 0:16 * n].rearrange("p (g j) -> p g j", j=4), AX.X, ALU.add))

            def experts(l):
                dve.wait_ge(rt_psum, l + 1)
                own(nc.vector.tensor_reduce(pair(score), PS[:, 0, 0:4 * NE].rearrange("p (t c e) -> p t e c", t=NT, c=2), AX.X, ALU.add))
                dve.sem_inc(acc_free, 1)
                own(nc.vector.tensor_reduce(mrow[:, 0:2], pair(score), AX.X, ALU.max))
                own(TTop(pair(lg), pair(score), bc(mrow[:, 0:2], NE), ALU.subtract))
                dve.sem_inc(re_asked, 1)
                t0 = 4 * TURNS_FFN + NE * TURNS_E * l
                step(t0, 0)
                own(nc.vector.tensor_scalar(x[:], x[:], ALPHA, None, ALU.mult))
                dve.wait_ge(re_ready, l + 1)
                own(nc.vector.tensor_reduce(den[:, 0:2], pair(lg), AX.X, ALU.add))
                own(nc.vector.reciprocal(den[:, 0:2], den[:, 0:2]))
                own(TTop(pair(score), pair(lg), bc(den[:, 0:2], NE), ALU.mult))
                own(TTop(pair(bi), pair(score), row(rbias), ALU.add))
                first_of(wsel, bi, 8)
                own(nc.vector.tensor_scalar(sel, wsel, 1.5, None, ALU.is_lt))
                own(TTop(wsel, sel, bi, ALU.mult))
                step(t0, 1)
                own(nc.vector.tensor_reduce(gsum, wsel.rearrange("p (g j) -> p g j", j=4), AX.X, ALU.add))
                first_of(grank, gsum, 2)
                own(nc.vector.tensor_scalar(grank, grank, 0.5, None, ALU.is_lt))
                own(TTop(sel.rearrange("p (g j) -> p g j", j=4), sel.rearrange("p (g j) -> p g j", j=4), bc(grank, 4), ALU.mult))
                own(TTop(sel, sel, score, ALU.mult))
                own(nc.vector.tensor_reduce(den[:, 0:2], pair(sel), AX.X, ALU.add))
                own(nc.vector.reciprocal(den[:, 0:2], den[:, 0:2]))
                own(TTop(pair(comb), pair(sel), bc(den[:, 0:2], NE), ALU.mult))

                def add(e, by_tile=False):
                    dve.wait_ge(acc_free, 17 * l + 1 + e)
                    for t in range(NT):
                        if by_tile and t == 0:
                            dve.wait_ge(tile_done, 2 * DEPTH + l + 1)
                        elif by_tile or t == 0:
                            dve.wait_ge(used[2], 2 * (t0 + TURNS_E * e + TURNS_E) + 1)
                        last = nc.vector.scalar_tensor_tensor(out=x[:, t], in0=acc[:, t * D:(t + 1) * D], scalar=comb[:, ds(t * NE + e, 1)],
                                                              in1=x[:, t], op0=ALU.mult, op1=ALU.add)
                    last.then_inc(acc_free, 1)

                with dve.Fori(0, NE - 1) as e:
                    t = t0 + TURNS_E * e
                    step(t + 1, 0)
                    step(t + 1, 1)
                    step(t + 2, 0, between=lambda: add(e))
                    step(t + 2, 1)
                t = t0 + TURNS_E * (NE - 1)
                step(t + 1, 0)
                step(t + 1, 1, False)
                if l == 0:
                    split_chunks(2)
                    dve.wait_ge(mem_split, 1)
                    nc.vector.tensor_tensor(xTl[:].rearrange("p k s -> p (k s)"), memT.rearrange("p k s -> p (k s)"),
                                            xTh[:].rearrange("p k s -> p (k s)").bitcast(F32), ALU.subtract).then_inc(mem_split, 1)
                add(NE - 1, True)
                dve.wait_ge(acc_free, 17 * (l + 1))

            turn_for_group(8, W0)
            turn_rows(9, memT)
            for l in range(DEPTH):
                n = 28 if l == 0 else 42
                r = 10 if l == 0 else 16
                if l == 0:
                    window_attention()
                    turn_for_group(10)
                    residual(n)
                    r = 11
                else:
                    split_chunks(6)
                    turn_for_group(15, S)
                    split_chunks(2, S)
                    for j in range(2):
                        dve.wait_ge(group_done, 40 + j + 1 + CR)
                        bs = slice(4 * j, 4 * j + 4)
                        src = PS[:, 2 * j:2 * j + 2, :].rearrange("p b (k s) -> p (b k) s", k=2)
                        TTop(mapT[:, bs], src, bc(pscale[:, bs], S), ALU.mult)
                        own(TTop(xTh[:, bs], src, bc(pscale[:, bs], S), ALU.mult))
                        TTop(xTl[:, bs], mapT[:, bs], xTh[:, bs].bitcast(F32), ALU.subtract).then_inc(group_out, 1)
                        split_chunks(1)
                    residual(n)
                    r = 16
                layer_norm(3 * l, RSQ * DEPTH + 2 + 3 * l)
                turn_for_group(r)
                split_chunks(6)
                memory_attention(l)
                turn_for_group(r + 1)
                residual(n + 4)
                layer_norm(3 * l + 1, RSQ * DEPTH + 3 + 3 * l)
                turn_for_steps(r + 2, 4 * TURNS_FFN + NE * TURNS_E * l)
                experts(l)
                layer_norm(3 * l + 2, RSQ * DEPTH + 4 + 3 * l, True, l == 0)
                if l == 0:
                    split_chunks(10)
                    turn_for_group(14)

        @block.tensor
        def _(pe):
            mm = nc.tensor.matmul
            pe.wait_ge(tab_in, 16)
            pe.wait_ge(setup, 3)
            for m in range(3):
                pe.sem_inc(used[m], 1)
            pe.sem_inc(chunk_used, 4)
            pe.sem_inc(group_done, CR)
            pe.sem_inc(group_out, CR)

            def keep_busy(rounds, bank=7):
                with pe.Fori(0, rounds):
                    for _ in range(8):
                        mm(PS[:, bank, :], zero[:, 0:P], zero[:], start=True, stop=True)

            def turn_rows(r, src=xn):
                pe.wait_ge(xn_ready, r + 1)
                for b in range(4):
                    for n in range(4):
                        last = nc.tensor.transpose(PS[:, 4 + b, n * P:(n + 1) * P], src[:, n % 2, (2 * b + n // 2) * P:(2 * b + n // 2 + 1) * P], ident)
                    last.then_inc(xT_psum, 1)
                turned(r)

            def turned(r):
                pe.wait_ge(xT_act, 4 * r + 4)
                hold(pe, xT_dve, 4 * r + 4)

            def gate_up(turn, j):
                for m in range(2):
                    pe.wait_ge(lo_done[m], 2 * turn + j + 1 + CR)
                    if m == 0:
                        pe.wait_ge(hT_ready, 2 * turn + j + 1)
                    for k in range(KB):
                        out_, ks = PS[:, 4 + j, m * S:(m + 1) * S], slice(k * P, (k + 1) * P)
                        mm(out_, whi[:, m, ks], xTh[:, k, :], start=(k == 0), stop=False)
                        mm(out_, whi[:, m, ks], xTl[:, k, :], start=False, stop=False)
                        last = mm(out_, wlo[:, m, ks], xTh[:, k, :], start=False, stop=(k == KB - 1))
                    last.then_inc(used[m], 1)

            def down(turn, j, opens=None, ends=False):
                pe.wait_ge(lo_done[2], 2 * turn + j + 1 + CR)
                pe.wait_ge(hT_ready, 2 * turn + j + 1 + CR)
                if opens is not None:
                    pe.wait_ge(acc_free, opens)
                for t in range(NT):
                    ts = slice(t * P, (t + 1) * P)
                    for n in range(2):
                        out_, ns = PS[:, 2 * t + n, :], slice(n * 512, (n + 1) * 512)
                        mm(out_, hTh[:, j, ts], whi[:, 2, ns], start=(opens is not None), stop=False, skip_group_check=True)
                        mm(out_, hTh[:, j, ts], wlo[:, 2, ns], start=False, stop=False, skip_group_check=True)
                        last = mm(out_, hTl[:, j, ts], whi[:, 2, ns], start=False, stop=False, skip_group_check=True)
                    if ends and t == 0:
                        last.then_inc(tile_done, 1)
                last.then_inc(used[2], 1)

            def step(turn, j, opens=None):
                gate_up(turn + j, 1 - j)
                down(turn, j, opens)

            def ffn(t0):
                for b in range(4):
                    mm(PS[:, b, :], zero[:, 0:P], zero[:], start=True, stop=False, skip_group_check=True)
                gate_up(t0, 0)
                with pe.Fori(0, TURNS_FFN - 1) as g:
                    for j in range(2):
                        step(t0 + g, j)
                step(t0 + TURNS_FFN - 1, 0)
                down(t0 + TURNS_FFN - 1, 1, ends=True)
                keep_busy(5)

            def experts(t0, free):
                gate_up(t0, 0)
                step(t0, 0, free)
                with pe.Fori(0, NE - 1) as e:
                    t = t0 + TURNS_E * e
                    step(t, 1)
                    step(t + 1, 0)
                    step(t + 1, 1)
                    step(t + 2, 0, free + 1 + e)
                t = t0 + TURNS_E * (NE - 1)
                step(t, 1)
                step(t + 1, 0)
                down(t + 1, 1, ends=True)

            def group_end(n4):
                pe.wait_ge(chunk_used, 4 * n4 + 4 + 4)
                pe.sem_inc(group_done, 1)

            def group(n, n4, ns, slot, width):
                pe.wait_ge(group_out, n + 1)
                for c in range(4):
                    pe.wait_ge(chunk_lo, 4 * ns + c + 1 + 4)
                    for t in range(NT):
                        for i in range(2):
                            out_, k, ts, ws = PS[:, 2 * slot + t, 0:width], 2 * c + i, slice(t * P, (t + 1) * P), slice(i * width, (i + 1) * width)
                            mm(out_, xTh[:, k, ts], whi[:, SPLIT_AT[c], ws], start=(k == 0), stop=False)
                            mm(out_, xTh[:, k, ts], wlo[:, SPLIT_AT[c], ws], start=False, stop=False)
                            last = mm(out_, xTl[:, k, ts], whi[:, SPLIT_AT[c], ws], start=False, stop=(k == KB - 1))
                    last.then_inc(chunk_used, 1)
                group_end(n4)

            keep_busy(3)
            with pe.Fori(0, DEPTH) as l:
                turn_rows(4 * l)
                ffn(2 * TURNS_FFN * l)
                turn_rows(4 * l + 1)
                with pe.Fori(0, 4) as g:
                    for j in range(2):
                        n = 10 * l + 2 * g + j
                        group(n, n, n, j, GW)
                pe.wait_ge(qk_rot, l + 1)
                for q in range(4):
                    for t in range(NT):
                        n = 2 * q + t
                        last = nc.tensor.transpose(PS[:, 4 + n // 4, (n % 4) * P:(n % 4 + 1) * P],
                                                   qk[:, t, 2 * q:2 * q + 2, :].rearrange("p h n -> p (h n)"), ident)
                last.then_inc(qkT_psum, 1)
                pe.wait_ge(qkT_ready, l + 1)
                pe.wait_ge(group_out, 10 * l + 8 + CR)

                def scores(h):
                    b, q = 64 * (h % 2), h // 2
                    if h >= 2:
                        pe.wait_ge(ret_p, 4 * l + h - 1)
                    mm(PS[:, 6 + h % 2, 0:S], qkT[b:b + 64, 2 + q, 0, :], qkT[b:b + 64, q, :, :].rearrange("p t n -> p (t n)"), start=True, stop=True)
                    mm(PS[:, 6 + h % 2, S:S + P], qkT[b:b + 64, 2 + q, 1, :], qkT[b:b + 64, q, 1, :], start=True, stop=True).then_inc(ret_s, 1)

                def values(h):
                    pe.wait_ge(ret_p, 4 * l + h + 1)
                    v = [proj[:, t, VCOL + h * P:VCOL + (h + 1) * P] for t in range(NT)]
                    o = [PS[:, t, h * P:(h + 1) * P] for t in range(NT)]
                    mm(o[0], PT[:, h % 2, 0:P], v[0], start=True, stop=True)
                    mm(o[1], PT[:, h % 2, P:2 * P], v[0], start=True, stop=False)
                    return mm(o[1], PT[:, h % 2, 2 * P:3 * P], v[1], start=False, stop=True)

                scores(0)
                scores(1)
                values(0)
                scores(2)
                values(1)
                scores(3)
                values(2)
                values(3).then_inc(ret_o, 1)
                pe.wait_ge(lora_act, 2 * l + 2)
                pe.wait_ge(shifted, l + 1)
                for b in range(2):
                    for t in range(NT):
                        last = nc.tensor.transpose(PS[:, 4, (2 * b + t) * P:(2 * b + t + 1) * P], proj[:, t, 1536 + b * P:1536 + (b + 1) * P], ident)
                last.then_inc(lT_psum, 1)
                pe.wait_ge(lT_ready, l + 1)
                pe.wait_ge(ret_oc, l + 1)
                pe.wait_ge(param_in, 160 * l + 160)
                for t in range(NT):
                    ts = slice(t * P, (t + 1) * P)
                    mm(PS[:, t, :], lT[0:64, 0, ts], WL[0:64], start=True, stop=True)
                    mm(PS[:, 2 + t, :], lT[64:128, 0, ts], WL[64:128], start=True, stop=True)
                    last = mm(PS[:, 6 + t, :], lT[:, 1, ts], GL, start=True, stop=True)
                last.then_inc(lora_out, 1)
                pe.wait_ge(z_ready, 2 * l + 2)
                pe.wait_ge(sig_ready, 2 * l + 1)
                for t in range(NT):
                    mm(PS[:, t, :], tab[:, T_CUMI:T_CUMI + P], sw[:, t], start=True, stop=True)
                    mm(PS[:, 2 + t, :], tab[:, T_CUMX:T_CUMX + P], sw[:, t], start=True, stop=True)
                    for q in range(4):
                        c0 = (4 * t + q) * 2
                        last = mm(PS[:, 5, c0:c0 + 2], sw[:, t, q * P:(q + 1) * P], tab[:, T_TOT:T_TOT + 2], start=True, stop=True)
                last.then_inc(cum_psum, 1)
                keep_busy(5, 4)
                pe.wait_ge(tilde, l + 1)
                for t in range(NT):
                    if t:
                        pe.wait_ge(y_ready, 2 * l + t)
                        pe.wait_ge(z_state, 3 * l + 2)
                    for q in range(4):
                        qs = slice(q * P, (q + 1) * P)
                        nc.tensor.transpose(PS[:, q // 2, (q % 2) * 256:(q % 2) * 256 + P], tl[:, 0, t, qs], ident)
                        nc.tensor.transpose(PS[:, q // 2, (q % 2) * 256 + P:(q % 2) * 256 + 256], tl[:, 3, t, qs], ident)
                        nc.tensor.transpose(PS[:, 2, qs], tl[:, 1, t, qs], ident)
                        last = nc.tensor.transpose(PS[:, 3, qs], tl[:, 2, t, qs], ident)
                    last.then_inc(tr_psum, 1)
                    pe.wait_ge(tr_act, 2 * l + t + 1)
                    pe.wait_ge(tr_dve, 2 * l + t + 1)
                    for h in range(RH):
                        b, q = 64 * (h % 2), h // 2
                        if h >= 4:
                            pe.wait_ge(L_ready, 16 * l + 8 * t + h - 3)
                        mm(PS[:, 4 + h % 4, 0:256], BT[b:b + 64, q, :], ART[b:b + 64, q, :], start=True, stop=True)
                        mm(PS[:, 4 + h % 4, 256:512], KT[b:b + 64, q, :], ART[b:b + 64, q, :], start=True, stop=True).then_inc(L_psum, 1)
                    v = [proj[:, t, 2 * RW + h * RN:2 * RW + (h + 1) * RN] for h in range(RH)]
                    for h in range(RH):
                        pe.wait_ge(L_ready, 16 * l + 8 * t + h + 1)
                        last = mm(PS[:, 0, h * RN:(h + 1) * RN], Lm[:, h, 256:384], v[h], start=True, stop=True)
                    last.then_inc(av_psum, 1)
                    for lev in range(6):
                        for hf in range(2):
                            base = 24 * l + 12 * t + 2 * lev + hf
                            pe.wait_ge(aoff_ready, base + 1)
                            if lev:
                                pe.wait_ge(t_ready, base - 1)
                                if lev > 1:
                                    pe.wait_ge(q_ready, 20 * l + 10 * t + 2 * (lev - 2) + hf + 1)
                            for h in range(4 * hf, 4 * hf + 4):
                                last = mm(PS[:, 2 + hf, (h % 4) * P:(h % 4 + 1) * P], Aoff[:, h], TM[:, h] if lev else ident, start=True, stop=True)
                            last.then_inc(q_psum, 1)
                        if lev == 0:
                            continue
                        for hf in range(2):
                            pe.wait_ge(q_ready, 20 * l + 10 * t + 2 * (lev - 1) + hf + 1)
                            for h in range(4 * hf, 4 * hf + 4):
                                hs = slice((h % 4) * P, (h % 4 + 1) * P)
                                if lev < 5:
                                    mm(PS[:, 4 + hf, hs], TT[:, h], QM[:, h], start=True, stop=True)
                                last = mm(PS[:, 6 + hf, hs], QM[:, h], TT[:, h], start=True, stop=True)
                            last.then_inc(t_psum, 1)
                    pe.wait_ge(t_ready, 24 * l + 12 * t + 12)
                    for h in range(RH):
                        b, q = 64 * (h % 2), h // 2
                        last = mm(PS[b:b + 64, 1, q * P:(q + 1) * P], tl[:, 0, t, h * RN:(h + 1) * RN], TT[:, h], start=True, stop=True)
                    last.then_inc(gT_psum, 1)
                    pe.wait_ge(av_ready, 2 * l + t + 1)
                    for hf in range(2):
                        ch = 2 * t + hf
                        rows = slice(64 * hf, 64 * hf + 64)
                        if hf == 0:
                            for h in range(RH):
                                last = mm(PS[:, 2, h * RN:(h + 1) * RN], TT[:, h], AV[:, h * RN:(h + 1) * RN],
                                          start=(h == 0), stop=False, skip_group_check=True)
                            pe.wait_ge(gT_ready, 2 * l + t + 1)
                        if ch:
                            pe.wait_ge(z_state, 3 * l + ch)
                            for q in range(4):
                                last = mm(PS[rows, 2, q * P:(q + 1) * P], tl[:, 3, t, q * P + 64 * hf:q * P + 64 * hf + 64],
                                          Zs[:, ch - 1, q, :], start=False, stop=False, skip_group_check=True)
                        last.then_inc(u_psum, 1)
                        pe.wait_ge(u_ready, 4 * l + ch + 1)
                        if ch == 3:
                            break
                        for q in range(4):
                            qs = slice(q * P, (q + 1) * P)
                            mm(PS[:, 3, qs], tl[rows, 1, t, qs], U[rows, qs], start=True, stop=False)
                            last = mm(PS[:, 3, qs], tl[rows, 2, t, qs], proj[rows, t, 2 * RW + q * P:2 * RW + (q + 1) * P], start=False, stop=True)
                        last.then_inc(z_psum, 1)
                    for h in range(RH):
                        b, q = 64 * (h % 2), h // 2
                        hs = slice(h * RN, (h + 1) * RN)
                        mm(PS[:, 1, hs], Lm[:, h, 128:256], U[:, hs], start=(h == 0), stop=False, skip_group_check=True)
                        mm(PS[:, 1, hs], Lm[:, h, 384:512], v[h], start=False, stop=False, skip_group_check=True)
                    for q in range(4):
                        for hf in range(2):
                            ch = 2 * t + hf
                            if ch:
                                last = mm(PS[64 * hf:64 * hf + 64, 1, q * P:(q + 1) * P], ART[:, q, P + 64 * hf:P + 64 * hf + 64],
                                          Zs[:, ch - 1, q, :], start=False, stop=False, skip_group_check=True)
                    last.then_inc(y_psum, 1)
                keep_busy(5)
                turn_rows(4 * l + 2)
                for j in range(2):
                    group(10 * l + 8 + j, 10 * l + 8 + j, 10 * l + 8 + j, j, 512)
                keep_busy(4)
                turn_rows(4 * l + 3)
                ffn(2 * TURNS_FFN * l + TURNS_FFN)
            n4 = 10 * DEPTH
            ns = 10 * DEPTH

            def group2(n, width):
                nonlocal n4, ns
                group(n, n4, ns, n % 2, width)
                n4, ns = n4 + 1, ns + 1

            def memory_values(n):
                nonlocal n4
                slot = n % 2
                pe.wait_ge(group_out, n + 1)
                for c in range(4):
                    pe.wait_ge(chunk_in[c], 16 * n4 + 16)
                    w = chunk_raw(c, 2, 512)
                    for t in range(NT):
                        for i in range(2):
                            last = mm(PS[:, 2 * slot + t, :], memT[:, 2 * c + i, t * P:(t + 1) * P], w[:, i, :],
                                      start=(c == 0 and i == 0), stop=(c == 3 and i == 1))
                    last.then_inc(chunk_used, 1)
                group_end(n4)
                n4 += 1

            def group_turned(n, split):
                nonlocal n4, ns
                slot = n % 2
                pe.wait_ge(group_out, n + 1)
                for c in range(4):
                    if split:
                        pe.wait_ge(chunk_lo, 4 * ns + c + 1 + 4)
                    else:
                        pe.wait_ge(chunk_in[c], 16 * n4 + 16)
                    w = chunk_raw(c, 2, 512)
                    for f in range(4):
                        out_ = PS[:, 2 * slot + f // 2, (f % 2) * S:(f % 2 + 1) * S]
                        for i in range(2):
                            k, ws = 2 * c + i, slice(i * 512 + f * P, i * 512 + (f + 1) * P)
                            opens, closes = k == 0 and f % 2 == 0, k == KB - 1
                            if split:
                                mm(out_, whi[:, SPLIT_AT[c], ws], xTh[:, k, :], start=opens, stop=False, skip_group_check=True)
                                mm(out_, whi[:, SPLIT_AT[c], ws], xTl[:, k, :], start=False, stop=False, skip_group_check=True)
                                last = mm(out_, wlo[:, SPLIT_AT[c], ws], xTh[:, k, :], start=False, stop=closes, skip_group_check=True)
                            else:
                                last = mm(out_, w[:, i, f * P:(f + 1) * P], memT[:, k, :], start=opens, stop=closes, skip_group_check=True)
                    last.then_inc(chunk_used, 1)
                group_end(n4)
                n4 += 1
                ns += split

            turn_rows(8, x)
            pe.wait_ge(par2_in, 176)
            turn_rows(9, mem)
            for l in range(DEPTH):
                n = 20 if l == 0 else 38
                for j in range(4 if l == 0 else 2):
                    group2(n + j, W0 if l == 0 else 512)
                n += 4 if l == 0 else 2
                if l == 0:
                    for j in range(2):
                        group_turned(n + j, False)
                    pe.wait_ge(rope_ready, 2)
                    for q in range(4):
                        for t in range(NT):
                            i = 2 * q + t
                            nc.tensor.transpose(PS[:, 4 + i // 4, (i % 4) * P:(i % 4 + 1) * P], hid[:, t, q * P:(q + 1) * P], ident)
                    for g in range(2):
                        for t in range(NT):
                            i = 2 * g + t
                            last = nc.tensor.transpose(PS[:, 6, i * P:(i + 1) * P], kdup[:, t, g].rearrange("p c n -> p (c n)"), ident)
                    last.then_inc(swT_psum, 1)
                    pe.wait_ge(swT_ready, 1)
                    for h in range(QH):
                        b, q, g = 64 * (h % 2), h // 2, h // 4
                        if h >= 4:
                            pe.wait_ge(sc_read, h - 3)
                        mm(PS[:, 4 + h % 4, 0:P], qT2[b:b + 64, q, 0], kT2[b:b + 64, g, 0], start=True, stop=True)
                        mm(PS[:, 4 + h % 4, P:SW], qT2[b:b + 64, q, 1], kT2[b:b + 64, g].rearrange("p t n -> p (t n)"), start=True, stop=True)\
                            .then_inc(sc_psum, 1)
                    pe.wait_ge(sc_read, QH)
                    for g in range(SG):
                        last = nc.tensor.transpose(PS[:, 4 + g // 4, (g % 4) * P:(g % 4 + 1) * P], sgw[:, g], ident)
                    last.then_inc(sgT_psum, 1)
                    for j in range(2):
                        memory_values(n + 2 + j)
                    n += 4
                    pe.wait_ge(sgT_ready, 1)
                    pe.wait_ge(vg_ready, 1)
                    vg = hid[:, :, 1280:1792]
                    for g in range(SG):
                        last = mm(PS[:, 6 + g // 4, (g % 4) * P:(g % 4 + 1) * P], sgT[:, g], vg[:, :, g * 64:(g + 1) * 64], start=True, stop=True)
                    last.then_inc(sgu_psum, 1)
                    pe.wait_ge(p_ready, 1)
                    pe.wait_ge(group_out, n + CR)
                    for half in range(2):
                        for i in range(12):
                            h, b3 = 4 * half + i // 3, i % 3
                            last = nc.tensor.transpose(PS[:, 3 * half + i // 4, (i % 4) * P:(i % 4 + 1) * P], Sc[:, h, b3 * P:(b3 + 1) * P], ident)
                        last.then_inc(pT_psum, 1)
                    pe.wait_ge(pT_ready, 2)
                    pe.wait_ge(gate_read, 1)
                    for h in range(QH):
                        ks = slice(640 + 64 * (h // 4), 704 + 64 * (h // 4))
                        os_ = slice(h * HD, (h + 1) * HD)
                        mm(PS[:, 6, os_], pTw[:, h, 0], hid[:, 0, ks], start=True, stop=True)
                        mm(PS[:, 7, os_], pTw[:, h, 1], hid[:, 0, ks], start=True, stop=False)
                        last = mm(PS[:, 7, os_], pTw[:, h, 2], hid[:, 1, ks], start=False, stop=True)
                    last.then_inc(pv_psum, 1)
                    turn_rows(10)
                    r = 11
                else:
                    pe.wait_ge(pool_in, 16)
                    pe.wait_ge(group_out, n + CR)
                    for k in range(KB):
                        for t in range(NT):
                            last = mm(PS[:, 4 + k // 2, (k % 2) * S:(k % 2 + 1) * S], hid1[:, t, k * P:(k + 1) * P], pool_t[:, k // 2, t],
                                      start=(t == 0), stop=(t == NT - 1))
                        if k % 2:
                            last.then_inc(xT_psum, 1)
                    turned(15)
                    for j in range(2):
                        pe.wait_ge(group_out, n + 1)
                        for g in range(2):
                            pe.wait_ge(chunk_lo, 4 * ns + 2 * j + g + 1 + 4)
                            for d in range(2):
                                for c in range(2):
                                    out_, k, ws = PS[:, 2 * j + g, d * S:(d + 1) * S], 2 * (2 * j + g) + c, slice(c * S + d * P, c * S + (d + 1) * P)
                                    mm(out_, whi[:, SPLIT_AT[2 * j + g], ws], xTh[:, k, :], start=(c == 0), stop=False)
                                    mm(out_, whi[:, SPLIT_AT[2 * j + g], ws], xTl[:, k, :], start=False, stop=False)
                                    last = mm(out_, wlo[:, SPLIT_AT[2 * j + g], ws], xTh[:, k, :], start=False, stop=(c == 1))
                            last.then_inc(chunk_used, 1)
                        pe.wait_ge(chunk_used, 4 * n4 + 2 * j + 2 + 4)
                        pe.sem_inc(group_done, 1)
                        n += 1
                    n4, ns = n4 + 1, ns + 1
                    pe.wait_ge(group_out, n + CR)
                    r = 16
                for j in range(2):
                    group2(n + j, 512)
                n += 2
                keep_busy(4)
                turn_rows(r, x)
                for j in range(2):
                    group_turned(n + j, True)
                n += 2
                pe.wait_ge(group_out, n + CR)
                for h in range(XH):
                    for t in range(NT):
                        for d in range(2):
                            last = mm(PS[:, 4 + h, t * S:(t + 1) * S], qT[:, 2 * h + d, t * P:(t + 1) * P], kT[:, 2 * h + d, :],
                                      start=(d == 0), stop=(d == 1))
                last.then_inc(xs_psum, 1)
                keep_busy(3, 0)
                pe.wait_ge(xp_ready, l + 1)
                for h in range(XH):
                    for m in range(NT):
                        for t in range(NT):
                            last = nc.tensor.transpose(PS[:, h, m * S + t * P:m * S + (t + 1) * P], px[:, 2 * h + t, m * P:(m + 1) * P], ident)
                last.then_inc(xpT_psum, 1)
                pe.wait_ge(xpT_ready, l + 1)
                for h in range(XH):
                    for d in range(2):
                        for m in range(NT):
                            last = mm(PS[:, 4 + h, d * S:(d + 1) * S], vM[:, m, (2 * h + d) * P:(2 * h + d + 1) * P], pxT[:, h, m, :],
                                      start=(m == 0), stop=(m == NT - 1))
                    last.then_inc(xT_psum, 1)
                turned(r + 1)
                for j in range(2):
                    group2(n + j, 512)
                keep_busy(4)
                turn_rows(r + 2, x)
                pe.wait_ge(rw_split, 2)
                for t in range(NT):
                    for k in range(KB):
                        out_, ts = PS[:, 0, t * 2 * NE:(t + 1) * 2 * NE], slice(t * P, (t + 1) * P)
                        both = rws[:, k].rearrange("p c e -> p (c e)")
                        mm(out_, xTh[:, k, ts], both, start=(k == 0), stop=False)
                        last = mm(out_, xTl[:, k, ts], both, start=False, stop=(k == KB - 1))
                last.then_inc(rt_psum, 1)
                experts(4 * TURNS_FFN + NE * TURNS_E * l, 17 * l + 1)
                if l == 0:
                    pe.wait_ge(mem_split, 2)
                    pe.wait_ge(acc_free, 17)
                    for j in range(2):
                        group_turned(34 + j, True)
                    for j in range(2):
                        group2(36 + j, 512)
                    turn_rows(14, x)


_INS = ["x", "ffn1_norm", "ffn1_w_gate", "ffn1_w_up", "ffn1_w_down", "mix_norm", "w_in", "shift_mu", "w0", "w_lora_up",
        "a0", "a_lora_up", "g_lora_up", "k_k", "k_a", "r_k", "ln_x_w", "ln_x_b", "w_out", "ffn2_norm", "ffn2_w_gate",
        "ffn2_w_up", "ffn2_w_down", "final_norm", "mem_2", "positions_2", "router_w_2", "router_bias_2",
        "l0_w_in_2", "l0_sinks_2", "l0_sgu_ln_g_2", "l0_sgu_ln_b_2", "l0_sgu_w_2", "l0_sgu_b_2", "l0_w_out_2",
        "l0_ln1_g_2", "l0_ln1_b_2", "l0_xq_2", "l0_xkv_2", "l0_xo_2", "l0_ln2_g_2", "l0_ln2_b_2", "l0_e_gate_2",
        "l0_e_up_2", "l0_e_down_2", "l0_ln3_g_2", "l0_ln3_b_2", "l1_w_in_2", "l1_pool_w_2", "l1_pool_scale_2",
        "l1_w_out_2", "l1_ln1_g_2", "l1_ln1_b_2", "l1_xq_2", "l1_xkv_2", "l1_xo_2", "l1_ln2_g_2", "l1_ln2_b_2",
        "l1_e_gate_2", "l1_e_up_2", "l1_e_down_2", "l1_ln3_g_2", "l1_ln3_b_2"]


def kernel(**inputs):
    import concourse.bacc as bacc
    from concourse.bass_utils import run_bass_kernel_spmd as run

    nc = bacc.Bacc("TRN2", target_bir_lowering=False, num_devices=1)
    arrays, args = {}, {}
    for name in _INS + ["tables"]:
        a = tables() if name == "tables" else np.ascontiguousarray(inputs[name])
        arrays[f"in_{name}_dram"] = a
        args[name] = nc.dram_tensor(f"in_{name}_dram", a.shape, mybir.dt.from_np(a.dtype), kind="ExternalInput").ap()
    out = nc.dram_tensor("out_0_dram", (1, S, D), F32, kind="ExternalOutput").ap()
    both_blocks(nc, args, out)
    r = run(nc, [arrays], core_ids=[0])
    return r.results[0]["out_0_dram"]
```
